# Optimizing a Trainium2 kernel written in Bass

```python
import math
import jax, jax.numpy as jnp
from jax import lax
import numpy as np

D_MODEL = 1024
BATCH = 1
SEQ = 2048
DEPTH = 1

N_META = 16
BLOCK = 128
PAD = BLOCK - N_META
RET_HEADS = 4
RET_DK = 128
RET_DV = 128
FOX_HEADS = 8
FOX_HD = 64
MIX_WIDTH = RET_HEADS * RET_DV + FOX_HEADS * FOX_HD
IN_SIZES = (RET_HEADS * RET_DK, RET_HEADS * RET_DK, RET_HEADS * RET_DV, RET_HEADS * RET_DV, FOX_HEADS * FOX_HD, FOX_HEADS * FOX_HD, FOX_HEADS * FOX_HD, FOX_HEADS)
IN_COLS = sum(IN_SIZES)
N_EXPERTS = 64
TOP_K = 6
N_GROUPS = 8
TOPK_GROUPS = 4
EXPERT_FF = 256
SHARED_FF = 256
ROUTED_SCALE = 2.5
DISPATCH_BLOCK = 128
ROPE_BASE = 10000.0
LN_EPS = 1e-5
NEG_INF = -1e30
ALPHA = (2.0 * DEPTH) ** 0.25
BETA = (8.0 * DEPTH) ** -0.25

kernel_name = 'hybrid_retention_fox_moe_block'

def layer_norm(x, g, b):
    xf = x.astype(jnp.float32)
    xc = xf - jnp.mean(xf, -1, keepdims=True)
    var = jnp.mean(xc * xc, -1, keepdims=True)
    y = xc * lax.rsqrt(var + LN_EPS) * g.astype(jnp.float32) + b.astype(jnp.float32)
    return y.astype(x.dtype)

def head_norm(y):
    yc = y - jnp.mean(y, -1, keepdims=True)
    return yc * lax.rsqrt(jnp.mean(yc * yc, -1, keepdims=True) + LN_EPS)

def rotary(t, pos):
    half = t.shape[-1] // 2
    inv = ROPE_BASE ** (-jnp.arange(half, dtype=jnp.float32) / half)
    ang = pos[:, None] * inv[None, :]
    cos = jnp.cos(ang)[None, :, None, :]
    sin = jnp.sin(ang)[None, :, None, :]
    t1, t2 = t[..., :half], t[..., half:]
    return jnp.concatenate([t1 * cos - t2 * sin, t2 * cos + t1 * sin], -1)

def retention(q, k, v):
    b, lp, h, dk = q.shape
    dv = v.shape[-1]
    nc = lp // BLOCK
    lg = jnp.log1p(-jnp.exp2(-5.0 - jnp.arange(h, dtype=jnp.float32)))
    idx = jnp.arange(BLOCK, dtype=jnp.float32)
    rel = idx[:, None] - idx[None, :]
    causal = rel >= 0
    dmask = jnp.where(causal[None], jnp.exp(jnp.where(causal, rel, 0.0)[None] * lg[:, None, None]), 0.0)
    zeta = jnp.exp((BLOCK - 1.0 - idx)[None, :] * lg[:, None])
    xi = jnp.exp((idx + 1.0)[None, :] * lg[:, None])
    g_chunk = jnp.exp(BLOCK * lg)
    qc = q.reshape(b, nc, BLOCK, h, dk)
    kc = k.reshape(b, nc, BLOCK, h, dk)
    vc = v.reshape(b, nc, BLOCK, h, dv)
    scores = jnp.einsum('bnihd,bnjhd->bnhij', qc, kc) * dmask[None, None]
    inner = jnp.einsum('bnhij,bnjhe->bnihe', scores, vc)
    kv = jnp.einsum('bnjhd,hj,bnjhe->bnhde', kc, zeta, vc)

    def step(state, kv_n):
        return g_chunk[None, :, None, None] * state + kv_n, state

    _, prev = lax.scan(step, jnp.zeros((b, h, dk, dv), q.dtype), jnp.moveaxis(kv, 1, 0))
    prev = jnp.moveaxis(prev, 0, 1)
    cross = jnp.einsum('bnihd,hi,bnhde->bnihe', qc, xi, prev)
    return (inner + cross).reshape(b, lp, h, dv)

def forgetting_attention(q, k, v, logf):
    b, lp, h, d = q.shape
    scale = d ** -0.5
    c = jnp.transpose(jnp.cumsum(logf, axis=1), (0, 2, 1))
    kpos = jnp.arange(lp)
    outs = []
    for i in range(lp // BLOCK):
        q0, kend = i * BLOCK, (i + 1) * BLOCK
        s = jnp.einsum('bqhd,bkhd->bhqk', q[:, q0:kend], k[:, :kend]) * scale
        s = s + c[:, :, q0:kend, None] - c[:, :, None, :kend]
        qpos = jnp.arange(q0, kend)
        mask = (kpos[None, :kend] <= qpos[:, None]) & (kpos[None, :kend] >= PAD)
        p = jax.nn.softmax(jnp.where(mask[None, None], s, NEG_INF), axis=-1)
        outs.append(jnp.einsum('bhqk,bkhd->bqhd', p, v[:, :kend]))
    return jnp.concatenate(outs, axis=1)

def hybrid_mixer(h, w_in, b_forget, w_out):
    b, l, _ = h.shape
    lp = l + PAD
    proj = jnp.einsum('bld,dc->blc', h, w_in).astype(jnp.float32)
    points, acc = [], 0
    for sz in IN_SIZES[:-1]:
        acc += sz
        points.append(acc)
    rq, rk, rv, rg, fq, fk, fv, ff = jnp.split(proj, points, axis=-1)
    logf = jax.nn.log_sigmoid(ff + b_forget.astype(jnp.float32))

    def pad(t):
        return jnp.pad(t, ((0, 0), (PAD, 0), (0, 0)))

    def heads(t, nh):
        return pad(t).reshape(b, lp, nh, -1)

    pos = jnp.arange(lp, dtype=jnp.float32) - PAD
    ret = retention(rotary(heads(rq, RET_HEADS), pos),
                    rotary(heads(rk, RET_HEADS), pos) * (RET_DK ** -0.5),
                    heads(rv, RET_HEADS))[:, PAD:]
    ret = head_norm(ret).reshape(b, l, RET_HEADS * RET_DV) * jax.nn.silu(rg)
    fox = forgetting_attention(heads(fq, FOX_HEADS), heads(fk, FOX_HEADS), heads(fv, FOX_HEADS), pad(logf))[:, PAD:]
    fox = fox.reshape(b, l, FOX_HEADS * FOX_HD)
    mixed = jnp.concatenate([ret, fox], axis=-1).astype(h.dtype)
    return jnp.einsum('blc,cd->bld', mixed, w_out)

def swiglu(t, wg, wu, wd):
    return (jax.nn.silu(t @ wg) * (t @ wu)) @ wd

def routed_experts(t, w_router, router_bias, we_gate, we_up, we_down):
    n, d = t.shape
    scores = jax.nn.sigmoid((t @ w_router).astype(jnp.float32))
    biased = scores + router_bias.astype(jnp.float32)
    grp = biased.reshape(n, N_GROUPS, N_EXPERTS // N_GROUPS)
    group_score = jnp.sum(lax.top_k(grp, 2)[0], axis=-1)
    _, top_groups = lax.top_k(group_score, TOPK_GROUPS)
    gmask = jnp.any(top_groups[:, :, None] == jnp.arange(N_GROUPS)[None, None, :], axis=1)
    emask = jnp.repeat(gmask, N_EXPERTS // N_GROUPS, axis=1)
    _, top_e = lax.top_k(jnp.where(emask, biased, NEG_INF), TOP_K)
    gates = jnp.take_along_axis(scores, top_e, axis=1)
    gates = gates / jnp.sum(gates, -1, keepdims=True) * ROUTED_SCALE
    nk = n * TOP_K
    e_flat = top_e.reshape(nk)
    tok_flat = jnp.repeat(jnp.arange(n, dtype=jnp.int32), TOP_K)
    order = jnp.argsort(e_flat)
    e_s, tok_s, g_s = e_flat[order], tok_flat[order], gates.reshape(nk)[order]
    counts = jnp.bincount(e_flat, length=N_EXPERTS)
    padded = (counts + DISPATCH_BLOCK - 1) // DISPATCH_BLOCK * DISPATCH_BLOCK
    start = jnp.cumsum(counts) - counts
    pend = jnp.cumsum(padded)
    pstart = pend - padded
    dest = pstart[e_s] + jnp.arange(nk, dtype=jnp.int32) - start[e_s]
    n_blocks = -(-(nk + N_EXPERTS * (DISPATCH_BLOCK - 1)) // DISPATCH_BLOCK)
    rows = n_blocks * DISPATCH_BLOCK
    buf_tok = jnp.full((rows,), n, jnp.int32).at[dest].set(tok_s)
    buf_gate = jnp.zeros((rows,), jnp.float32).at[dest].set(g_s)
    blk_e = jnp.minimum(jnp.searchsorted(pend, jnp.arange(n_blocks, dtype=jnp.int32) * DISPATCH_BLOCK, side='right'), N_EXPERTS - 1)
    t_pad = jnp.concatenate([t, jnp.zeros((1, d), t.dtype)], axis=0)

    def step(acc, blk):
        tok, gate, e = blk
        y = swiglu(t_pad[tok], we_gate[e], we_up[e], we_down[e])
        return acc.at[tok].add(y * gate[:, None].astype(y.dtype)), None

    acc, _ = lax.scan(step, jnp.zeros((n + 1, d), t.dtype),
                      (buf_tok.reshape(n_blocks, DISPATCH_BLOCK), buf_gate.reshape(n_blocks, DISPATCH_BLOCK), blk_e))
    return acc[:n]

def setup_inputs(seed: int = 0) -> dict:
    key = jax.random.key(seed)
    ks = jax.random.split(key, 19)

    def nrm(k, shape, scale):
        return jax.random.normal(k, shape, jnp.float32) * scale

    return {
        'x': nrm(ks[0], (BATCH, SEQ, D_MODEL), 1.0),
        'meta': nrm(ks[1], (N_META, D_MODEL), 1.0),
        'ln0_g': 1.0 + nrm(ks[2], (D_MODEL,), 0.01),
        'ln0_b': nrm(ks[3], (D_MODEL,), 0.01),
        'w_in': nrm(ks[4], (DEPTH, D_MODEL, IN_COLS), D_MODEL ** -0.5),
        'b_forget': jax.random.uniform(ks[5], (DEPTH, FOX_HEADS), jnp.float32, 1.0, 4.0),
        'w_out': nrm(ks[6], (DEPTH, MIX_WIDTH, D_MODEL), BETA * MIX_WIDTH ** -0.5),
        'ln1_g': 1.0 + nrm(ks[7], (DEPTH, D_MODEL), 0.01),
        'ln1_b': nrm(ks[8], (DEPTH, D_MODEL), 0.01),
        'w_router': nrm(ks[9], (DEPTH, D_MODEL, N_EXPERTS), D_MODEL ** -0.5),
        'router_bias': nrm(ks[10], (DEPTH, N_EXPERTS), 0.01),
        'we_gate': nrm(ks[11], (DEPTH, N_EXPERTS, D_MODEL, EXPERT_FF), D_MODEL ** -0.5),
        'we_up': nrm(ks[12], (DEPTH, N_EXPERTS, D_MODEL, EXPERT_FF), D_MODEL ** -0.5),
        'we_down': nrm(ks[13], (DEPTH, N_EXPERTS, EXPERT_FF, D_MODEL), BETA * EXPERT_FF ** -0.5),
        'ws_gate': nrm(ks[14], (DEPTH, D_MODEL, SHARED_FF), D_MODEL ** -0.5),
        'ws_up': nrm(ks[15], (DEPTH, D_MODEL, SHARED_FF), D_MODEL ** -0.5),
        'ws_down': nrm(ks[16], (DEPTH, SHARED_FF, D_MODEL), BETA * SHARED_FF ** -0.5),
        'ln2_g': 1.0 + nrm(ks[17], (DEPTH, D_MODEL), 0.01),
        'ln2_b': nrm(ks[18], (DEPTH, D_MODEL), 0.01),
    }

def reference(x, meta, ln0_g, ln0_b, w_in, b_forget, w_out, ln1_g, ln1_b, w_router, router_bias,
              we_gate, we_up, we_down, ws_gate, ws_up, ws_down, ln2_g, ln2_b):
    b, s, d = x.shape
    h = jnp.concatenate([jnp.broadcast_to(meta[None].astype(x.dtype), (b, N_META, d)), x], axis=1)
    h = layer_norm(h, ln0_g, ln0_b)
    l = h.shape[1]
    for i in range(DEPTH):
        h = layer_norm(ALPHA * h + hybrid_mixer(h, w_in[i], b_forget[i], w_out[i]), ln1_g[i], ln1_b[i])
        t = h.reshape(b * l, d)
        moe = swiglu(t, ws_gate[i], ws_up[i], ws_down[i]) + routed_experts(t, w_router[i], router_bias[i], we_gate[i], we_up[i], we_down[i])
        h = layer_norm(ALPHA * h + moe.reshape(b, l, d), ln2_g[i], ln2_b[i])
    return h[:, N_META:]


_drawn_inputs = setup_inputs


def setup_inputs(seed=0):
    import zlib

    import numpy as np

    out = dict(_drawn_inputs(seed))
    spreads = {}
    factors = {}
    for name, (base, spread) in spreads.items():
        noise = np.random.default_rng([zlib.crc32(name.encode()), seed]).standard_normal(out[name].shape)
        drawn = base * np.exp(spread * noise) if base else spread * noise
        out[name] = __import__('jax').numpy.asarray(drawn.astype(out[name].dtype))
    for name, factor in factors.items():
        out[name] = (out[name] * factor).astype(out[name].dtype)
    return out
```

```python
import math
from contextlib import ExitStack

import concourse.bass as bass
import numpy as np
from concourse import mybir

F32 = mybir.dt.float32
U32 = mybir.dt.uint32
I32 = mybir.dt.int32
ALU = mybir.AluOpType
ACT = mybir.ActivationFunctionType
AX = mybir.AxisListType

P = 128
D = 1024
DC = D // P
SEQ = 2048
NX = SEQ // P
META = 16
TOK = META + SEQ
NB = -(-TOK // P)
RH, RD = 4, 128
FH, FD = 8, 64
MIX = RH * RD + FH * FD
IN_COLS = 4 * RH * RD + 3 * FH * FD + FH
FQ0 = 4 * RH * RD
FK0 = FQ0 + FH * FD
FV0 = FK0 + FH * FD
FF0 = FV0 + FH * FD
PAIRS = FH // 2
NE, TOPK, NG, TOPG = 64, 6, 8, 4
GE = NE // NG
FF = 256
FC = FF // P
CAP = 256
SLOTS = SEQ
MAXOV = max(b for b in range(1, 200)
            if any(P * b + (CAP - P + 1) * n <= SEQ * TOPK and b <= n * ((SEQ - CAP) // P)
                   for n in range(1, NE + 1)))
EPS = 1e-5
NEG = -1e30
ALPHA = 2.0 ** 0.25
ROUTED = 2.5
BANK = 512
RC = P + 4


def constants():
    f = np.float32
    half = RD // 2
    inv = (f(10000.0) ** (-np.arange(half, dtype=f) / f(half))).astype(f)
    ang = (np.arange(TOK, dtype=f)[:, None] * inv[None, :]).astype(f)
    rope = np.concatenate([np.cos(ang), np.sin(ang)], 1).astype(f)
    lg = np.log1p(-np.exp2(-5.0 - np.arange(RH, dtype=np.float64)))
    i = np.arange(P, dtype=np.float64)
    scale = RD ** -0.5
    ret = np.zeros((RH, P, RC), f)
    for h in range(RH):
        causal = i[None, :] >= i[:, None]
        ret[h, :, :P] = np.where(causal, np.exp(-(i[:, None] + 1) * lg[h]) * scale, 0)
        ret[h, :, P] = np.exp((P - 1 - i) * lg[h]) * scale
        ret[h, :, P + 1] = np.exp((i + 1) * lg[h])
        ret[h, :, P + 2] = np.exp(P * lg[h])
        ret[h, :META, P + 3] = np.exp((META - 1 - i[:META]) * lg[h]) * scale
    ident = np.eye(P, dtype=f)
    causal = np.where(i[None, :] <= i[:, None], 0, NEG).astype(f)
    before = (i[:, None] < i[None, :]).astype(f)
    thr = np.broadcast_to(P * np.arange(CAP // P, SLOTS // P, dtype=f), (P, SLOTS // P - CAP // P))
    iota = np.broadcast_to(np.arange(NE, dtype=f), (P, NE))
    slot0 = np.broadcast_to(np.arange(NE, dtype=f) * SLOTS, (P, NE))
    pcol = i.astype(f)[:, None]
    square = np.concatenate([ident, causal, before, iota, slot0, thr, pcol], 1)
    return {"rope": rope, "retc": ret, "square": np.ascontiguousarray(square)}


SQ_IDENT, SQ_CAUSAL, SQ_BEFORE = 0, P, 2 * P
SQ_IOTA = 3 * P
SQ_SLOT0 = SQ_IOTA + NE
SQ_THR = SQ_SLOT0 + NE
NTHR = SLOTS // P - CAP // P
SQ_PCOL = SQ_THR + NTHR
SQ_COLS = SQ_PCOL + 1


class Phase:

    used = []

    def __init__(self, nc, name):
        self.nc, self.name, self.ctx = nc, name, ExitStack()

    def __enter__(self):
        self.ctx.__enter__()
        return self

    def __exit__(self, *a):
        return self.ctx.__exit__(*a)

    def sb(self, name, shape, dt=F32):
        return self.ctx.enter_context(self.nc.sbuf_tensor(f"{self.name}_{name}", shape, dt))

    def sem(self, name):
        self.used.append(self.nc.alloc_semaphore(name=f"{self.name}_{name}"))
        return self.used[-1]

    @classmethod
    def reset(cls, nc):
        nc.clear_and_free_semaphores(cls.used)
        cls.used = []
        nc.all_engine_barrier()

    def sems(self, name, n):
        return [self.sem(f"{name}{i}") for i in range(n)]

    def block(self):
        return self.ctx.enter_context(self.nc.Block())


def flat(ap):
    return ap.rearrange("p a b -> p (a b)")


def embed_phase(nc, ps, ident, hT, square, x, meta, ln_g, ln_b, ln_gcol, ln_bcol, w_in, b_forget, h_rows, v_rows, cq, ck):
    with Phase(nc, "emb") as ph:
        sb, sem = ph.sb, ph.sem
        gcol, bcol = sb("gcol", [P, DC]), sb("bcol", [P, DC])
        grow, brow = sb("grow", [P, D]), sb("brow", [P, D])
        wv = sb("wv", [P, DC, FH * FD])
        wf = sb("wf", [P, DC, FH])
        bf = sb("bf", [FH, 1])
        xin = [sb(f"xin{i}", [P, D]) for i in range(3)]
        xn = [sb(f"xn{i}", [P, D]) for i in range(2)]
        hr = [sb(f"hr{i}", [P, D]) for i in range(2)]
        vst = [sb(f"vst{i}", [P, FH * FD]) for i in range(2)]
        st = [sb(f"st{i}", [P, 2, 6]) for i in range(2)]
        mv = [sb(f"mv{i}", [P, 2]) for i in range(2)]
        ve = [sb(f"ve{i}", [P, 1]) for i in range(2)]
        rstd = [sb(f"rstd{i}", [P, 1]) for i in range(2)]
        mhalf = sb("mhalf", [P, 1])
        z, t1, t2 = sb("z", [FH, TOK]), sb("t1", [FH, TOK]), sb("t2", [FH, TOK])
        ones = sb("ones", [FH, TOK])
        const, wv_in, wf_in = sem("const"), sem("wv_in"), sem("wf_in")
        x_in, h_out, v_out = ph.sems("x_in", 3), ph.sems("h_out", 2), ph.sems("v_out", 2)
        half, stats, aggr, epsd, rstds, normed = (sem(n) for n in
                                                  ("half", "stats", "aggr", "epsd", "rstds", "normed"))
        scaled, hrow, turned, hT_a, hT_d = (sem(n) for n in ("scaled", "hrow", "turned", "hT_a", "hT_d"))
        v_done, v_copied, f_done, f_copied, ones_set = (sem(n) for n in
                                                        ("v_done", "v_copied", "f_done", "f_copied", "ones_set"))
        gate, gate_e, gate_a, c_out = (sem(n) for n in ("gate", "gate_e", "gate_a", "c_out"))
        NT = NX + 1
        rows = [META] + [P] * NX
        tok0 = [0] + [META + P * i for i in range(NX)]
        vrows = [min(P, TOK - P * b) for b in range(NB)]
        FCH = [(o, min(BANK, TOK - o)) for o in range(0, TOK, BANK)]
        f_tile = [-(-(o + n - META) // P) for o, n in FCH]
        block = ph.block()

        @block.sync
        def _(sp):
            def load(i):
                if i >= 3:
                    sp.wait_ge(normed, i - 2)
                src = meta if i == 0 else x[P * (i - 1):P * i, :]
                sp.dma_start(xin[i % 3][0:rows[i], :], src).then_inc(x_in[i % 3], 16)

            load(0)
            load(1)
            sp.dma_start(ident[:, :], square[:, SQ_IDENT:SQ_IDENT + P]).then_inc(const, 16)
            sp.dma_start(gcol[:, :], ln_gcol).then_inc(const, 16)
            sp.dma_start(bcol[:, :], ln_bcol).then_inc(const, 16)
            sp.dma_start(grow[:, :], ln_g.partition_broadcast(P)).then_inc(const, 16)
            sp.dma_start(brow[:, :], ln_b.partition_broadcast(P)).then_inc(const, 16)
            sp.dma_start(bf[:, :], b_forget.rearrange("(h o) -> h o", o=1)).then_inc(const, 16)
            load(2)
            w = w_in.rearrange("(c p) n -> p c n", p=P)
            sp.dma_start(wv[:, :, :], w[:, :, FV0:FV0 + FH * FD]).then_inc(wv_in, 16)
            sp.dma_start(wf[:, :, :], w[:, :, FF0:FF0 + FH]).then_inc(wf_in, 16)
            for i in range(NT):
                if i + 3 < NT:
                    load(i + 3)
                if i >= 1:
                    sp.wait_ge(hrow, i)
                    sp.dma_start(h_rows[P * (i - 1):P * i, :], hr[(i - 1) % 2][:, :]).then_inc(h_out[(i - 1) % 2], 16)
                for b in ([i - 1] if 1 <= i < NT - 1 else [NT - 2, NT - 1] if i == NT - 1 else []):
                    sp.wait_ge(v_copied, b + 1)
                    sp.dma_start(v_rows[P * b:P * b + vrows[b], :], vst[b % 2][0:vrows[b], :]).then_inc(v_out[b % 2], 16)
            sp.wait_ge(gate, 5)
            sp.dma_start(cq[:, 0, :], t1[:, :]).then_inc(c_out, 16)
            sp.dma_start(cq[:, 1, :], ones[:, :]).then_inc(c_out, 16)
            sp.dma_start(ck[:, 0, :], ones[:, :]).then_inc(c_out, 16)
            sp.dma_start(ck[:, 1, :], t2[:, :]).then_inc(c_out, 16)
            sp.wait_ge(c_out, 64)
            for i in range(2):
                sp.wait_ge(h_out[i], 16 * (NX // 2))
                sp.wait_ge(v_out[i], 16 * len(range(i, NB, 2)))

        @block.gpsimd
        def _(pool):
            pool.memset(mhalf[:, :], -0.5).then_inc(half, 1)
            pool.memset(ones[:, :], 1.0).then_inc(ones_set, 1)
            pool.wait_ge(half, 1)
            pool.wait_ge(const, 96)
            for i in range(NT):
                r = rows[i]
                pool.wait_ge(aggr, i + 1)
                pool.tensor_scalar(ve[i % 2][0:r, :], mv[i % 2][0:r, 1:2], EPS, None, ALU.add).then_inc(epsd, 1)
                pool.wait_ge(epsd, i + 1)
                pool.tensor_tensor(rstd[i % 2][0:r, :], ve[i % 2][0:r, :], mhalf[0:r, :], ALU.pow).then_inc(rstds, 1)
                if i >= 1:
                    pool.wait_ge(scaled, i)
                    k = (i - 1) % 2
                    pool.tensor_tensor(hr[k][:, :], hr[k][:, :], brow[:, :], ALU.add).then_inc(hrow, 1)

        @block.vector
        def _(dve):
            def moments(i):
                r = rows[i]
                dve.wait_ge(x_in[i % 3], 16 * (i // 3 + 1))
                for a in range(2):
                    dve.bn_stats(st[i % 2][0:r, a, :], xin[i % 3][0:r, a * BANK:(a + 1) * BANK]).then_inc(stats, 1)
                dve.wait_ge(stats, 2 * i + 2)
                if i >= 2:
                    dve.wait_ge(normed, i - 1)
                dve.bn_aggr(mv[i % 2][0:r, :], st[i % 2][0:r, :, :]).then_inc(aggr, 1)

            def normalise(i):
                r = rows[i]
                dve.wait_ge(rstds, i + 1)
                if i >= 2:
                    dve.wait_ge(turned, i - 1)
                dve.tensor_scalar(xn[i % 2][0:r, :], xin[i % 3][0:r, :], mv[i % 2][0:r, 0:1],
                                  rstd[i % 2][0:r, 0:1], ALU.subtract, ALU.mult).then_inc(normed, 1)

            def rest(i):
                r = rows[i]
                if i >= 1:
                    k = (i - 1) % 2
                    if i >= 3:
                        dve.wait_ge(h_out[k], 16 * ((i - 1) // 2))
                    dve.wait_ge(normed, i + 1)
                    dve.tensor_tensor(hr[k][:, :], xn[i % 2][:, :], grow[:, :], ALU.mult).then_inc(scaled, 1)
                dve.wait_ge(turned, i + 1)
                for c in range(4, DC):
                    ins = dve.tensor_scalar(hT[:, c, tok0[i]:tok0[i] + r],
                                            ps[:, 2 * (i % 2) + 1, (c - 4) * P:(c - 4) * P + r],
                                            gcol[:, c:c + 1], bcol[:, c:c + 1], ALU.mult, ALU.add)
                ins.then_inc(hT_d, 1)

            moments(0)
            dve.wait_ge(const, 96)
            for i in range(NT):
                normalise(i)
                if i + 1 < NT:
                    moments(i + 1)
                rest(i)
            dve.wait_ge(f_copied, len(FCH))
            dve.scalar_tensor_tensor(out=t1[:, :], in0=z[:, :], scalar=-1.0, in1=z[:, :],
                                     op0=ALU.mult, op1=ALU.min).then_inc(gate, 1)
            dve.wait_ge(gate_a, 1)
            dve.scalar_tensor_tensor(out=t2[:, :], in0=z[:, :], scalar=0.0, in1=t1[:, :],
                                     op0=ALU.min, op1=ALU.subtract).then_inc(gate, 1)
            dve.wait_ge(gate, 2)
            dve.wait_ge(ones_set, 1)
            dve.tensor_tensor_scan(t1[:, :], ones[:, :], t2[:, :], 0.0, ALU.mult, ALU.add).then_inc(gate, 1)
            dve.wait_ge(gate, 3)
            dve.tensor_scalar(t2[:, :], t1[:, :], -1.0, None, ALU.mult).then_inc(gate, 2)

        @block.scalar
        def _(act):
            act.wait_ge(const, 96)

            def copy_v(b):
                act.wait_ge(v_done, b + 1)
                if b >= 2:
                    act.wait_ge(v_out[b % 2], 16 * (b // 2))
                nc.scalar.copy(vst[b % 2][0:vrows[b], :], ps[0:vrows[b], 4 + b % 2, :]).then_inc(v_copied, 1)

            for i in range(NT):
                r = rows[i]
                act.wait_ge(turned, i + 1)
                for c in range(4):
                    ins = nc.scalar.activation(hT[:, c, tok0[i]:tok0[i] + r],
                                               ps[:, 2 * (i % 2), c * P:c * P + r], ACT.Identity,
                                               bias=bcol[:, c:c + 1], scale=gcol[:, c:c + 1])
                ins.then_inc(hT_a, 1)
                if i >= 2:
                    copy_v(i - 2)
                for k in (k for k, t in enumerate(f_tile) if t == i):
                    o, n = FCH[k]
                    act.wait_ge(f_done, k + 1)
                    nc.scalar.activation(z[:, o:o + n], ps[0:FH, 6 + k % 2, 0:n], ACT.Identity,
                                         bias=bf[:, 0:1]).then_inc(f_copied, 1)
                if i == NT - 1:
                    copy_v(NT - 2)
                    copy_v(NT - 1)
            act.wait_ge(gate, 1)
            nc.scalar.activation(t2[:, :], t1[:, :], ACT.Exp).then_inc(gate_e, 1)
            act.wait_ge(gate_e, 1)
            nc.scalar.activation(t1[:, :], t2[:, :], ACT.Ln, bias=1.0).then_inc(gate_a, 1)

        @block.tensor
        def _(pe):
            def turn(i):
                r = rows[i]
                pe.wait_ge(normed, i + 1)
                if i >= 2:
                    pe.wait_ge(hT_a, i - 1)
                    pe.wait_ge(hT_d, i - 1)
                for c in range(DC):
                    ins = pe.transpose(ps[:, 2 * (i % 2) + c // 4, (c % 4) * P:(c % 4) * P + r],
                                       xn[i % 2][0:r, c * P:(c + 1) * P], ident[0:r, 0:r])
                ins.then_inc(turned, 1)

            def values(b):
                pe.wait_ge(hT_a, min(b + 2, NT))
                pe.wait_ge(hT_d, min(b + 2, NT))
                if b >= 2:
                    pe.wait_ge(v_copied, b - 1)
                for c in range(DC):
                    ins = pe.matmul(ps[0:vrows[b], 4 + b % 2, :], hT[:, c, P * b:P * b + vrows[b]], wv[:, c, :],
                                    start=(c == 0), stop=(c == DC - 1))
                ins.then_inc(v_done, 1)

            def forget(k):
                o, n = FCH[k]
                if k >= 2:
                    pe.wait_ge(f_copied, k - 1)
                for c in range(DC):
                    ins = pe.matmul(ps[0:FH, 6 + k % 2, 0:n], wf[:, c, :], hT[:, c, o:o + n],
                                    start=(c == 0), stop=(c == DC - 1))
                ins.then_inc(f_done, 1)

            pe.wait_ge(const, 96)
            pe.wait_ge(wv_in, 16)
            pe.wait_ge(wf_in, 16)
            for i in range(NT):
                turn(i)
                if i >= 2:
                    values(i - 2)
                for k in (k for k, t in enumerate(f_tile) if t == i):
                    pe.wait_ge(hT_a, i + 1)
                    pe.wait_ge(hT_d, i + 1)
                    forget(k)
            values(NT - 2)
            values(NT - 1)


def retention_phase(nc, ps, ident, hT, w_in, rope, retc, mixed):
    with Phase(nc, "ret") as ph:
        sb, sem = ph.sb, ph.sem
        NM = NX + 1
        SLICES = 4
        cs, csm = sb("cs", [P, NX, RD]), sb("csm", [META, RD])
        wr = [sb(f"w{u}", [P, DC, 4 * RD]) for u in range(2)]
        rc = [sb(f"rc{u}", [P, RC]) for u in range(2)]
        qk = [sb(f"qk{b}", [P, 2 * RD]) for b in range(2)]
        v = [sb(f"v{b}", [P, RD]) for b in range(2)]
        vz = [sb(f"vz{b}", [P, RD]) for b in range(2)]
        cosd, sind = sb("cosd", [P, 2 * RD]), sb("sind", [P, 2 * RD])
        r = [sb(f"r{b}", [P, 2 * RD]) for b in range(2)]
        rT = [sb(f"rT{b}", [P, 2 * RD]) for b in range(2)]
        sT = [sb(f"sT{b}", [P, P]) for b in range(2)]
        S = [sb(f"S{b}", [RD, RD]) for b in range(2)]
        ret = [sb(f"ret{u}", [P, NX, RD]) for u in range(2)]
        sg = [sb(f"sg{u}", [P, NX, RD]) for u in range(2)]
        bn = [sb(f"bn{u}", [P, NX, 6]) for u in range(2)]
        mv = [sb(f"mv{u}", [P, NX, 2]) for u in range(2)]
        ve = [sb(f"ve{u}", [P, NX]) for u in range(2)]
        rstd = [sb(f"rstd{u}", [P, NX]) for u in range(2)]
        mhalf = sb("mhalf", [P, NX])
        tab, half = sem("tab"), sem("half")
        w_in_s = ph.sems("w_in", 2)
        proj, evac, products, rotated = (sem(n) for n in ("proj", "evac", "products", "rotated"))
        turned, turned_c, scored, masked, state_mm, state, att, out_c = (
            sem(n) for n in ("turned", "turned_c", "scored", "masked", "state_mm", "state", "att", "out_c"))
        moments, aggr, epsd, rstds, centred, gated = (
            sem(n) for n in ("moments", "aggr", "epsd", "rstds", "centred", "gated"))
        mix_out = ph.sems("mix_out", 2)
        spare = [sem(f"spare{i}") for i in range(3)]
        block = ph.block()
        w = w_in.rearrange("(c p) n -> p c n", p=P)

        @block.sync
        def _(sp):
            def load(h):
                u = h % 2
                if h >= 2:
                    sp.wait_ge(att, NX * (h - 1))
                    sp.wait_ge(state, NX * (h - 1))
                    sp.wait_ge(proj, NM * (h - 1))
                for s in range(SLICES):
                    sp.dma_start(wr[u][:, :, s * RD:(s + 1) * RD],
                                 w[:, :, (s * RH + h) * RD:(s * RH + h + 1) * RD]).then_inc(w_in_s[u], 16)
                sp.dma_start(rc[u][:, :], retc[h]).then_inc(w_in_s[u], 16)

            load(0)
            sp.dma_start(cs[:, :, :], rope[META:TOK, :].rearrange("(n p) d -> p n d", p=P)).then_inc(tab, 16)
            sp.dma_start(csm[:, :], rope[0:META, :]).then_inc(tab, 16)
            load(1)
            for h in range(RH):
                if h + 2 < RH:
                    load(h + 2)
                sp.wait_ge(gated, h + 1)
                sp.dma_start(mixed[:, h * RD:(h + 1) * RD].rearrange("(n p) d -> p n d", p=P),
                             ret[h % 2][:, :, :]).then_inc(mix_out[h % 2], 16)
            for u in range(2):
                sp.wait_ge(mix_out[u], 16 * (RH // 2))

        @block.gpsimd
        def _(pool):
            pool.memset(mhalf[:, :], -0.5).then_inc(half, 1)
            pool.wait_ge(half, 1)
            for h in range(RH):
                u = h % 2
                pool.wait_ge(aggr, NX * (h + 1))
                pool.tensor_scalar(ve[u][:, :], mv[u][:, :, 1], EPS, None, ALU.add).then_inc(epsd, 1)
                pool.wait_ge(epsd, h + 1)
                pool.tensor_tensor(rstd[u][:, :], ve[u][:, :], mhalf[:, :], ALU.pow).then_inc(rstds, 1)

        @block.scalar
        def _(act):
            act.wait_ge(w_in_s[0], 80)
            with act.Fori(0, RH // 2) as j:
                for u in range(2):
                    def evacuate(m):
                        b, n = (u + m) % 2, META if m == 0 else P
                        bank = ps[0:n, b, :]
                        act.wait_ge(proj, (j * 2 + u) * NM + m + 1)
                        if m == 2:
                            act.wait_ge(state_mm, (j * 2 + u) * NX + 1)
                        if m >= 3:
                            act.wait_ge(att, (j * 2 + u) * NX + m - 2)
                        if m == 0:
                            act.wait_ge(w_in_s[u], j * 80 + 80)
                            act.wait_ge(att, (j * 2 + u) * NX)
                            act.sem_inc(spare[0], 1)
                        zeta = rc[u][0:n, P + 3:P + 4] if m == 0 else rc[u][:, P:P + 1]
                        if m > 0:
                            nc.scalar.activation(qk[b][:, 0:RD], bank[:, 0:RD], ACT.Copy, scale=rc[u][:, P + 1:P + 2])
                            nc.scalar.copy(v[b][:, :], bank[:, 2 * RD:3 * RD])
                        nc.scalar.copy(qk[b][0:n, RD:2 * RD], bank[:, RD:2 * RD])
                        ins = nc.scalar.activation(vz[b][0:n, :], bank[:, 2 * RD:3 * RD], ACT.Copy, scale=zeta)
                        if m > 0:
                            ins = nc.scalar.activation(sg[u][:, m - 1, :], bank[:, 3 * RD:4 * RD], ACT.Silu)
                        ins.then_inc(evac, 1)

                    act.wait_ge(mix_out[u], j * 16)
                    act.sem_inc(spare[0], 1)
                    evacuate(0)
                    evacuate(1)
                    evacuate(2)
                    for n in range(NX):
                        m = n + 1
                        act.wait_ge(turned, (j * 2 + u) * NX + n + 1)
                        nc.scalar.copy(rT[n % 2][:, :], ps[:, 2, 0:2 * RD]).then_inc(turned_c, 1)
                        act.wait_ge(att, (j * 2 + u) * NX + n + 1)
                        nc.scalar.copy(ret[u][:, n, :], ps[:, 4 + n % 2, 0:RD]).then_inc(out_c, 1)
                        if m + 2 < NM:
                            evacuate(m + 2)

        @block.vector
        def _(dve):
            dve.wait_ge(tab, 32)
            with dve.Fori(0, RH // 2) as j:
                for u in range(2):
                    def rotate(m):
                        b, n = (u + m) % 2, META if m == 0 else P
                        g0 = 1 if m == 0 else 0
                        t = csm[0:n, :] if m == 0 else cs[:, m - 1, :]
                        four = lambda x: x.rearrange("p (g h d) -> p g h d", g=2, h=2)[0:n, g0:, :, :]
                        src, c4, s4, dst = four(qk[b][:, :]), four(cosd[:, :]), four(sind[:, :]), four(r[b][:, :])
                        tb = lambda a: t[:, a * 64:(a + 1) * 64].unsqueeze(1).to_broadcast([n, 2 - g0, 64])
                        dve.wait_ge(evac, (j * 2 + u) * NM + m + 1)
                        dve.wait_ge(rotated, ((j * 2 + u) * NM + m) * 2)
                        for h in range(2):
                            dve.tensor_tensor(c4[:, :, h, :], src[:, :, h, :], tb(0), ALU.mult).then_inc(products, 1)
                            dve.tensor_tensor(s4[:, :, h, :], src[:, :, 1 - h, :], tb(1), ALU.mult).then_inc(products, 1)
                        dve.wait_ge(products, ((j * 2 + u) * NM + m + 1) * 4)
                        dve.tensor_tensor(dst[:, :, 0, :], c4[:, :, 0, :], s4[:, :, 0, :], ALU.subtract).then_inc(rotated, 1)
                        dve.tensor_tensor(dst[:, :, 1, :], c4[:, :, 1, :], s4[:, :, 1, :], ALU.add).then_inc(rotated, 1)

                    def update(m):
                        dve.wait_ge(state_mm, (j * 2 + u) * NX + m + 1)
                        if m == 0:
                            dve.tensor_copy(S[0][:, :], ps[:, 6, 0:RD]).then_inc(state, 1)
                        else:
                            dve.wait_ge(state, (j * 2 + u) * NX + m)
                            dve.sem_inc(spare[1], 1)
                            dve.scalar_tensor_tensor(out=S[m % 2][:, :], in0=S[(m - 1) % 2][:, :],
                                                     scalar=rc[u][:, P + 2:P + 3], in1=ps[:, 6, 0:RD],
                                                     op0=ALU.mult, op1=ALU.add).then_inc(state, 1)

                    rotate(0)
                    rotate(1)
                    update(0)
                    rotate(2)
                    for n in range(NX):
                        m = n + 1
                        dve.wait_ge(scored, (j * 2 + u) * NX + n + 1)
                        dve.tensor_tensor(sT[n % 2][:, :], ps[:, 3, 0:P], rc[u][:, 0:P], ALU.mult).then_inc(masked, 1)
                        if m < NX:
                            update(m)
                        dve.wait_ge(out_c, (j * 2 + u) * NX + n + 1)
                        dve.bn_stats(bn[u][:, n, :], ret[u][:, n, :]).then_inc(moments, 1)
                        dve.wait_ge(moments, (j * 2 + u) * NX + n + 1)
                        dve.sem_inc(spare[1], 1)
                        dve.bn_aggr(mv[u][:, n, :], bn[u][:, n, :]).then_inc(aggr, 1)
                        if m + 2 < NM:
                            rotate(m + 2)
                    dve.wait_ge(rstds, j * 2 + u + 1)
                    dve.sem_inc(spare[1], 1)
                    for n in range(NX):
                        ins = dve.tensor_scalar(ret[u][:, n, :], ret[u][:, n, :], mv[u][:, n, 0:1], rstd[u][:, n:n + 1],
                                                ALU.subtract, ALU.mult)
                    ins.then_inc(centred, 1)
                    dve.wait_ge(centred, j * 2 + u + 1)
                    dve.sem_inc(spare[1], 1)
                    dve.tensor_tensor(flat(ret[u][:, :, :]), flat(ret[u][:, :, :]), flat(sg[u][:, :, :]),
                                      ALU.mult).then_inc(gated, 1)

        @block.tensor
        def _(pe):
            with pe.Fori(0, RH // 2) as j:
                for u in range(2):
                    def project(m):
                        n, t0 = (META, 0) if m == 0 else (P, META + P * (m - 1))
                        b = (u + m) % 2
                        lo, hi = (RD, 3 * RD) if m == 0 else (0, 4 * RD)
                        if m < 2:
                            if u == 1:
                                pe.wait_ge(evac, (j * 2 + u) * NM + m - 1)
                            else:
                                pe.wait_ge(evac, j * (2 * NM))
                        else:
                            pe.wait_ge(evac, (j * 2 + u) * NM + m - 1)
                        for c in range(DC):
                            ins = pe.matmul(ps[0:n, b, lo:hi], hT[:, c, t0:t0 + n], wr[u][:, c, lo:hi],
                                            start=(c == 0), stop=(c == DC - 1))
                        ins.then_inc(proj, 1)

                    def outer(m):
                        b, n = (u + m) % 2, META if m == 0 else P
                        if m == 0:
                            pe.wait_ge(rotated, ((j * 2 + u) * NM + m + 1) * 2)
                        pe.wait_ge(state, (j * 2 + u) * NX + m)
                        ins = pe.matmul(ps[:, 6, 0:RD], r[b][0:n, RD:2 * RD], vz[b][0:n, :], start=True, stop=True)
                        ins.then_inc(state_mm, 1)

                    pe.wait_ge(w_in_s[u], j * 80 + 80)
                    project(0)
                    project(1)
                    outer(0)
                    project(2)
                    for n in range(NX):
                        m = n + 1
                        b = (u + m) % 2
                        pe.wait_ge(rotated, ((j * 2 + u) * NM + m + 1) * 2)
                        pe.wait_ge(turned_c, (j * 2 + u) * NX + n)
                        for a in range(2):
                            ins = pe.transpose(ps[:, 2, a * RD:(a + 1) * RD], r[b][:, a * RD:(a + 1) * RD], ident[:, :])
                        ins.then_inc(turned, 1)
                        if m + 2 < NM:
                            project(m + 2)
                        pe.wait_ge(turned_c, (j * 2 + u) * NX + n + 1)
                        pe.matmul(ps[:, 3, 0:P], rT[n % 2][:, RD:2 * RD], rT[n % 2][:, 0:RD],
                                  start=True, stop=True).then_inc(scored, 1)
                        if m < NX:
                            outer(m)
                        pe.wait_ge(state, (j * 2 + u) * NX + m)
                        if n >= 2:
                            pe.wait_ge(out_c, (j * 2 + u) * NX + n - 1)
                        pe.matmul(ps[:, 4 + n % 2, 0:RD], rT[n % 2][:, 0:RD], S[(m - 1) % 2][:, :],
                                  start=True, stop=False)
                        pe.wait_ge(masked, (j * 2 + u) * NX + n + 1)
                        pe.matmul(ps[:, 4 + n % 2, 0:RD], sT[n % 2][:, :], v[b][:, :],
                                  start=False, stop=True).then_inc(att, 1)


def fox_phase(nc, ps, ident, hT, square, w_in, v_rows, cq, ck, mixed):
    with Phase(nc, "fox") as ph:
        sb, sem = ph.sb, ph.sem
        AUG = FD + 2
        wqk = [sb(f"w{u}", [P, DC, 4 * FD]) for u in range(2)]
        vp = [sb(f"v{u}", [P, NB, 2 * FD]) for u in range(2)]
        qa, ka = sb("qa", [AUG, 2, SEQ]), sb("ka", [AUG, 2, TOK])
        fo = [sb(f"fo{u}", [P, NX, 2 * FD]) for u in range(2)]
        prob = [sb(f"prob{b}", [P, TOK]) for b in range(2)]
        pT = [sb(f"pT{b}", [P, BANK]) for b in range(4)]
        causal = sb("causal", [P, P])
        nm = [sb(f"nm{b}", [P, 3]) for b in range(2)]
        rs = [sb(f"rs{b}", [P, 2]) for b in range(2)]
        rsum = [sb(f"rsum{b}", [P, 1]) for b in range(2)]
        rinv = [sb(f"rinv{b}", [P, 1]) for b in range(2)]
        tab = sem("tab")
        w_s, v_s = ph.sems("w", 2), ph.sems("v", 2)
        c_s, fox_out = sem("c"), ph.sems("out", 2)
        proj, proj_a, proj_d = sem("proj"), sem("proj_a"), sem("proj_d")
        s_a, s_b, capped, maxed, negm = (sem(n) for n in ("s_a", "s_b", "capped", "maxed", "negm"))
        exp_a, exp_b, turned, pt_a, pt_d = (sem(n) for n in ("exp_a", "exp_b", "turned", "pt_a", "pt_d"))
        attended, summed, inverted, normed = (sem(n) for n in ("attended", "summed", "inverted", "normed"))
        spare = [sem(f"spare{i}") for i in range(3)]
        HALF = 2 * BANK
        U = 2 * NX
        keys = [META + P * (i % NX + 1) for i in range(U)]
        wide = [k > HALF for k in keys]
        blocks = [-(-k // P) for k in keys]
        groups = [-(-n // 4) for n in blocks]
        before_b = [sum(wide[:i]) for i in range(U + 1)]
        before_g = [sum(groups[:i]) for i in range(U + 1)]
        ga = [min(2, g) for g in groups]
        before_a = [sum(ga[:i]) for i in range(U + 1)]
        before_d = [before_g[i] - before_a[i] for i in range(U + 1)]
        QCH = [(0, BANK * i, META + BANK * i, BANK) for i in range(SEQ // BANK)]
        KCH = [(1, o, o, min(BANK, TOK - o)) for o in range(0, TOK, BANK)]
        CH = QCH + KCH
        block = ph.block()
        w = w_in.rearrange("(c p) n -> p c n", p=P)
        flatps = ps[:, :, :].rearrange("p a b -> p (a b)")

        @block.sync
        def _(sp):
            def load(p):
                u = p % 2
                if p >= 2:
                    sp.wait_ge(normed, U * (p - 1))
                sp.dma_start(wqk[u][:, :, 0:2 * FD], w[:, :, FQ0 + 2 * FD * p:FQ0 + 2 * FD * (p + 1)]).then_inc(w_s[u], 16)
                sp.dma_start(wqk[u][:, :, 2 * FD:4 * FD], w[:, :, FK0 + 2 * FD * p:FK0 + 2 * FD * (p + 1)]).then_inc(w_s[u], 16)
                full = (NB - 1) * P
                sp.dma_start(vp[u][:, 0:NB - 1, :],
                             v_rows[0:full, 2 * FD * p:2 * FD * (p + 1)].rearrange("(n p) d -> p n d", p=P)).then_inc(v_s[u], 16)
                sp.dma_start(vp[u][0:TOK - full, NB - 1, :],
                             v_rows[full:TOK, 2 * FD * p:2 * FD * (p + 1)]).then_inc(v_s[u], 16)

            sp.dma_start(causal[:, :], square[:, SQ_CAUSAL:SQ_CAUSAL + P]).then_inc(tab, 16)
            load(0)
            load(1)
            for p in range(PAIRS):
                if p >= 1:
                    sp.wait_ge(normed, U * p)
                for a in range(2):
                    sp.dma_start(qa[FD:AUG, a, :], cq[2 * p + a, :, META:TOK]).then_inc(c_s, 16)
                    sp.dma_start(ka[FD:AUG, a, :], ck[2 * p + a]).then_inc(c_s, 16)
                if 1 <= p and p + 1 < PAIRS:
                    load(p + 1)
                if p >= 1:
                    sp.dma_start(mixed[:, RH * RD + 2 * FD * (p - 1):RH * RD + 2 * FD * p].rearrange("(n p) d -> p n d", p=P),
                                 fo[(p - 1) % 2][:, :, :]).then_inc(fox_out[(p - 1) % 2], 16)
            p = PAIRS
            sp.wait_ge(normed, U * p)
            sp.dma_start(mixed[:, RH * RD + 2 * FD * (p - 1):RH * RD + 2 * FD * p].rearrange("(n p) d -> p n d", p=P),
                         fo[(p - 1) % 2][:, :, :]).then_inc(fox_out[(p - 1) % 2], 16)
            for u in range(2):
                sp.wait_ge(fox_out[u], 16 * (PAIRS // 2))

        @block.scalar
        def _(act):
            with act.Fori(0, PAIRS // 2) as j:
                for pu in range(2):
                    p = j * 2 + pu

                    def proj_copy(t):
                        side, o, _, n = CH[t]
                        act.wait_ge(proj, p * len(CH) + t + 1)
                        if t == 0:
                            act.wait_ge(attended, p * U)
                            act.sem_inc(spare[0], 1)
                        dst = (ka if side else qa)[0:FD, 0, o:o + n]
                        nc.scalar.activation(dst, ps[0:FD, t % 4, 0:n], ACT.Copy,
                                             scale=1.0 if side else FD ** -0.5).then_inc(proj_a, 1)

                    def exps(i):
                        b, k = i % 2, keys[i]
                        act.wait_ge(negm, p * U + i + 1)
                        act.sem_inc(spare[0], 1)
                        if i >= 2:
                            act.wait_ge(normed, p * U + i - 1)
                        bias = nm[b][:, 2:3] if wide[i] else nm[b][:, 0:1]
                        n = min(k, HALF)
                        nc.scalar.activation(prob[b][:, 0:n], flatps[:, 0:n], ACT.Exp, bias=bias,
                                             accum_out=rs[b][:, 0:1]).then_inc(exp_a, 1)
                        if wide[i]:
                            nc.scalar.activation(prob[b][:, n:k], flatps[:, n:k], ACT.Exp, bias=bias,
                                                 accum_out=rs[b][:, 1:2]).then_inc(exp_b, 1)

                    def probs_back(i, g):
                        nb = blocks[i]
                        full = min(4, nb - 1 - 4 * g)
                        act.wait_ge(turned, p * before_g[U] + before_g[i] + g + 1)
                        ins = None
                        if full > 0:
                            ins = nc.scalar.copy(pT[g % 4][:, 0:full * P], ps[:, 5 + g % 2, 0:full * P])
                        if full < 4:
                            ins = nc.scalar.copy(pT[g % 4][0:META, full * P:(full + 1) * P],
                                                 ps[0:META, 5 + g % 2, full * P:(full + 1) * P])
                        ins.then_inc(pt_a, 1)

                    for t in range(len(CH)):
                        proj_copy(t)
                    exps(0)
                    for i in range(U):
                        for g in range(ga[i]):
                            probs_back(i, g)
                        if i + 1 < U:
                            exps(i + 1)

        @block.vector
        def _(dve):
            dve.wait_ge(tab, 16)
            with dve.Fori(0, PAIRS // 2) as j:
                for pu in range(2):
                    p = j * 2 + pu

                    def proj_copy(t):
                        side, o, _, n = CH[t]
                        dve.wait_ge(proj, p * len(CH) + t + 1)
                        if t == 0:
                            dve.wait_ge(attended, p * U)
                            dve.sem_inc(spare[1], 1)
                        dst = (ka if side else qa)[0:FD, 1, o:o + n]
                        dve.tensor_scalar(dst, ps[FD:2 * FD, t % 4, 0:n], 1.0 if side else FD ** -0.5, None,
                                          ALU.mult).then_inc(proj_d, 1)

                    def maxima(i):
                        b, k = i % 2, keys[i]
                        dve.wait_ge(s_a, p * U + i + 1)
                        dve.sem_inc(spare[1], 1)
                        diag = flatps[:, k - P:k]
                        n = min(k, HALF)
                        if i >= 2:
                            dve.wait_ge(exp_a, p * U + i - 1)
                            dve.wait_ge(exp_b, p * before_b[U] + before_b[i - 1])
                            dve.sem_inc(spare[1], 1)
                        if wide[i] and k - P < HALF:
                            dve.wait_ge(s_b, p * before_b[U] + before_b[i] + 1)
                        late = wide[i] and k - P >= HALF
                        if not late:
                            dve.tensor_tensor(diag, diag, causal[:, :], ALU.add).then_inc(capped, 1)
                            dve.wait_ge(capped, p * U + i + 1)
                        dve.tensor_reduce(nm[b][:, 0:1], flatps[:, 0:n], AX.X, ALU.max,
                                          negate=True).then_inc(maxed if wide[i] else negm, 1)
                        if wide[i]:
                            if late:
                                dve.wait_ge(s_b, p * before_b[U] + before_b[i] + 1)
                                dve.tensor_tensor(diag, diag, causal[:, :], ALU.add).then_inc(capped, 1)
                                dve.wait_ge(capped, p * U + i + 1)
                            dve.tensor_reduce(nm[b][:, 1:2], flatps[:, n:k], AX.X, ALU.max,
                                              negate=True).then_inc(maxed, 1)
                            dve.wait_ge(maxed, (p * before_b[U] + before_b[i] + 1) * 2)
                            dve.tensor_tensor(nm[b][:, 2:3], nm[b][:, 0:1], nm[b][:, 1:2], ALU.min).then_inc(negm, 1)

                    def probs_back(i, g):
                        nb = blocks[i]
                        full = min(4, nb - 1 - 4 * g)
                        dve.wait_ge(turned, p * before_g[U] + before_g[i] + g + 1)
                        if full > 0:
                            ins = dve.tensor_copy(pT[g % 4][:, 0:full * P], ps[:, 5 + g % 2, 0:full * P])
                        if full < 4:
                            ins = dve.tensor_copy(pT[g % 4][0:META, full * P:(full + 1) * P],
                                                  ps[0:META, 5 + g % 2, full * P:(full + 1) * P])
                        ins.then_inc(pt_d, 1)

                    def normalise(i):
                        b, a = i % 2, i // NX
                        dve.wait_ge(exp_a, p * U + i + 1)
                        src = rs[b][:, 0:1]
                        if wide[i]:
                            dve.wait_ge(exp_b, p * before_b[U] + before_b[i] + 1)
                            dve.sem_inc(spare[1], 1)
                            dve.tensor_tensor(rsum[b][:, :], rs[b][:, 0:1], rs[b][:, 1:2], ALU.add).then_inc(summed, 1)
                            dve.wait_ge(summed, p * before_b[U] + before_b[i] + 1)
                            src = rsum[b][:, :]
                        dve.reciprocal(rinv[b][:, :], src).then_inc(inverted, 1)
                        dve.wait_ge(inverted, p * U + i + 1)
                        dve.wait_ge(attended, p * U + i + 1)
                        dve.tensor_scalar(fo[pu][:, i % NX, a * FD:(a + 1) * FD], ps[:, 7, 0:FD], rinv[b][:, 0:1], None,
                                          ALU.mult).then_inc(normed, 1)

                    for t in range(len(CH)):
                        proj_copy(t)
                    dve.wait_ge(fox_out[pu], j * 16)
                    dve.sem_inc(spare[1], 1)
                    maxima(0)
                    for i in range(U):
                        if i + 1 < U:
                            maxima(i + 1)
                        for g in range(ga[i], groups[i]):
                            probs_back(i, g)
                        normalise(i)

        @block.tensor
        def _(pe):
            with pe.Fori(0, PAIRS // 2) as j:
                for pu in range(2):
                    p = j * 2 + pu

                    def project(t):
                        side, o, tok, n = CH[t]
                        if t >= 4:
                            pe.wait_ge(proj_a, p * len(CH) + t - 3)
                            pe.wait_ge(proj_d, p * len(CH) + t - 3)
                        for c in range(DC):
                            ins = pe.matmul(ps[:, t % 4, 0:n], wqk[pu][:, c, side * 2 * FD:(side + 1) * 2 * FD],
                                            hT[:, c, tok:tok + n], start=(c == 0), stop=(c == DC - 1))
                        ins.then_inc(proj, 1)

                    def scores(i):
                        k, a = keys[i], i // NX
                        q = qa[:, a, (i % NX) * P:(i % NX + 1) * P]
                        pe.wait_ge(exp_a, p * U + i)
                        for o in range(0, k, BANK):
                            n = min(BANK, k - o)
                            if o == HALF:
                                pe.wait_ge(exp_b, p * before_b[U] + before_b[i])
                            ins = pe.matmul(ps[:, o // BANK, 0:n], q, ka[:, a, o:o + n], start=True, stop=True)
                            if o + n == min(k, HALF):
                                ins.then_inc(s_a, 1)
                        if wide[i]:
                            ins.then_inc(s_b, 1)

                    def attend(i):
                        nb, a, b = blocks[i], i // NX, i % 2

                        def turn(g):
                            pe.wait_ge(pt_a, p * before_a[U] + before_a[i] + min(g, ga[i]))
                            if g >= 2:
                                pe.wait_ge(pt_d, p * before_d[U] + before_d[i] + g - 2)
                            else:
                                pe.wait_ge(pt_d, p * before_d[U] + before_d[i])
                            if 4 * g * P >= HALF:
                                pe.wait_ge(exp_b, p * before_b[U] + before_b[i] + 1)
                            for x in range(4 * g, min(4 * g + 4, nb)):
                                rows = META if x == nb - 1 else P
                                ins = pe.transpose(ps[0:rows, 5 + g % 2, (x % 4) * P:(x % 4 + 1) * P],
                                                   prob[b][:, x * P:x * P + rows], ident[:, :])
                            ins.then_inc(turned, 1)

                        def weigh(g):
                            if g < ga[i]:
                                pe.wait_ge(pt_a, p * before_a[U] + before_a[i] + g + 1)
                            else:
                                pe.wait_ge(pt_d, p * before_d[U] + before_d[i] + g - 1)
                            for x in range(4 * g, min(4 * g + 4, nb)):
                                rows = META if x == nb - 1 else P
                                ins = pe.matmul(ps[:, 7, 0:FD], pT[g % 4][0:rows, (x % 4) * P:(x % 4 + 1) * P],
                                                vp[pu][0:rows, x, a * FD:(a + 1) * FD],
                                                start=(x == 0), stop=(x == nb - 1))
                            return ins

                        pe.wait_ge(exp_a, p * U + i + 1)
                        pe.wait_ge(normed, p * U + i)
                        turn(0)
                        for g in range(groups[i]):
                            if g + 1 < groups[i]:
                                turn(g + 1)
                            ins = weigh(g)
                        ins.then_inc(attended, 1)

                    pe.wait_ge(w_s[pu], j * 32 + 32)
                    pe.wait_ge(exp_a, p * U)
                    for t in range(len(CH)):
                        project(t)
                    pe.wait_ge(proj_a, (p + 1) * len(CH))
                    pe.wait_ge(proj_d, (p + 1) * len(CH))
                    pe.wait_ge(c_s, (p + 1) * 64)
                    pe.wait_ge(v_s[pu], j * 32 + 32)
                    scores(0)
                    for i in range(U):
                        if i + 1 < U:
                            scores(i + 1)
                        attend(i)


def wide(ap):
    return ap.rearrange("p a b -> p (a b)")


def middle_phase(nc, ps, square, mixed, h_rows, w_out, ln_g, ln_b, w_router, router_bias,
                 ws_gate, ws_up, ws_down, t_rows, base_rows, table, route):
    ident, iota, tables = route.ident, route.iota, route.tables
    with Phase(nc, "mid") as ph:
        sb, sem = ph.sb, ph.sem
        wo = sb("wo", [P, MIX // P, D])
        wgu = sb("wgu", [P, DC, 2 * FF])
        wdn = sb("wdn", [P, FC, D])
        wr = sb("wr", [P, DC, NE])
        grow, brow, rb = sb("grow", [P, D]), sb("brow", [P, D]), sb("rb", [P, NE])
        blank = sb("blank", [P, 2 * NE * SLOTS // P])
        zrow = sb("zrow", [1, D])
        mix = [sb(f"mix{b}", [P, MIX]) for b in range(2)]
        y = [sb(f"y{b}", [P, D]) for b in range(2)]
        mT = sb("mT", [P, MIX // P, P])
        tT = sb("tT", [P, DC, P])
        t = [sb(f"t{b}", [P, D]) for b in range(2)]
        base = [sb(f"base{b}", [P, D]) for b in range(2)]
        st, mv, ve, rstd, mhalf = (sb(n, s) for n, s in (("st", [P, 2, 6]), ("mv", [P, 2]), ("ve", [P, 1]),
                                                          ("rstd", [P, 1]), ("mhalf", [P, 1])))
        sc = [sb(f"sc{b}", [P, NE]) for b in range(2)]
        sig, hs, h2, h2T = sb("sig", [P, FF]), sb("hs", [P, FF]), sb("h2", [P, FF]), sb("h2T", [P, FC, P])
        biased, masked = sb("biased", [P, NE]), sb("masked", [P, NE])
        g8, gs, gv, gif, gm = sb("g8", [P, NG, 8]), sb("gs", [P, NG]), sb("gv", [P, 8]), sb("gif", [P, 8]), sb("gm", [P, NG])
        gi, e8 = sb("gi", [P, 8], U32), sb("e8", [P, 8], U32)
        goh = sb("goh", [P, NG, TOPG])
        v8, ef = sb("v8", [P, 8]), sb("ef", [P, 8])
        oh, tmp = sb("oh", [P, TOPK, NE]), sb("tmp", [P, TOPK, NE])
        chosen = sb("chosen", [P, NE])
        gk, gsum, ginv, rk = sb("gk", [P, TOPK]), sb("gsum", [P, 1]), sb("ginv", [P, 1]), sb("rk", [P, TOPK])
        slot = [sb(f"slot{b}", [P, TOPK], U32) for b in range(2)]
        entry = [sb(f"entry{b}", [P, TOPK, 2]) for b in range(2)]
        w_s, const, cleared, blank_s = sem("w"), sem("const"), sem("cleared"), sem("blank")
        mix_in, h_in = ph.sems("mix_in", 2), ph.sems("h_in", 2)
        t_out, base_out, scat = ph.sems("t_out", 2), ph.sems("base_out", 2), ph.sems("scat", 2)
        mturned, mT_a, mT_d, projected, summed = (sem(n) for n in ("mturned", "mT_a", "mT_d", "projected", "summed"))
        stats, aggr, epsd, rstds, centred, scaled, t_ready = (
            sem(n) for n in ("stats", "aggr", "epsd", "rstds", "centred", "scaled", "t_ready"))
        tturned, tT_a, tT_d, routed, scored, gated_up, sigd, h_half, h_done, hturned, hT_c = (
            sem(n) for n in ("tturned", "tT_a", "tT_d", "routed", "scored", "gated_up", "sigd", "h_half", "h_done",
                             "hturned", "hT_c"))
        down, based, ranked, slotted, chain, run_s, tokens = (
            sem(n) for n in ("down", "based", "ranked", "slotted", "chain", "run", "tokens"))
        spare = [sem(f"spare{i}") for i in range(2)]
        block = ph.block()
        PAIRS_ = NX // 2
        CH_N = 20

        def pairs(eng, body):
            body(0)
            with eng.Fori(1, PAIRS_ - 1) as j:
                body(j)
            body(PAIRS_ - 1)

        def is_first(j, b):
            return isinstance(j, int) and j == 0 and b == 0

        def is_last(j, b):
            return isinstance(j, int) and j == PAIRS_ - 1 and b == 1

        def rows(ap, i):
            return ap[bass.ds(i * P, P), :]

        @block.sync
        def _(sp):
            def load(i, k, b):
                if k is not None:
                    sp.wait_ge(mturned, k)
                sp.dma_start(mix[b][:, :], rows(mixed, i)).then_inc(mix_in[b], 16)
                if k is not None:
                    sp.wait_ge(scaled, k)
                sp.dma_start(y[b][:, :], rows(h_rows, i)).then_inc(h_in[b], 16)

            load(0, None, 0)
            sp.dma_start(wo[:, :, :], w_out.rearrange("(c p) n -> p c n", p=P)).then_inc(w_s, 16)
            load(1, None, 1)
            sp.dma_start(grow[:, :], ln_g.partition_broadcast(P)).then_inc(const, 16)
            sp.dma_start(brow[:, :], ln_b.partition_broadcast(P)).then_inc(const, 16)
            sp.dma_start(rb[:, :], router_bias.partition_broadcast(P)).then_inc(const, 16)
            sp.dma_start(wr[:, :, :], w_router.rearrange("(c p) n -> p c n", p=P)).then_inc(w_s, 16)
            sp.dma_start(wgu[:, :, 0:FF], ws_gate.rearrange("(c p) n -> p c n", p=P)).then_inc(w_s, 16)
            sp.dma_start(wgu[:, :, FF:2 * FF], ws_up.rearrange("(c p) n -> p c n", p=P)).then_inc(w_s, 16)
            sp.dma_start(wdn[:, :, :], ws_down.rearrange("(c p) n -> p c n", p=P)).then_inc(w_s, 16)
            sp.wait_ge(blank_s, 2)
            sp.dma_start(table.rearrange("(p n) o -> p (n o)", p=P), blank[:, :]).then_inc(cleared, 16)
            sp.dma_start(t_rows[SEQ:SEQ + 1, :], zrow[:, :]).then_inc(cleared, 16)
            sp.dma_start(base_rows[SEQ:SEQ + 1, :], zrow[:, :]).then_inc(cleared, 16)

            def body(j):
                for b in range(2):
                    i = j * 2 + b
                    sp.wait_ge(t_ready, i + 1)
                    sp.dma_start(rows(t_rows, i), t[b][:, :]).then_inc(t_out[b], 16)
                    if not (isinstance(j, int) and j == PAIRS_ - 1):
                        load(i + 2, i + 1, b)
                    sp.wait_ge(based, i + 1)
                    sp.dma_start(rows(base_rows, i), base[b][:, :]).then_inc(base_out[b], 16)

            pairs(sp, body)
            for b in range(2):
                sp.wait_ge(t_out[b], 16 * PAIRS_)
                sp.wait_ge(base_out[b], 16 * PAIRS_)

        @block.gpsimd
        def _(pool):
            pool.memset(mhalf[:, :], -0.5).then_inc(tokens, 1)
            pool.memset(blank[:, :], float(SEQ)).then_inc(blank_s, 1)
            pool.memset(zrow[:, :], 0.0).then_inc(blank_s, 1)
            pool.memset(route.count[:, :], 0.0).then_inc(tokens, 1)
            for b in range(2):
                pool.wait_ge(tables, 16)
                pool.tensor_scalar(entry[b][:, :, 0], route.pcol.to_broadcast([P, TOPK]), float((b - 2) * P), None,
                                   ALU.add).then_inc(tokens, 1)
            pool.wait_ge(tokens, 4)
            pool.wait_ge(const, 48)

            def norm(i):
                pool.wait_ge(aggr, i + 1)
                pool.sem_inc(spare[0], 1)
                pool.tensor_scalar(ve[:, :], mv[:, 1:2], EPS, None, ALU.add).then_inc(epsd, 1)
                pool.wait_ge(epsd, i + 1)
                pool.tensor_tensor(rstd[:, :], ve[:, :], mhalf[:, :], ALU.pow).then_inc(rstds, 1)

            def shift(i, b):
                pool.wait_ge(scaled, i + 1)
                pool.tensor_tensor(t[b][:, :], t[b][:, :], brow[:, :], ALU.add).then_inc(t_ready, 1)

            def scatter(i, j, b):
                pool.wait_ge(scat[b], j * (16 * TOPK))
                pool.sem_inc(spare[0], 1)
                pool.tensor_scalar(entry[b][:, :, 0], entry[b][:, :, 0], float(2 * P), None, ALU.add).then_inc(tokens, 1)
                pool.wait_ge(tokens, i + 5)
                pool.wait_ge(slotted, i + 1)
                pool.sem_inc(spare[0], 1)
                for k in range(TOPK):
                    pool.indirect_dma_start(out=table, out_offset=bass.IndirectOffsetOnAxis(ap=slot[b][:, k:k + 1], axis=0),
                                            in_=entry[b][:, k, :], in_offset=None).then_inc(scat[b], 16)

            norm(0)
            shift(0, 0)
            pool.wait_ge(cleared, 48)

            def body(j):
                for b in range(2):
                    i = j * 2 + b
                    if not is_last(j, b):
                        norm(i + 1)
                        shift(i + 1, 1 - b)
                    if not is_first(j, b):
                        scatter(i - 1, j - 1 + b, 1 - b)

            pairs(pool, body)
            scatter(NX - 1, PAIRS_ - 1, 1)
            for b in range(2):
                pool.wait_ge(scat[b], 16 * TOPK * PAIRS_)

        @block.scalar
        def _(act):
            def mT_copy(i):
                act.wait_ge(mturned, i + 1)
                nc.scalar.copy(flat(mT[:, 0:4, :]), ps[:, 0, :]).then_inc(mT_a, 1)

            mT_copy(0)

            def body(j):
                for b in range(2):
                    i = j * 2 + b
                    if not is_last(j, b):
                        mT_copy(i + 1)
                    act.wait_ge(tturned, i + 1)
                    nc.scalar.copy(flat(tT[:, 0:4, :]), ps[:, 0, :]).then_inc(tT_a, 1)
                    act.wait_ge(chain, i * CH_N)
                    act.wait_ge(routed, i + 1)
                    act.sem_inc(spare[1], 1)
                    nc.scalar.activation(sc[b][:, :], ps[:, 6, 0:NE], ACT.Sigmoid).then_inc(scored, 1)
                    act.wait_ge(gated_up, i + 1)
                    act.wait_ge(h_done, i)
                    act.sem_inc(spare[1], 1)
                    nc.scalar.activation(sig[:, :], ps[:, 7, 0:FF], ACT.Sigmoid).then_inc(sigd, 1)
                    act.wait_ge(hturned, i + 1)
                    nc.scalar.copy(flat(h2T[:, :, :]), ps[:, 6, 0:FF]).then_inc(hT_c, 1)

            pairs(act, body)

        @block.vector
        def _(dve):
            dve.wait_ge(const, 48)
            dve.wait_ge(tables, 16)
            dve.wait_ge(tokens, 4)

            def mT_copy(i):
                dve.wait_ge(mturned, i + 1)
                dve.tensor_copy(flat(mT[:, 4:8, :]), ps[:, 1, :]).then_inc(mT_d, 1)

            def residual(i, b):
                dve.wait_ge(h_in[b], (i - b) * 8 + 16)
                dve.wait_ge(projected, i + 1)
                dve.sem_inc(spare[0], 1)
                dve.scalar_tensor_tensor(out=y[b][:, :], in0=y[b][:, :], scalar=ALPHA, in1=wide(ps[:, 2:4, :]),
                                         op0=ALU.mult, op1=ALU.add).then_inc(summed, 1)
                dve.wait_ge(summed, i + 1)
                for a in range(2):
                    dve.bn_stats(st[:, a, :], y[b][:, a * BANK:(a + 1) * BANK]).then_inc(stats, 1)
                dve.wait_ge(stats, i * 2 + 2)
                dve.wait_ge(scaled, i)
                dve.sem_inc(spare[0], 1)
                dve.bn_aggr(mv[:, :], st[:, :, :]).then_inc(aggr, 1)
                dve.wait_ge(rstds, i + 1)
                dve.wait_ge(aggr, i + 1)
                dve.sem_inc(spare[0], 1)
                dve.tensor_scalar(y[b][:, :], y[b][:, :], mv[:, 0:1], rstd[:, 0:1], ALU.subtract, ALU.mult).then_inc(centred, 1)
                dve.wait_ge(t_out[b], (i - b) * 8)
                dve.wait_ge(centred, i + 1)
                dve.sem_inc(spare[0], 1)
                dve.tensor_tensor(t[b][:, :], y[b][:, :], grow[:, :], ALU.mult).then_inc(scaled, 1)

            def pick(i, b, at):
                n = [0]

                def link(ins, hold=False):
                    n[0] += 1
                    ins.then_inc(chain, 1)
                    dve.wait_ge(chain, i * CH_N + n[0])
                    if hold:
                        dve.sem_inc(spare[0], 1)

                dve.wait_ge(scored, i + 1)
                link(dve.tensor_tensor(biased[:, :], sc[b][:, :], rb[:, :], ALU.add), True)
                for g in range(NG):
                    ins = dve.max(g8[:, g, :], biased[:, g * GE:(g + 1) * GE])
                link(ins)
                link(dve.tensor_tensor(gs[:, :], g8[:, :, 0], g8[:, :, 1], ALU.add), True)
                link(dve.max(gv[:, :], gs[:, :]), True)
                link(dve.max_index(gi[:, :], gv[:, :], gs[:, :]))
                link(dve.tensor_copy(gif[:, :], gi[:, :]))
                link(dve.tensor_tensor(goh[:, :, :], iota[:, 0:NG].unsqueeze(2).to_broadcast([P, NG, TOPG]),
                                       gif[:, 0:TOPG].unsqueeze(1).to_broadcast([P, NG, TOPG]), ALU.is_equal))
                link(dve.tensor_reduce(gm[:, :], goh[:, :, :], AX.X, ALU.max))
                link(dve.tensor_scalar(gm[:, :], gm[:, :], -1.0, -NEG, ALU.add, ALU.mult))
                link(dve.tensor_tensor(masked[:, :].rearrange("p (g e) -> p g e", g=NG),
                                       biased[:, :].rearrange("p (g e) -> p g e", g=NG),
                                       gm[:, :].unsqueeze(2).to_broadcast([P, NG, GE]), ALU.add), True)
                link(dve.max(v8[:, :], masked[:, :]), True)
                link(dve.max_index(e8[:, :], v8[:, :], masked[:, :]))
                link(dve.tensor_copy(ef[:, :], e8[:, :]))
                link(dve.tensor_tensor(oh[:, :, :], iota.unsqueeze(1).to_broadcast([P, TOPK, NE]),
                                       ef[:, 0:TOPK].unsqueeze(2).to_broadcast([P, TOPK, NE]), ALU.is_equal))
                link(dve.tensor_reduce(chosen[:, :], oh[:, :, :].rearrange("p k e -> p e k"), AX.X, ALU.add))
                link(dve.tensor_tensor(tmp[:, :, :], oh[:, :, :], sc[b][:, :].unsqueeze(1).to_broadcast([P, TOPK, NE]),
                                       ALU.mult))
                link(dve.tensor_reduce(gk[:, :], tmp[:, :, :], AX.X, ALU.add))
                link(dve.tensor_reduce(gsum[:, :], gk[:, :], AX.X, ALU.add))
                link(dve.reciprocal(ginv[:, :], gsum[:, :]))
                dve.sem_inc(spare[0], 1)
                link(dve.tensor_scalar(route.gate[:, at, :], gk[:, :], ginv[:, 0:1], ROUTED, ALU.mult, ALU.mult))
                assert n[0] == CH_N

            def number(i, j, b, at):
                dve.wait_ge(ranked, i + 1)
                dve.tensor_tensor(tmp[:, :, :], oh[:, :, :], ps[:, 6, 0:NE].unsqueeze(1).to_broadcast([P, TOPK, NE]),
                                  ALU.mult).then_inc(run_s, 1)
                dve.wait_ge(run_s, i * 3 + 1)
                dve.tensor_reduce(rk[:, :], tmp[:, :, :], AX.X, ALU.add).then_inc(run_s, 1)
                dve.wait_ge(run_s, i * 3 + 2)
                dve.wait_ge(scat[b], j * (16 * TOPK))
                dve.sem_inc(spare[0], 1)
                dve.tensor_copy(route.expert[:, at, :], ef[:, 0:TOPK])
                dve.tensor_copy(route.rank[:, at, :], rk[:, :])
                dve.tensor_copy(entry[b][:, :, 1], route.gate[:, at, :].rearrange("p a k -> p (a k)"))
                dve.tensor_tensor(route.count[:, :], route.count[:, :], chosen[:, :], ALU.add).then_inc(run_s, 1)
                dve.scalar_tensor_tensor(out=slot[b][:, :], in0=ef[:, 0:TOPK], scalar=float(SLOTS), in1=rk[:, :],
                                         op0=ALU.mult, op1=ALU.add).then_inc(slotted, 1)

            mT_copy(0)
            residual(0, 0)

            def body(j):
                for b in range(2):
                    i = j * 2 + b
                    prev = (i - 1) if isinstance(j, int) else bass.ds(i - 1, 1)
                    if not is_last(j, b):
                        mT_copy(i + 1)
                    if not is_first(j, b):
                        pick_at(i - 1, 1 - b)
                    dve.wait_ge(tturned, i + 1)
                    dve.tensor_copy(flat(tT[:, 4:8, :]), ps[:, 1, :]).then_inc(tT_d, 1)
                    if not is_last(j, b):
                        residual(i + 1, 1 - b)
                    dve.wait_ge(sigd, i + 1)
                    dve.tensor_tensor(hs[:, :], sig[:, :], ps[:, 7, 0:FF], ALU.mult).then_inc(h_half, 1)
                    dve.wait_ge(h_half, i + 1)
                    dve.tensor_tensor(h2[:, :], hs[:, :], ps[:, 7, FF:2 * FF], ALU.mult).then_inc(h_done, 1)
                    if not is_first(j, b):
                        number_at(i - 1, j - 1 + b, 1 - b)
                    dve.wait_ge(base_out[b], j * 16)
                    dve.wait_ge(down, i + 1)
                    dve.wait_ge(t_ready, i + 1)
                    dve.sem_inc(spare[0], 1)
                    dve.scalar_tensor_tensor(out=base[b][:, :], in0=t[b][:, :], scalar=ALPHA, in1=wide(ps[:, 4:6, :]),
                                             op0=ALU.mult, op1=ALU.add).then_inc(based, 1)

            def sl(i):
                return slice(i, i + 1) if isinstance(i, int) else bass.ds(i, 1)

            def pick_at(i, b):
                pick(i, b, sl(i))

            def number_at(i, j, b):
                number(i, j, b, sl(i))

            pairs(dve, body)
            pick_at(NX - 1, 1)
            number_at(NX - 1, PAIRS_ - 1, 1)

        @block.tensor
        def _(pe):
            def project(i, b):
                pe.wait_ge(mix_in[b], (i - b) * 8 + 16)
                if not (isinstance(i, int) and i == 0):
                    pe.wait_ge(tT_a, i - 1)
                    pe.wait_ge(tT_d, i - 1)
                for c in range(MIX // P):
                    ins = pe.transpose(ps[:, c // 4, (c % 4) * P:(c % 4 + 1) * P], mix[b][:, c * P:(c + 1) * P], ident)
                ins.then_inc(mturned, 1)
                pe.wait_ge(mT_a, i + 1)
                pe.wait_ge(mT_d, i + 1)
                pe.wait_ge(summed, i)
                for a in range(2):
                    for c in range(MIX // P):
                        ins = pe.matmul(ps[:, 2 + a, :], mT[:, c, :], wo[:, c, a * BANK:(a + 1) * BANK],
                                        start=(c == 0), stop=(c == MIX // P - 1))
                ins.then_inc(projected, 1)

            def rank(i):
                pe.wait_ge(chain, i * CH_N + 15)
                pe.wait_ge(run_s, i * 3)
                pe.matmul(ps[:, 6, 0:NE], route.before, chosen[:, :], start=True, stop=False)
                pe.matmul(ps[:, 6, 0:NE], route.ones[:, :], route.count[:, :], start=False, stop=True).then_inc(ranked, 1)

            pe.wait_ge(w_s, 16 * 5)
            pe.wait_ge(tables, 16)
            pe.wait_ge(route.ones_set, 1)
            project(0, 0)

            def body(j):
                for b in range(2):
                    i = j * 2 + b
                    if not is_last(j, b):
                        project(i + 1, 1 - b)
                        pe.wait_ge(mT_a, i + 2)
                        pe.wait_ge(mT_d, i + 2)
                    pe.wait_ge(t_ready, i + 1)
                    for c in range(DC):
                        ins = pe.transpose(ps[:, c // 4, (c % 4) * P:(c % 4 + 1) * P], t[b][:, c * P:(c + 1) * P], ident)
                    ins.then_inc(tturned, 1)
                    pe.wait_ge(tT_a, i + 1)
                    pe.wait_ge(tT_d, i + 1)
                    pe.wait_ge(hT_c, i)
                    for c in range(DC):
                        ins = pe.matmul(ps[:, 6, 0:NE], tT[:, c, :], wr[:, c, :], start=(c == 0), stop=(c == DC - 1))
                    ins.then_inc(routed, 1)
                    pe.wait_ge(h_done, i)
                    for c in range(DC):
                        ins = pe.matmul(ps[:, 7, :], tT[:, c, :], wgu[:, c, :], start=(c == 0), stop=(c == DC - 1))
                    ins.then_inc(gated_up, 1)
                    pe.wait_ge(scored, i + 1)
                    if not is_first(j, b):
                        rank(i - 1)
                        pe.wait_ge(run_s, i * 3 - 2)
                    pe.wait_ge(h_done, i + 1)
                    for c in range(FC):
                        ins = pe.transpose(ps[:, 6, c * P:(c + 1) * P], h2[:, c * P:(c + 1) * P], ident)
                    ins.then_inc(hturned, 1)
                    pe.wait_ge(hT_c, i + 1)
                    pe.wait_ge(based, i)
                    for a in range(2):
                        for c in range(FC):
                            ins = pe.matmul(ps[:, 4 + a, :], h2T[:, c, :], wdn[:, c, a * BANK:(a + 1) * BANK],
                                            start=(c == 0), stop=(c == FC - 1))
                    ins.then_inc(down, 1)

            pairs(pe, body)
            rank(NX - 1)


class Route:

    def __init__(self, nc, ctx):
        sb = lambda n, s, dt=F32: ctx.enter_context(nc.sbuf_tensor(n, s, dt))
        self.sq = sb("sq", [P, SQ_COLS])
        self.ident = self.sq[:, SQ_IDENT:SQ_IDENT + P]
        self.causal = self.sq[:, SQ_CAUSAL:SQ_CAUSAL + P]
        self.before = self.sq[:, SQ_BEFORE:SQ_BEFORE + P]
        self.iota = self.sq[:, SQ_IOTA:SQ_IOTA + NE]
        self.slot0 = self.sq[:, SQ_SLOT0:SQ_SLOT0 + NE]
        self.thr = self.sq[:, SQ_THR:SQ_THR + NTHR]
        self.pcol = self.sq[:, SQ_PCOL:SQ_PCOL + 1]
        self.ones = sb("ones", [P, P])
        self.count = sb("count", [P, NE])
        self.expert = sb("expert", [P, NX, TOPK])
        self.rank = sb("rank", [P, NX, TOPK])
        self.gate = sb("gate", [P, NX, TOPK])
        self.extra0 = sb("extra0", [P, NE])
        self.index = sb("index", [P, NE * (CAP // P)], U32)
        self.over = sb("over", [1, 2 * P], I32)
        self.n_over = sb("n_over", [1, 1], I32)
        self.tables = ctx.enter_context(nc.semaphore("tables"))
        self.ones_set = ctx.enter_context(nc.semaphore("ones_set"))


def table_phase(nc, ps, table, over_rows, route):
    NBLK = NE * (CAP // P)
    with Phase(nc, "tab") as ph:
        sb, sem = ph.sb, ph.sem
        lists = sb("lists", [NBLK, P, 2])
        cnt, more, nov, end = sb("cnt", [P, NE]), sb("more", [P, NE, NTHR]), sb("nov", [P, NE]), sb("end", [P, NE])
        a_, b_, m_ = sb("a", [P, NE]), sb("b", [P, NE]), sb("m", [P, NE])
        place, onesr = sb("place", [P, NE]), sb("onesr", [P, NE])
        ej, sj, both = sb("ej", [P, 1]), sb("sj", [P, 1]), sb("both", [P, 2], I32)
        listed, turned, counted, chain, over_s, back, done = (
            sem(n) for n in ("listed", "turned", "counted", "chain", "over", "back", "done"))
        block = ph.block()

        @block.sync
        def _(sp):
            src = table.rearrange("(e b p) o -> e b (p o)", b=SLOTS // P, p=P)
            for k in range(CAP // P):
                sp.dma_start(flat(lists[k * NE:(k + 1) * NE, :, :]), src[:, k, :]).then_inc(listed, 16)
            sp.wait_ge(done, 1)
            sp.dma_start(over_rows, both[:, :]).then_inc(over_s, 16)
            sp.wait_ge(over_s, 16)
            sp.dma_start(route.over[:, :], over_rows.rearrange("(o p) k -> o (p k)", o=1)).then_inc(back, 16)
            sp.wait_ge(back, 16)

        @block.tensor
        def _(pe):
            pe.matmul(ps[:, 0, 0:NE], route.ones[:, :], route.count[:, :], start=True, stop=True).then_inc(counted, 1)
            pe.wait_ge(listed, 16 * (CAP // P))
            pe.transpose(ps[:, 1, 0:NBLK], lists[:, :, 0], route.ident).then_inc(turned, 1)

        @block.vector
        def _(dve):
            n = [0]

            def link(ins):
                n[0] += 1
                ins.then_inc(chain, 1)
                dve.wait_ge(chain, n[0])

            link(dve.memset(onesr[:, :], 1.0))
            dve.wait_ge(counted, 1)
            link(dve.tensor_copy(cnt[:, :], ps[:, 0, 0:NE]))
            link(dve.tensor_tensor(more[:, :, :], cnt[:, :].unsqueeze(2).to_broadcast([P, NE, NTHR]),
                                   route.thr.unsqueeze(1).to_broadcast([P, NE, NTHR]), ALU.is_gt))
            link(dve.tensor_reduce(nov[:, :], more[:, :, :], AX.X, ALU.add))
            link(dve.tensor_tensor_scan(end[:, :], onesr[:, :], nov[:, :], 0.0, ALU.mult, ALU.add))
            link(dve.tensor_tensor(route.extra0[:, :], end[:, :], nov[:, :], ALU.subtract))
            link(dve.tensor_copy(route.n_over[:, :], end[0:1, NE - 1:NE]))
            link(dve.tensor_scalar(a_[:, :], route.extra0[:, :], route.pcol, None, ALU.is_le))
            link(dve.tensor_scalar(b_[:, :], end[:, :], route.pcol, None, ALU.is_gt))
            link(dve.tensor_tensor(m_[:, :], a_[:, :], b_[:, :], ALU.mult))
            link(dve.tensor_tensor(a_[:, :], m_[:, :], route.iota, ALU.mult))
            link(dve.tensor_reduce(ej[:, :], a_[:, :], AX.X, ALU.add))
            link(dve.scalar_tensor_tensor(out=place[:, :], in0=route.extra0[:, :], scalar=-float(P), in1=route.slot0,
                                          op0=ALU.mult, op1=ALU.add))
            link(dve.tensor_scalar(a_[:, :], route.pcol.to_broadcast([P, NE]), float(P), float(CAP), ALU.mult, ALU.add))
            link(dve.tensor_tensor(place[:, :], place[:, :], a_[:, :], ALU.add))
            link(dve.tensor_tensor(b_[:, :], m_[:, :], place[:, :], ALU.mult))
            link(dve.tensor_reduce(sj[:, :], b_[:, :], AX.X, ALU.add))
            link(dve.tensor_copy(both[:, 0:1], ej[:, :]))
            dve.tensor_copy(both[:, 1:2], sj[:, :]).then_inc(done, 1)
            dve.wait_ge(turned, 1)
            link(dve.tensor_copy(route.index[:, :], ps[:, 1, 0:NBLK]))


def expert_phase(nc, ps, t_rows, we_gate, we_up, we_down, y_rows, route):
    with Phase(nc, "exp") as ph:
        sb, sem = ph.sb, ph.sem
        NBK = CAP // P
        wg = [sb(f"wg{u}", [P, DC, FF]) for u in range(2)]
        wu = [sb(f"wu{u}", [P, DC, FF]) for u in range(2)]
        wd = [sb(f"wd{u}", [P, FC, D]) for u in range(2)]
        xg = [[sb(f"xg{u}{k}", [P, D]) for k in range(NBK)] for u in range(2)]
        ix = [[sb(f"ix{u}{k}", [P, 1], U32) for k in range(NBK)] for u in range(2)]
        xT = [sb(f"xT{u}", [P, DC, CAP]) for u in range(2)]
        sl = [sb(f"sl{f}", [P, CAP]) for f in range(FC)]
        hh = [sb(f"hh{u}", [P, FC, CAP]) for u in range(2)]
        yo = [[sb(f"yo{u}{k}", [P, D]) for k in range(NBK)] for u in range(2)]
        wgu_in, wd_in, x_in = ph.sems("wgu_in", 2), ph.sems("wd_in", 2), ph.sems("x_in", 4)
        y_out = ph.sems("y_out", 4)
        turned, gu, down = ph.sems("turned", 2), ph.sems("gu", 2), ph.sems("down", 2)
        ixd, xT_a, xT_d, silud, hd, y_a, y_d = (sem(n) for n in ("ixd", "xT_a", "xT_d", "silud", "hd", "y_a", "y_d"))
        spare = [sem(f"spare{i}") for i in range(2)]
        block = ph.block()
        N2 = NE // 2

        @block.sync
        def _(sp):
            with sp.Fori(0, N2) as j:
                for u in range(2):
                    e = j * 2 + u
                    one = lambda w: w[bass.ds(e, 1)].rearrange("a (c p) f -> p (a c) f", p=P)
                    sp.wait_ge(gu[u], j * FC)
                    sp.dma_start(wg[u][:, :, :], one(we_gate)).then_inc(wgu_in[u], 16)
                    sp.dma_start(wu[u][:, :, :], one(we_up)).then_inc(wgu_in[u], 16)
                    sp.wait_ge(down[u], j * NBK)
                    sp.dma_start(wd[u][:, :, :], one(we_down)).then_inc(wd_in[u], 16)

        @block.gpsimd
        def _(pool):
            with pool.Fori(0, N2) as j:
                for u in range(2):
                    for k in range(NBK):
                        s = u * NBK + k
                        pool.wait_ge(x_in[s], j * 16)
                        pool.sem_inc(spare[0], 1)
                        pool.tensor_copy(ix[u][k][:, :], route.index[:, bass.ds(j * 2 + (u + k * NE), 1)]).then_inc(ixd, 1)
                        pool.wait_ge(ixd, j * (2 * NBK) + s + 1)
                        pool.wait_ge(turned[u], j * (2 * NBK))
                        pool.sem_inc(spare[0], 1)
                        pool.indirect_dma_start(out=xg[u][k][:, :], out_offset=None, in_=t_rows,
                                                in_offset=bass.IndirectOffsetOnAxis(ap=ix[u][k][:, :], axis=0)
                                                ).then_inc(x_in[s], 16)

        def run(eng, body):
            with eng.Fori(0, N2 - 1) as j:
                body(j)
            body(N2 - 1)

        def last(j, u):
            return isinstance(j, int) and u == 1

        @block.scalar
        def _(act):
            def x_copy(j, u, g):
                act.wait_ge(turned[u], j * 4 + g + 1)
                k = g // 2
                nc.scalar.copy(xT[u][:, 0:4, k * P:(k + 1) * P],
                               ps[:, 0, :].rearrange("p (c t) -> p c t", c=4)).then_inc(xT_a, 1)

            x_copy(0, 0, 0)
            x_copy(0, 0, 2)

            def body(j):
                for u in range(2):
                    e = j * 2 + u
                    for f in range(FC):
                        act.wait_ge(gu[u], j * FC + f + 1)
                        act.wait_ge(hd, e * FC)
                        act.sem_inc(spare[1], 1)
                        nc.scalar.activation(sl[f][:, :], ps[:, 2 + f, 0:CAP], ACT.Silu).then_inc(silud, 1)
                    if not last(j, u):
                        x_copy(j + u, 1 - u, 0)
                    for k in range(NBK):
                        act.wait_ge(y_out[u * NBK + k], j * 16)
                        act.wait_ge(down[u], j * NBK + k + 1)
                        act.sem_inc(spare[1], 1)
                        nc.scalar.copy(yo[u][k][:, 0:BANK], ps[:, 4 + 2 * k, :]).then_inc(y_a, 1)
                        if k == 0 and not last(j, u):
                            x_copy(j + u, 1 - u, 2)
                        act.wait_ge(y_d, e * NBK + k + 1)
                        act.wait_ge(y_a, e * NBK + k + 1)
                        act.dma_start(y_rows[bass.ds(e * CAP + k * P, P), :], yo[u][k][:, :]).then_inc(y_out[u * NBK + k], 16)

            run(act, body)
            for s in range(2 * NBK):
                act.wait_ge(y_out[s], 16 * N2)

        @block.vector
        def _(dve):
            def x_copy(j, u, g):
                dve.wait_ge(turned[u], j * 4 + g + 1)
                k = g // 2
                dve.tensor_copy(xT[u][:, 4:8, k * P:(k + 1) * P],
                                ps[:, 1, :].rearrange("p (c t) -> p c t", c=4)).then_inc(xT_d, 1)

            x_copy(0, 0, 1)
            x_copy(0, 0, 3)

            def body(j):
                for u in range(2):
                    e = j * 2 + u
                    for f in range(FC):
                        dve.wait_ge(silud, e * FC + f + 1)
                        dve.tensor_tensor(hh[u][:, f, :], sl[f][:, :], ps[:, 2 + f, CAP:2 * CAP], ALU.mult).then_inc(hd, 1)
                    if not last(j, u):
                        x_copy(j + u, 1 - u, 1)
                    for k in range(NBK):
                        dve.wait_ge(y_out[u * NBK + k], j * 16)
                        dve.wait_ge(down[u], j * NBK + k + 1)
                        dve.sem_inc(spare[0], 1)
                        dve.tensor_copy(yo[u][k][:, BANK:D], ps[:, 5 + 2 * k, :]).then_inc(y_d, 1)
                        if k == 0 and not last(j, u):
                            x_copy(j + u, 1 - u, 3)

            run(dve, body)

        @block.tensor
        def _(pe):
            def turn(e, j, u, g):
                k, h = g // 2, g % 2
                if h == 0:
                    pe.wait_ge(x_in[u * NBK + k], j * 16 + 16)
                pe.wait_ge(xT_d if h else xT_a, e * 2 + k)
                for c in range(4):
                    ins = pe.transpose(ps[:, h, c * P:(c + 1) * P], xg[u][k][:, (4 * h + c) * P:(4 * h + c + 1) * P],
                                       route.ident)
                ins.then_inc(turned[u], 1)

            for g in range(4):
                turn(0, 0, 0, g)

            def body(j):
                for u in range(2):
                    e = j * 2 + u
                    pe.wait_ge(xT_a, e * 2 + 2)
                    pe.wait_ge(xT_d, e * 2 + 2)
                    pe.wait_ge(wgu_in[u], j * 32 + 32)
                    for f in range(FC):
                        pe.wait_ge(hd, e * FC)
                        for s, w in enumerate((wg[u], wu[u])):
                            for c in range(DC):
                                ins = pe.matmul(ps[:, 2 + f, s * CAP:(s + 1) * CAP], w[:, c, f * P:(f + 1) * P],
                                                xT[u][:, c, :], start=(c == 0), stop=(c == DC - 1))
                        ins.then_inc(gu[u], 1)
                    nj = j + u
                    if not last(j, u):
                        turn(e + 1, nj, 1 - u, 0)
                        turn(e + 1, nj, 1 - u, 1)
                    pe.wait_ge(hd, e * FC + FC)
                    pe.wait_ge(wd_in[u], j * 16 + 16)
                    for k in range(NBK):
                        pe.wait_ge(y_a, e * NBK)
                        pe.wait_ge(y_d, e * NBK)
                        for h in range(2):
                            for f in range(FC):
                                ins = pe.matmul(ps[:, 4 + 2 * k + h, :], hh[u][:, f, k * P:(k + 1) * P],
                                                wd[u][:, f, h * BANK:(h + 1) * BANK], start=(f == 0), stop=(f == FC - 1))
                        ins.then_inc(down[u], 1)
                        if k == 0 and not last(j, u):
                            turn(e + 1, nj, 1 - u, 2)
                            turn(e + 1, nj, 1 - u, 3)

            run(pe, body)


def overflow_phase(nc, ps, t_rows, table, we_gate, we_up, we_down, base_rows, route):
    with Phase(nc, "ovf") as ph:
        sb, sem = ph.sb, ph.sem
        wg, wu, wd = sb("wg", [P, DC, FF]), sb("wu", [P, DC, FF]), sb("wd", [P, FC, D])
        ids, ix = sb("ids", [P, 2]), sb("ix", [P, 1], U32)
        xg, xT, base = sb("xg", [P, D]), sb("xT", [P, DC, P]), sb("base", [P, D])
        sl, hh, yo = sb("sl", [P, FC, P]), sb("hh", [P, FC, P]), sb("yo", [P, D])
        w_s, ids_in, ixd, x_in, base_in, y_out = (sem(n) for n in ("w", "ids_in", "ixd", "x_in", "base_in", "y_out"))
        turned, xT_c, gu, silud, hd, down, copied = (
            sem(n) for n in ("turned", "xT_c", "gu", "silud", "hd", "down", "copied"))
        spare = [sem(f"spare{i}") for i in range(3)]
        block = ph.block()

        def blocks(eng, body):
            n = eng.value_load(route.n_over[0:1, 0:1], min_val=0, max_val=MAXOV)
            with eng.Fori(0, MAXOV) as j:
                with eng.If(n > j):
                    body(j)
                eng.nop()

        @block.sync
        def _(sp):
            def body(j):
                e = sp.value_load(route.over[0:1, bass.ds(j * 2, 1)], min_val=0, max_val=NE - 1)
                s = sp.value_load(route.over[0:1, bass.ds(j * 2 + 1, 1)], min_val=0, max_val=NE * SLOTS - P)
                one = lambda w: w[bass.ds(e, 1)].rearrange("a (c p) f -> p (a c) f", p=P)
                sp.wait_ge(y_out, j * 16)
                sp.sem_inc(spare[0], 1)
                sp.dma_start(ids[:, :], table[bass.ds(s, P), :]).then_inc(ids_in, 16)
                sp.dma_start(wg[:, :, :], one(we_gate)).then_inc(w_s, 16)
                sp.dma_start(wu[:, :, :], one(we_up)).then_inc(w_s, 16)
                sp.dma_start(wd[:, :, :], one(we_down)).then_inc(w_s, 16)

            blocks(sp, body)

        @block.gpsimd
        def _(pool):
            def body(j):
                pool.wait_ge(ids_in, j * 16 + 16)
                pool.sem_inc(spare[1], 1)
                pool.tensor_copy(ix[:, :], ids[:, 0:1]).then_inc(ixd, 1)
                pool.wait_ge(ixd, j + 1)
                pool.sem_inc(spare[1], 1)
                pool.indirect_dma_start(out=xg[:, :], out_offset=None, in_=t_rows,
                                        in_offset=bass.IndirectOffsetOnAxis(ap=ix[:, :], axis=0)).then_inc(x_in, 16)
                pool.indirect_dma_start(out=base[:, :], out_offset=None, in_=base_rows,
                                        in_offset=bass.IndirectOffsetOnAxis(ap=ix[:, :], axis=0)).then_inc(base_in, 16)
                pool.wait_ge(copied, j + 1)
                pool.sem_inc(spare[1], 1)
                pool.indirect_dma_start(out=base_rows, out_offset=bass.IndirectOffsetOnAxis(ap=ix[:, :], axis=0),
                                        in_=yo[:, :], in_offset=None).then_inc(y_out, 16)
                pool.wait_ge(y_out, j * 16 + 16)
                pool.sem_inc(spare[1], 1)

            blocks(pool, body)

        @block.tensor
        def _(pe):
            def body(j):
                pe.wait_ge(x_in, j * 16 + 16)
                for c in range(DC):
                    ins = pe.transpose(ps[:, c // 4, (c % 4) * P:(c % 4 + 1) * P], xg[:, c * P:(c + 1) * P], route.ident)
                ins.then_inc(turned, 1)
                pe.wait_ge(xT_c, j + 1)
                pe.wait_ge(w_s, j * 48 + 48)
                for s, w in enumerate((wg, wu)):
                    for f in range(FC):
                        for c in range(DC):
                            ins = pe.matmul(ps[:, 2 + s, f * P:(f + 1) * P], w[:, c, f * P:(f + 1) * P], xT[:, c, :],
                                            start=(c == 0), stop=(c == DC - 1))
                ins.then_inc(gu, 1)
                pe.wait_ge(hd, j + 1)
                for h in range(2):
                    for f in range(FC):
                        ins = pe.matmul(ps[:, 4 + h, :], hh[:, f, :], wd[:, f, h * BANK:(h + 1) * BANK],
                                        start=(f == 0), stop=(f == FC - 1))
                ins.then_inc(down, 1)

            blocks(pe, body)

        @block.scalar
        def _(act):
            def body(j):
                act.wait_ge(gu, j + 1)
                nc.scalar.activation(flat(sl[:, :, :]), ps[:, 2, 0:FF], ACT.Silu).then_inc(silud, 1)

            blocks(act, body)

        @block.vector
        def _(dve):
            def body(j):
                dve.wait_ge(turned, j + 1)
                dve.tensor_copy(flat(xT[:, :, :]), wide(ps[:, 0:2, :])).then_inc(xT_c, 1)
                dve.wait_ge(silud, j + 1)
                dve.tensor_tensor(flat(hh[:, :, :]), flat(sl[:, :, :]), ps[:, 3, 0:FF], ALU.mult).then_inc(hd, 1)
                dve.wait_ge(down, j + 1)
                dve.wait_ge(base_in, j * 16 + 16)
                dve.sem_inc(spare[2], 1)
                dve.scalar_tensor_tensor(out=yo[:, :], in0=wide(ps[:, 4:6, :]), scalar=ids[:, 1:2], in1=base[:, :],
                                         op0=ALU.mult, op1=ALU.add).then_inc(copied, 1)

            blocks(dve, body)


def combine_phase(nc, ps, base_rows, y_rows, ln_g, ln_b, out, route):
    with Phase(nc, "com") as ph:
        sb, sem = ph.sb, ph.sem
        grow, brow = sb("grow", [P, D]), sb("brow", [P, D])
        base = [sb(f"base{b}", [P, D]) for b in range(2)]
        g = [[sb(f"g{b}{k}", [P, D]) for k in range(TOPK)] for b in range(2)]
        dg = [sb(f"dg{b}", [P, TOPK, P]) for b in range(2)]
        o = [sb(f"o{b}", [P, D]) for b in range(2)]
        ex, rk, gt = sb("ex", [P, TOPK]), sb("rk", [P, TOPK]), [sb(f"gt{b}", [P, TOPK]) for b in range(2)]
        kept = sb("kept", [P, TOPK])
        slot = [sb(f"slot{b}", [P, TOPK], U32) for b in range(2)]
        st, mv, ve, rstd, mhalf = (sb(n, s) for n, s in (("st", [P, 2, 6]), ("mv", [P, 2]), ("ve", [P, 1]),
                                                          ("rstd", [P, 1]), ("mhalf", [P, 1])))
        const, half = sem("const"), sem("half")
        base_in, g_in, out_s = ph.sems("base_in", 2), ph.sems("g_in", 2), ph.sems("out", 2)
        added = ph.sems("added", 2)
        chain, diag, summed, stats, aggr, epsd, rstds, centred, scaled, ready = (
            sem(n) for n in ("chain", "diag", "summed", "stats", "aggr", "epsd", "rstds", "centred",
                             "scaled", "ready"))
        spare = [sem(f"spare{i}") for i in range(2)]
        block = ph.block()
        N2 = NX // 2
        CH_N = 5

        @block.sync
        def _(sp):
            sp.dma_start(grow[:, :], ln_g.partition_broadcast(P)).then_inc(const, 16)
            sp.dma_start(brow[:, :], ln_b.partition_broadcast(P)).then_inc(const, 16)
            for b in range(2):
                sp.dma_start(base[b][:, :], base_rows[b * P:(b + 1) * P, :]).then_inc(base_in[b], 16)

            def body(j, more):
                for b in range(2):
                    i = j * 2 + b
                    if more:
                        sp.wait_ge(added[b], j + 1)
                        sp.dma_start(base[b][:, :], base_rows[bass.ds((i + 2) * P, P), :]).then_inc(base_in[b], 16)
                    sp.wait_ge(ready, i + 1)
                    sp.dma_start(out[bass.ds(i * P, P), :], o[b][:, :]).then_inc(out_s[b], 16)

            with sp.Fori(0, N2 - 1) as j:
                body(j, True)
            body(N2 - 1, False)
            for b in range(2):
                sp.wait_ge(out_s[b], 16 * N2)

        @block.gpsimd
        def _(pool):
            pool.memset(mhalf[:, :], -0.5).then_inc(half, 1)
            pool.wait_ge(half, 1)
            pool.wait_ge(const, 32)

            def gather(i, j, b):
                pool.wait_ge(chain, i * CH_N + CH_N)
                pool.wait_ge(added[b], j)
                pool.sem_inc(spare[0], 1)
                for k in range(TOPK):
                    pool.indirect_dma_start(out=g[b][k][:, :], out_offset=None, in_=y_rows,
                                            in_offset=bass.IndirectOffsetOnAxis(ap=slot[b][:, k:k + 1], axis=0)
                                            ).then_inc(g_in[b], 16)

            def norm(i, b):
                pool.wait_ge(aggr, i + 1)
                pool.sem_inc(spare[0], 1)
                pool.tensor_scalar(ve[:, :], mv[:, 1:2], EPS, None, ALU.add).then_inc(epsd, 1)
                pool.wait_ge(epsd, i + 1)
                pool.tensor_tensor(rstd[:, :], ve[:, :], mhalf[:, :], ALU.pow).then_inc(rstds, 1)
                pool.wait_ge(scaled, i + 1)
                pool.tensor_tensor(o[b][:, :], o[b][:, :], brow[:, :], ALU.add).then_inc(ready, 1)

            gather(0, 0, 0)
            gather(1, 0, 1)

            def body(j, more):
                for b in range(2):
                    i = j * 2 + b
                    norm(i, b)
                    if more:
                        gather(i + 2, j + 1, b)

            with pool.Fori(0, N2 - 1) as j:
                body(j, True)
            body(N2 - 1, False)

        @block.vector
        def _(dve):
            dve.wait_ge(const, 32)

            def slots(i, j, b):
                n = [0]

                def link(ins):
                    n[0] += 1
                    ins.then_inc(chain, 1)
                    dve.wait_ge(chain, i * CH_N + n[0])

                at = slice(i, i + 1) if isinstance(i, int) else bass.ds(i, 1)
                row = lambda x: x[:, at, :].rearrange("p a k -> p (a k)")
                dve.wait_ge(g_in[b], j * (16 * TOPK))
                dve.wait_ge(added[b], j)
                dve.sem_inc(spare[1], 1)
                dve.tensor_copy(rk[:, :], row(route.rank))
                dve.tensor_copy(gt[b][:, :], row(route.gate))
                link(dve.tensor_copy(ex[:, :], row(route.expert)))
                link(dve.tensor_scalar(kept[:, :], rk[:, :], float(CAP), None, ALU.is_lt))
                link(dve.tensor_scalar(rk[:, :], rk[:, :], float(CAP - 1), None, ALU.min))
                link(dve.tensor_tensor(gt[b][:, :], gt[b][:, :], kept[:, :], ALU.mult))
                link(dve.scalar_tensor_tensor(out=slot[b][:, :], in0=ex[:, :], scalar=float(CAP), in1=rk[:, :],
                                              op0=ALU.mult, op1=ALU.add))
                assert n[0] == CH_N
                for k in range(TOPK):
                    ins = dve.tensor_scalar(dg[b][:, k, :], route.ident, gt[b][:, k:k + 1], None, ALU.mult)
                ins.then_inc(diag, 1)

            def finish(i, j, b):
                dve.wait_ge(out_s[b], j * 16)
                dve.wait_ge(base_in[b], j * 16 + 16)
                dve.wait_ge(summed, i + 1)
                dve.sem_inc(spare[1], 1)
                dve.tensor_tensor(o[b][:, :], base[b][:, :], wide(ps[:, 2 * b:2 * b + 2, :]), ALU.add).then_inc(added[b], 1)
                dve.wait_ge(added[b], j + 1)
                for a in range(2):
                    dve.bn_stats(st[:, a, :], o[b][:, a * BANK:(a + 1) * BANK]).then_inc(stats, 1)
                dve.wait_ge(stats, i * 2 + 2)
                dve.sem_inc(spare[1], 1)
                dve.bn_aggr(mv[:, :], st[:, :, :]).then_inc(aggr, 1)

            def finish2(i, b):
                dve.wait_ge(rstds, i + 1)
                dve.wait_ge(aggr, i + 1)
                dve.sem_inc(spare[1], 1)
                dve.tensor_scalar(o[b][:, :], o[b][:, :], mv[:, 0:1], rstd[:, 0:1], ALU.subtract, ALU.mult).then_inc(centred, 1)
                dve.wait_ge(centred, i + 1)
                dve.tensor_tensor(o[b][:, :], o[b][:, :], grow[:, :], ALU.mult).then_inc(scaled, 1)

            slots(0, 0, 0)
            slots(1, 0, 1)

            def body(j, more):
                for b in range(2):
                    i = j * 2 + b
                    finish(i, j, b)
                    if more:
                        slots(i + 2, j + 1, b)
                    finish2(i, b)

            with dve.Fori(0, N2 - 1) as j:
                body(j, True)
            body(N2 - 1, False)

        @block.tensor
        def _(pe):
            with pe.Fori(0, N2) as j:
                for b in range(2):
                    i = j * 2 + b
                    pe.wait_ge(diag, i + 1)
                    pe.wait_ge(g_in[b], j * (16 * TOPK) + 16 * TOPK)
                    pe.wait_ge(added[b], j)
                    for h in range(2):
                        for k in range(TOPK):
                            ins = pe.matmul(ps[:, 2 * b + h, :], dg[b][:, k, :], g[b][k][:, h * BANK:(h + 1) * BANK],
                                            start=(k == 0), stop=(k == TOPK - 1))
                    ins.then_inc(summed, 1)


def build(nc, a, out):
    Phase.used = []
    dram = lambda name, shape, dt=F32: nc.dram_tensor(name, shape, dt).ap()
    h_rows, v_rows = dram("h_rows", (SEQ, D)), dram("v_rows", (TOK, FH * FD))
    cq, ck = dram("cq", (FH, 2, TOK)), dram("ck", (FH, 2, TOK))
    mixed, t_rows, base_rows = dram("mixed", (SEQ, MIX)), dram("t_rows", (SEQ + 1, D)), dram("base_rows", (SEQ + 1, D))
    table, over_rows = dram("table", (NE * SLOTS, 2)), dram("over_rows", (P, 2), I32)
    y_rows = dram("y_rows", (NE * CAP, D))
    with ExitStack() as ctx:
        ps = ctx.enter_context(nc.psum_tensor("ps", [P, 8, BANK], F32))
        with ExitStack() as first:
            ident = first.enter_context(nc.sbuf_tensor("ident", [P, P], F32))
            hT = first.enter_context(nc.sbuf_tensor("hT", [P, DC, TOK], F32))
            embed_phase(nc, ps, ident, hT, a["square"], a["x"], a["meta"], a["ln0_g"], a["ln0_b"], a["ln0_gcol"],
                        a["ln0_bcol"], a["w_in"], a["b_forget"], h_rows, v_rows, cq, ck)
            retention_phase(nc, ps, ident, hT, a["w_in"], a["rope"], a["retc"], mixed)
            fox_phase(nc, ps, ident, hT, a["square"], a["w_in"], v_rows, cq, ck, mixed)
        Phase.reset(nc)
        route = Route(nc, ctx)
        with nc.Block() as block:
            @block.sync
            def _(sp):
                sp.dma_start(route.sq[:, :], a["square"]).then_inc(route.tables, 16)
                sp.wait_ge(route.tables, 16)

            @block.gpsimd
            def _(pool):
                pool.memset(route.ones[:, :], 1.0).then_inc(route.ones_set, 1)
                pool.wait_ge(route.ones_set, 1)
        middle_phase(nc, ps, a["square"], mixed, h_rows, a["w_out"], a["ln1_g"], a["ln1_b"], a["w_router"],
                     a["router_bias"], a["ws_gate"], a["ws_up"], a["ws_down"], t_rows, base_rows, table, route)
        table_phase(nc, ps, table, over_rows, route)
        expert_phase(nc, ps, t_rows, a["we_gate"], a["we_up"], a["we_down"], y_rows, route)
        overflow_phase(nc, ps, t_rows, table, a["we_gate"], a["we_up"], a["we_down"], base_rows, route)
        combine_phase(nc, ps, base_rows, y_rows, a["ln2_g"], a["ln2_b"], out, route)


def kernel(**inputs):
    import concourse.bacc as bacc
    from concourse.bass_utils import run_bass_kernel_spmd

    nc = bacc.Bacc("TRN2", target_bir_lowering=False, num_devices=1)
    one = {"w_in", "b_forget", "w_out", "ln1_g", "ln1_b", "w_router", "router_bias", "we_gate", "we_up", "we_down",
           "ws_gate", "ws_up", "ws_down", "ln2_g", "ln2_b", "x"}
    data = {n: np.asarray(v)[0] if n in one else np.asarray(v) for n, v in inputs.items()}
    for n in ("g", "b"):
        data[f"ln0_{n}col"] = data[f"ln0_{n}"].reshape(DC, P).T
    data.update(constants())
    arrays, aps = {}, {}
    for n, v in data.items():
        v = np.ascontiguousarray(v)
        arrays[f"in_{n}"] = v
        aps[n] = nc.dram_tensor(f"in_{n}", v.shape, mybir.dt.from_np(v.dtype), kind="ExternalInput").ap()
    out = nc.dram_tensor("out", (SEQ, D), F32, kind="ExternalOutput").ap()
    build(nc, aps, out)
    got = run_bass_kernel_spmd(nc, [arrays], core_ids=[0])
    return got.results[0]["out"].reshape(1, SEQ, D)
```

```python
import math
from contextlib import ExitStack

import concourse.bass as bass
import numpy as np
from concourse import mybir

F32 = mybir.dt.float32
U32 = mybir.dt.uint32
I32 = mybir.dt.int32
ALU = mybir.AluOpType
ACT = mybir.ActivationFunctionType
AX = mybir.AxisListType

P = 128
D = 1024
DC = D // P
SEQ = 2048
NX = SEQ // P
META = 16
TOK = META + SEQ
NB = -(-TOK // P)
RH, RD = 4, 128
FH, FD = 8, 64
MIX = RH * RD + FH * FD
IN_COLS = 4 * RH * RD + 3 * FH * FD + FH
FQ0 = 4 * RH * RD
FK0 = FQ0 + FH * FD
FV0 = FK0 + FH * FD
FF0 = FV0 + FH * FD
PAIRS = FH // 2
NE, TOPK, NG, TOPG = 64, 6, 8, 4
GE = NE // NG
FF = 256
FC = FF // P
CAP = 256
SLOTS = SEQ
MAXOV = max(b for b in range(1, 200)
            if any(P * b + (CAP - P + 1) * n <= SEQ * TOPK and b <= n * ((SEQ - CAP) // P)
                   for n in range(1, NE + 1)))
EPS = 1e-5
NEG = -1e30
ALPHA = 2.0 ** 0.25
ROUTED = 2.5
BANK = 512
RC = P + 4
START = 1


def constants():
    f = np.float32
    half = RD // 2
    inv = (f(10000.0) ** (-np.arange(half, dtype=f) / f(half))).astype(f)
    ang = (np.arange(TOK, dtype=f)[:, None] * inv[None, :]).astype(f)
    rope = np.concatenate([np.cos(ang), np.sin(ang)], 1).astype(f)
    lg = np.log1p(-np.exp2(-5.0 - np.arange(RH, dtype=np.float64)))
    i = np.arange(P, dtype=np.float64)
    scale = RD ** -0.5
    ret = np.zeros((RH, P, RC), f)
    for h in range(RH):
        causal = i[None, :] >= i[:, None]
        ret[h, :, :P] = np.where(causal, np.exp(-(i[:, None] + 1) * lg[h]) * scale, 0)
        ret[h, :, P] = np.exp((P - 1 - i) * lg[h]) * scale
        ret[h, :, P + 1] = np.exp((i + 1) * lg[h])
        ret[h, :, P + 2] = np.exp(P * lg[h])
        ret[h, :META, P + 3] = np.exp((META - 1 - i[:META]) * lg[h]) * scale
    ident = np.eye(P, dtype=f)
    causal = np.where(i[None, :] <= i[:, None], 0, NEG).astype(f)
    before = (i[:, None] < i[None, :]).astype(f)
    thr = np.broadcast_to(P * np.arange(CAP // P, SLOTS // P, dtype=f), (P, SLOTS // P - CAP // P))
    iota = np.broadcast_to(np.arange(NE, dtype=f), (P, NE))
    slot0 = np.broadcast_to(np.arange(NE, dtype=f) * SLOTS, (P, NE))
    pcol = i.astype(f)[:, None]
    square = np.concatenate([ident, causal, before, iota, slot0, thr, pcol], 1)
    return {"rope": rope, "retc": ret, "square": np.ascontiguousarray(square)}


SQ_IDENT, SQ_CAUSAL, SQ_BEFORE = 0, P, 2 * P
SQ_IOTA = 3 * P
SQ_SLOT0 = SQ_IOTA + NE
SQ_THR = SQ_SLOT0 + NE
NTHR = SLOTS // P - CAP // P
SQ_PCOL = SQ_THR + NTHR
SQ_COLS = SQ_PCOL + 1


class Phase:

    used = []

    def __init__(self, nc, name):
        self.nc, self.name, self.ctx, self.mine = nc, name, ExitStack(), []

    def __enter__(self):
        self.ctx.__enter__()
        return self

    def __exit__(self, *a):
        return self.ctx.__exit__(*a)

    def sb(self, name, shape, dt=F32):
        return self.ctx.enter_context(self.nc.sbuf_tensor(f"{self.name}_{name}", shape, dt))

    def sem(self, name):
        new = self.nc.alloc_semaphore(name=f"{self.name}_{name}")
        self.used.append(new)
        self.mine.append(new)
        return new

    @classmethod
    def reset(cls, nc):
        nc.clear_and_free_semaphores(cls.used)
        cls.used = []
        nc.all_engine_barrier()

    def sems(self, name, n):
        return [self.sem(f"{name}{i}") for i in range(n)]

    def zero_sems(self, name, n):
        new = self.sems(name, n)
        self.mine = [s for s in self.mine if s not in new]
        return new

    def block(self):
        for s in self.mine:
            self.nc.gpsimd.sem_inc(s, START)
        self.nc.all_engine_barrier()
        return self.ctx.enter_context(self.nc.Block())


def flat(ap):
    return ap.rearrange("p a b -> p (a b)")


def embed_phase(nc, ps, ident, hT, square, x, meta, ln_g, ln_b, ln_gcol, ln_bcol, w_in, b_forget, h_rows, v_rows, cq, ck):
    with Phase(nc, "emb") as ph:
        sb, sem = ph.sb, ph.sem
        gcol, bcol = sb("gcol", [P, DC]), sb("bcol", [P, DC])
        grow, brow = sb("grow", [P, D]), sb("brow", [P, D])
        wv = sb("wv", [P, DC, FH * FD])
        wf = sb("wf", [P, DC, FH])
        bf = sb("bf", [FH, 1])
        xin = [sb(f"xin{i}", [P, D]) for i in range(3)]
        xn = [sb(f"xn{i}", [P, D]) for i in range(2)]
        hr = [sb(f"hr{i}", [P, D]) for i in range(2)]
        vst = [sb(f"vst{i}", [P, FH * FD]) for i in range(2)]
        st = [sb(f"st{i}", [P, 2, 6]) for i in range(2)]
        mv = [sb(f"mv{i}", [P, 2]) for i in range(2)]
        ve = [sb(f"ve{i}", [P, 1]) for i in range(2)]
        rstd = [sb(f"rstd{i}", [P, 1]) for i in range(2)]
        mhalf = sb("mhalf", [P, 1])
        z, t1, t2 = sb("z", [FH, TOK]), sb("t1", [FH, TOK]), sb("t2", [FH, TOK])
        ones = sb("ones", [FH, TOK])
        const, wv_in, wf_in = sem("const"), sem("wv_in"), sem("wf_in")
        x_in, h_out, v_out = ph.sems("x_in", 3), ph.sems("h_out", 2), ph.sems("v_out", 2)
        half, stats, aggr, epsd, rstds, normed = (sem(n) for n in
                                                  ("half", "stats", "aggr", "epsd", "rstds", "normed"))
        scaled, hrow, turned, hT_a, hT_d = (sem(n) for n in ("scaled", "hrow", "turned", "hT_a", "hT_d"))
        v_done, v_copied, f_done, f_copied, ones_set = (sem(n) for n in
                                                        ("v_done", "v_copied", "f_done", "f_copied", "ones_set"))
        gate, gate_e, gate_a, c_out = (sem(n) for n in ("gate", "gate_e", "gate_a", "c_out"))
        NT = NX + 1
        rows = [META] + [P] * NX
        tok0 = [0] + [META + P * i for i in range(NX)]
        vrows = [min(P, TOK - P * b) for b in range(NB)]
        FCH = [(o, min(BANK, TOK - o)) for o in range(0, TOK, BANK)]
        f_tile = [-(-(o + n - META) // P) for o, n in FCH]
        block = ph.block()

        @block.sync
        def _(sp):
            def load(i):
                if i >= 3:
                    sp.wait_ge(normed, i - 2 + START)
                src = meta if i == 0 else x[P * (i - 1):P * i, :]
                sp.dma_start(xin[i % 3][0:rows[i], :], src).then_inc(x_in[i % 3], 16)

            load(0)
            load(1)
            sp.dma_start(ident[:, :], square[:, SQ_IDENT:SQ_IDENT + P]).then_inc(const, 16)
            sp.dma_start(gcol[:, :], ln_gcol).then_inc(const, 16)
            sp.dma_start(bcol[:, :], ln_bcol).then_inc(const, 16)
            sp.dma_start(grow[:, :], ln_g.partition_broadcast(P)).then_inc(const, 16)
            sp.dma_start(brow[:, :], ln_b.partition_broadcast(P)).then_inc(const, 16)
            sp.dma_start(bf[:, :], b_forget.rearrange("(h o) -> h o", o=1)).then_inc(const, 16)
            load(2)
            w = w_in.rearrange("(c p) n -> p c n", p=P)
            sp.dma_start(wv[:, :, :], w[:, :, FV0:FV0 + FH * FD]).then_inc(wv_in, 16)
            sp.dma_start(wf[:, :, :], w[:, :, FF0:FF0 + FH]).then_inc(wf_in, 16)
            for i in range(NT):
                if i + 3 < NT:
                    load(i + 3)
                if i >= 1:
                    sp.wait_ge(hrow, i + START)
                    sp.dma_start(h_rows[P * (i - 1):P * i, :], hr[(i - 1) % 2][:, :]).then_inc(h_out[(i - 1) % 2], 16)
                for b in ([i - 1] if 1 <= i < NT - 1 else [NT - 2, NT - 1] if i == NT - 1 else []):
                    sp.wait_ge(v_copied, b + 1 + START)
                    sp.dma_start(v_rows[P * b:P * b + vrows[b], :], vst[b % 2][0:vrows[b], :]).then_inc(v_out[b % 2], 16)
            sp.wait_ge(gate, 5 + START)
            sp.dma_start(cq[:, 0, :], t1[:, :]).then_inc(c_out, 16)
            sp.dma_start(cq[:, 1, :], ones[:, :]).then_inc(c_out, 16)
            sp.dma_start(ck[:, 0, :], ones[:, :]).then_inc(c_out, 16)
            sp.dma_start(ck[:, 1, :], t2[:, :]).then_inc(c_out, 16)
            sp.wait_ge(c_out, 64 + START)
            for i in range(2):
                sp.wait_ge(h_out[i], 16 * (NX // 2) + START)
                sp.wait_ge(v_out[i], 16 * len(range(i, NB, 2)) + START)

        @block.gpsimd
        def _(pool):
            pool.memset(mhalf[:, :], -0.5).then_inc(half, 1)
            pool.memset(ones[:, :], 1.0).then_inc(ones_set, 1)
            pool.wait_ge(half, 1 + START)
            pool.wait_ge(const, 96 + START)
            for i in range(NT):
                r = rows[i]
                pool.wait_ge(aggr, i + 1 + START)
                pool.tensor_scalar(ve[i % 2][0:r, :], mv[i % 2][0:r, 1:2], EPS, None, ALU.add).then_inc(epsd, 1)
                pool.wait_ge(epsd, i + 1 + START)
                pool.tensor_tensor(rstd[i % 2][0:r, :], ve[i % 2][0:r, :], mhalf[0:r, :], ALU.pow).then_inc(rstds, 1)
                if i >= 1:
                    pool.wait_ge(scaled, i + START)
                    k = (i - 1) % 2
                    pool.tensor_tensor(hr[k][:, :], hr[k][:, :], brow[:, :], ALU.add).then_inc(hrow, 1)

        @block.vector
        def _(dve):
            def moments(i):
                r = rows[i]
                dve.wait_ge(x_in[i % 3], 16 * (i // 3 + 1) + START)
                for a in range(2):
                    dve.bn_stats(st[i % 2][0:r, a, :], xin[i % 3][0:r, a * BANK:(a + 1) * BANK]).then_inc(stats, 1)
                dve.wait_ge(stats, 2 * i + 2 + START)
                if i >= 2:
                    dve.wait_ge(normed, i - 1 + START)
                dve.bn_aggr(mv[i % 2][0:r, :], st[i % 2][0:r, :, :]).then_inc(aggr, 1)

            def normalise(i):
                r = rows[i]
                dve.wait_ge(rstds, i + 1 + START)
                if i >= 2:
                    dve.wait_ge(turned, i - 1 + START)
                dve.tensor_scalar(xn[i % 2][0:r, :], xin[i % 3][0:r, :], mv[i % 2][0:r, 0:1],
                                  rstd[i % 2][0:r, 0:1], ALU.subtract, ALU.mult).then_inc(normed, 1)

            def rest(i):
                r = rows[i]
                if i >= 1:
                    k = (i - 1) % 2
                    if i >= 3:
                        dve.wait_ge(h_out[k], 16 * ((i - 1) // 2) + START)
                    dve.wait_ge(normed, i + 1 + START)
                    dve.tensor_tensor(hr[k][:, :], xn[i % 2][:, :], grow[:, :], ALU.mult).then_inc(scaled, 1)
                dve.wait_ge(turned, i + 1 + START)
                for c in range(4, DC):
                    ins = dve.tensor_scalar(hT[:, c, tok0[i]:tok0[i] + r],
                                            ps[:, 2 * (i % 2) + 1, (c - 4) * P:(c - 4) * P + r],
                                            gcol[:, c:c + 1], bcol[:, c:c + 1], ALU.mult, ALU.add)
                ins.then_inc(hT_d, 1)

            moments(0)
            dve.wait_ge(const, 96 + START)
            for i in range(NT):
                normalise(i)
                if i + 1 < NT:
                    moments(i + 1)
                rest(i)
            dve.wait_ge(f_copied, len(FCH) + START)
            dve.scalar_tensor_tensor(out=t1[:, :], in0=z[:, :], scalar=-1.0, in1=z[:, :],
                                     op0=ALU.mult, op1=ALU.min).then_inc(gate, 1)
            dve.wait_ge(gate_a, 1 + START)
            dve.scalar_tensor_tensor(out=t2[:, :], in0=z[:, :], scalar=0.0, in1=t1[:, :],
                                     op0=ALU.min, op1=ALU.subtract).then_inc(gate, 1)
            dve.wait_ge(gate, 2 + START)
            dve.wait_ge(ones_set, 1 + START)
            dve.tensor_tensor_scan(t1[:, :], ones[:, :], t2[:, :], 0.0, ALU.mult, ALU.add).then_inc(gate, 1)
            dve.wait_ge(gate, 3 + START)
            dve.tensor_scalar(t2[:, :], t1[:, :], -1.0, None, ALU.mult).then_inc(gate, 2)

        @block.scalar
        def _(act):
            act.wait_ge(const, 96 + START)

            def copy_v(b):
                act.wait_ge(v_done, b + 1 + START)
                if b >= 2:
                    act.wait_ge(v_out[b % 2], 16 * (b // 2) + START)
                nc.scalar.copy(vst[b % 2][0:vrows[b], :], ps[0:vrows[b], 4 + b % 2, :]).then_inc(v_copied, 1)

            for i in range(NT):
                r = rows[i]
                act.wait_ge(turned, i + 1 + START)
                for c in range(4):
                    ins = nc.scalar.activation(hT[:, c, tok0[i]:tok0[i] + r],
                                               ps[:, 2 * (i % 2), c * P:c * P + r], ACT.Identity,
                                               bias=bcol[:, c:c + 1], scale=gcol[:, c:c + 1])
                ins.then_inc(hT_a, 1)
                if i >= 2:
                    copy_v(i - 2)
                for k in (k for k, t in enumerate(f_tile) if t == i):
                    o, n = FCH[k]
                    act.wait_ge(f_done, k + 1 + START)
                    nc.scalar.activation(z[:, o:o + n], ps[0:FH, 6 + k % 2, 0:n], ACT.Identity,
                                         bias=bf[:, 0:1]).then_inc(f_copied, 1)
                if i == NT - 1:
                    copy_v(NT - 2)
                    copy_v(NT - 1)
            act.wait_ge(gate, 1 + START)
            nc.scalar.activation(t2[:, :], t1[:, :], ACT.Exp).then_inc(gate_e, 1)
            act.wait_ge(gate_e, 1 + START)
            nc.scalar.activation(t1[:, :], t2[:, :], ACT.Ln, bias=1.0).then_inc(gate_a, 1)

        @block.tensor
        def _(pe):
            def turn(i):
                r = rows[i]
                pe.wait_ge(normed, i + 1 + START)
                if i >= 2:
                    pe.wait_ge(hT_a, i - 1 + START)
                    pe.wait_ge(hT_d, i - 1 + START)
                for c in range(DC):
                    ins = pe.transpose(ps[:, 2 * (i % 2) + c // 4, (c % 4) * P:(c % 4) * P + r],
                                       xn[i % 2][0:r, c * P:(c + 1) * P], ident[0:r, 0:r])
                ins.then_inc(turned, 1)

            def values(b):
                pe.wait_ge(hT_a, min(b + 2, NT) + START)
                pe.wait_ge(hT_d, min(b + 2, NT) + START)
                if b >= 2:
                    pe.wait_ge(v_copied, b - 1 + START)
                for c in range(DC):
                    ins = pe.matmul(ps[0:vrows[b], 4 + b % 2, :], hT[:, c, P * b:P * b + vrows[b]], wv[:, c, :],
                                    start=(c == 0), stop=(c == DC - 1))
                ins.then_inc(v_done, 1)

            def forget(k):
                o, n = FCH[k]
                if k >= 2:
                    pe.wait_ge(f_copied, k - 1 + START)
                for c in range(DC):
                    ins = pe.matmul(ps[0:FH, 6 + k % 2, 0:n], wf[:, c, :], hT[:, c, o:o + n],
                                    start=(c == 0), stop=(c == DC - 1))
                ins.then_inc(f_done, 1)

            pe.wait_ge(const, 96 + START)
            for i in range(NT):
                turn(i)
                if i == 2:
                    pe.wait_ge(wv_in, 16 + START)
                    pe.wait_ge(wf_in, 16 + START)
                if i >= 2:
                    values(i - 2)
                for k in (k for k, t in enumerate(f_tile) if t == i):
                    pe.wait_ge(hT_a, i + 1 + START)
                    pe.wait_ge(hT_d, i + 1 + START)
                    forget(k)
            values(NT - 2)
            values(NT - 1)


def retention_phase(nc, ps, ident, hT, w_in, rope, retc, mixed):
    with Phase(nc, "ret") as ph:
        sb, sem = ph.sb, ph.sem
        NM = NX + 1
        SLICES = 4
        cs, csm = sb("cs", [P, NX, RD]), sb("csm", [META, RD])
        wr = [sb(f"w{u}", [P, DC, 4 * RD]) for u in range(2)]
        rc = [sb(f"rc{u}", [P, RC]) for u in range(2)]
        qk = [sb(f"qk{b}", [P, 2 * RD]) for b in range(2)]
        v = [sb(f"v{b}", [P, RD]) for b in range(2)]
        vz = [sb(f"vz{b}", [P, RD]) for b in range(2)]
        cosd, sind = sb("cosd", [P, 2 * RD]), sb("sind", [P, 2 * RD])
        r = [sb(f"r{b}", [P, 2 * RD]) for b in range(2)]
        rT = [sb(f"rT{b}", [P, 2 * RD]) for b in range(2)]
        sT = [sb(f"sT{b}", [P, P]) for b in range(2)]
        S = [sb(f"S{b}", [RD, RD]) for b in range(2)]
        ret = [sb(f"ret{u}", [P, NX, RD]) for u in range(2)]
        sg = [sb(f"sg{u}", [P, NX, RD]) for u in range(2)]
        bn = [sb(f"bn{u}", [P, NX, 6]) for u in range(2)]
        mv = [sb(f"mv{u}", [P, NX, 2]) for u in range(2)]
        ve = [sb(f"ve{u}", [P, NX]) for u in range(2)]
        rstd = [sb(f"rstd{u}", [P, NX]) for u in range(2)]
        mhalf = sb("mhalf", [P, NX])
        tab, half = sem("tab"), sem("half")
        w_in_s = ph.sems("w_in", 2)
        proj, evac, products, rotated = (sem(n) for n in ("proj", "evac", "products", "rotated"))
        turned, turned_c, scored, masked, state_mm, state, att, out_c = (
            sem(n) for n in ("turned", "turned_c", "scored", "masked", "state_mm", "state", "att", "out_c"))
        moments, aggr, epsd, rstds, centred, gated = (
            sem(n) for n in ("moments", "aggr", "epsd", "rstds", "centred", "gated"))
        mix_out = ph.sems("mix_out", 2)
        spare = [sem(f"spare{i}") for i in range(3)]
        block = ph.block()
        w = w_in.rearrange("(c p) n -> p c n", p=P)

        @block.sync
        def _(sp):
            def load(h):
                u = h % 2
                if h >= 2:
                    sp.wait_ge(att, NX * (h - 1) + START)
                    sp.wait_ge(state, NX * (h - 1) + START)
                    sp.wait_ge(proj, NM * (h - 1) + START)
                for s in range(SLICES):
                    sp.dma_start(wr[u][:, :, s * RD:(s + 1) * RD],
                                 w[:, :, (s * RH + h) * RD:(s * RH + h + 1) * RD]).then_inc(w_in_s[u], 16)
                sp.dma_start(rc[u][:, :], retc[h]).then_inc(w_in_s[u], 16)

            load(0)
            sp.dma_start(cs[:, :, :], rope[META:TOK, :].rearrange("(n p) d -> p n d", p=P)).then_inc(tab, 16)
            sp.dma_start(csm[:, :], rope[0:META, :]).then_inc(tab, 16)
            load(1)
            for h in range(RH):
                if h + 2 < RH:
                    load(h + 2)
                sp.wait_ge(gated, h + 1 + START)
                sp.dma_start(mixed[:, h * RD:(h + 1) * RD].rearrange("(n p) d -> p n d", p=P),
                             ret[h % 2][:, :, :]).then_inc(mix_out[h % 2], 16)
            for u in range(2):
                sp.wait_ge(mix_out[u], 16 * (RH // 2) + START)

        @block.gpsimd
        def _(pool):
            pool.memset(mhalf[:, :], -0.5).then_inc(half, 1)
            pool.wait_ge(half, 1 + START)
            for h in range(RH):
                u = h % 2
                pool.wait_ge(aggr, NX * (h + 1) + START)
                pool.tensor_scalar(ve[u][:, :], mv[u][:, :, 1], EPS, None, ALU.add).then_inc(epsd, 1)
                pool.wait_ge(epsd, h + 1 + START)
                pool.tensor_tensor(rstd[u][:, :], ve[u][:, :], mhalf[:, :], ALU.pow).then_inc(rstds, 1)

        @block.scalar
        def _(act):
            act.wait_ge(w_in_s[0], 80 + START)
            with act.Fori(0, RH // 2) as j:
                for u in range(2):
                    def evacuate(m):
                        b, n = (u + m) % 2, META if m == 0 else P
                        bank = ps[0:n, b, :]
                        act.wait_ge(proj, (j * 2 + u) * NM + m + 1 + START)
                        if m == 2:
                            act.wait_ge(state_mm, (j * 2 + u) * NX + 1 + START)
                        if m >= 3:
                            act.wait_ge(att, (j * 2 + u) * NX + m - 2 + START)
                        if m == 0:
                            act.wait_ge(w_in_s[u], j * 80 + 80 + START)
                            act.wait_ge(att, (j * 2 + u) * NX + START)
                            act.sem_inc(spare[0], 1)
                        zeta = rc[u][0:n, P + 3:P + 4] if m == 0 else rc[u][:, P:P + 1]
                        if m > 0:
                            nc.scalar.activation(qk[b][:, 0:RD], bank[:, 0:RD], ACT.Copy, scale=rc[u][:, P + 1:P + 2])
                            nc.scalar.copy(v[b][:, :], bank[:, 2 * RD:3 * RD])
                        nc.scalar.copy(qk[b][0:n, RD:2 * RD], bank[:, RD:2 * RD])
                        ins = nc.scalar.activation(vz[b][0:n, :], bank[:, 2 * RD:3 * RD], ACT.Copy, scale=zeta)
                        if m > 0:
                            ins = nc.scalar.activation(sg[u][:, m - 1, :], bank[:, 3 * RD:4 * RD], ACT.Silu)
                        ins.then_inc(evac, 1)

                    act.wait_ge(mix_out[u], j * 16 + START)
                    act.sem_inc(spare[0], 1)
                    evacuate(0)
                    evacuate(1)
                    evacuate(2)
                    for n in range(NX):
                        m = n + 1
                        act.wait_ge(turned, (j * 2 + u) * NX + n + 1 + START)
                        nc.scalar.copy(rT[n % 2][:, :], ps[:, 2, 0:2 * RD]).then_inc(turned_c, 1)
                        act.wait_ge(att, (j * 2 + u) * NX + n + 1 + START)
                        nc.scalar.copy(ret[u][:, n, :], ps[:, 4 + n % 2, 0:RD]).then_inc(out_c, 1)
                        if m + 2 < NM:
                            evacuate(m + 2)

        @block.vector
        def _(dve):
            dve.wait_ge(tab, 32 + START)
            with dve.Fori(0, RH // 2) as j:
                for u in range(2):
                    def rotate(m):
                        b, n = (u + m) % 2, META if m == 0 else P
                        g0 = 1 if m == 0 else 0
                        t = csm[0:n, :] if m == 0 else cs[:, m - 1, :]
                        four = lambda x: x.rearrange("p (g h d) -> p g h d", g=2, h=2)[0:n, g0:, :, :]
                        src, c4, s4, dst = four(qk[b][:, :]), four(cosd[:, :]), four(sind[:, :]), four(r[b][:, :])
                        tb = lambda a: t[:, a * 64:(a + 1) * 64].unsqueeze(1).to_broadcast([n, 2 - g0, 64])
                        dve.wait_ge(evac, (j * 2 + u) * NM + m + 1 + START)
                        dve.wait_ge(rotated, ((j * 2 + u) * NM + m) * 2 + START)
                        for h in range(2):
                            dve.tensor_tensor(c4[:, :, h, :], src[:, :, h, :], tb(0), ALU.mult).then_inc(products, 1)
                            dve.tensor_tensor(s4[:, :, h, :], src[:, :, 1 - h, :], tb(1), ALU.mult).then_inc(products, 1)
                        dve.wait_ge(products, ((j * 2 + u) * NM + m + 1) * 4 + START)
                        dve.tensor_tensor(dst[:, :, 0, :], c4[:, :, 0, :], s4[:, :, 0, :], ALU.subtract).then_inc(rotated, 1)
                        dve.tensor_tensor(dst[:, :, 1, :], c4[:, :, 1, :], s4[:, :, 1, :], ALU.add).then_inc(rotated, 1)

                    def update(m):
                        dve.wait_ge(state_mm, (j * 2 + u) * NX + m + 1 + START)
                        if m == 0:
                            dve.tensor_copy(S[0][:, :], ps[:, 6, 0:RD]).then_inc(state, 1)
                        else:
                            dve.wait_ge(state, (j * 2 + u) * NX + m + START)
                            dve.sem_inc(spare[1], 1)
                            dve.scalar_tensor_tensor(out=S[m % 2][:, :], in0=S[(m - 1) % 2][:, :],
                                                     scalar=rc[u][:, P + 2:P + 3], in1=ps[:, 6, 0:RD],
                                                     op0=ALU.mult, op1=ALU.add).then_inc(state, 1)

                    rotate(0)
                    rotate(1)
                    update(0)
                    rotate(2)
                    for n in range(NX):
                        m = n + 1
                        dve.wait_ge(scored, (j * 2 + u) * NX + n + 1 + START)
                        dve.tensor_tensor(sT[n % 2][:, :], ps[:, 3, 0:P], rc[u][:, 0:P], ALU.mult).then_inc(masked, 1)
                        if m < NX:
                            update(m)
                        dve.wait_ge(out_c, (j * 2 + u) * NX + n + 1 + START)
                        dve.bn_stats(bn[u][:, n, :], ret[u][:, n, :]).then_inc(moments, 1)
                        dve.wait_ge(moments, (j * 2 + u) * NX + n + 1 + START)
                        dve.sem_inc(spare[1], 1)
                        dve.bn_aggr(mv[u][:, n, :], bn[u][:, n, :]).then_inc(aggr, 1)
                        if m + 2 < NM:
                            rotate(m + 2)
                    dve.wait_ge(rstds, j * 2 + u + 1 + START)
                    dve.sem_inc(spare[1], 1)
                    for n in range(NX):
                        ins = dve.tensor_scalar(ret[u][:, n, :], ret[u][:, n, :], mv[u][:, n, 0:1], rstd[u][:, n:n + 1],
                                                ALU.subtract, ALU.mult)
                    ins.then_inc(centred, 1)
                    dve.wait_ge(centred, j * 2 + u + 1 + START)
                    dve.sem_inc(spare[1], 1)
                    dve.tensor_tensor(flat(ret[u][:, :, :]), flat(ret[u][:, :, :]), flat(sg[u][:, :, :]),
                                      ALU.mult).then_inc(gated, 1)

        @block.tensor
        def _(pe):
            with pe.Fori(0, RH // 2) as j:
                for u in range(2):
                    def project(m):
                        n, t0 = (META, 0) if m == 0 else (P, META + P * (m - 1))
                        b = (u + m) % 2
                        lo, hi = (RD, 3 * RD) if m == 0 else (0, 4 * RD)
                        if m < 2:
                            if u == 1:
                                pe.wait_ge(evac, (j * 2 + u) * NM + m - 1 + START)
                            else:
                                pe.wait_ge(evac, j * (2 * NM) + START)
                        else:
                            pe.wait_ge(evac, (j * 2 + u) * NM + m - 1 + START)
                        for c in range(DC):
                            ins = pe.matmul(ps[0:n, b, lo:hi], hT[:, c, t0:t0 + n], wr[u][:, c, lo:hi],
                                            start=(c == 0), stop=(c == DC - 1))
                        ins.then_inc(proj, 1)

                    def outer(m):
                        b, n = (u + m) % 2, META if m == 0 else P
                        if m == 0:
                            pe.wait_ge(rotated, ((j * 2 + u) * NM + m + 1) * 2 + START)
                        pe.wait_ge(state, (j * 2 + u) * NX + m + START)
                        ins = pe.matmul(ps[:, 6, 0:RD], r[b][0:n, RD:2 * RD], vz[b][0:n, :], start=True, stop=True)
                        ins.then_inc(state_mm, 1)

                    pe.wait_ge(w_in_s[u], j * 80 + 80 + START)
                    project(0)
                    project(1)
                    outer(0)
                    project(2)
                    for n in range(NX):
                        m = n + 1
                        b = (u + m) % 2
                        pe.wait_ge(rotated, ((j * 2 + u) * NM + m + 1) * 2 + START)
                        pe.wait_ge(turned_c, (j * 2 + u) * NX + n + START)
                        for a in range(2):
                            ins = pe.transpose(ps[:, 2, a * RD:(a + 1) * RD], r[b][:, a * RD:(a + 1) * RD], ident[:, :])
                        ins.then_inc(turned, 1)
                        if m + 2 < NM:
                            project(m + 2)
                        pe.wait_ge(turned_c, (j * 2 + u) * NX + n + 1 + START)
                        pe.matmul(ps[:, 3, 0:P], rT[n % 2][:, RD:2 * RD], rT[n % 2][:, 0:RD],
                                  start=True, stop=True).then_inc(scored, 1)
                        if m < NX:
                            outer(m)
                        pe.wait_ge(state, (j * 2 + u) * NX + m + START)
                        if n >= 2:
                            pe.wait_ge(out_c, (j * 2 + u) * NX + n - 1 + START)
                        pe.matmul(ps[:, 4 + n % 2, 0:RD], rT[n % 2][:, 0:RD], S[(m - 1) % 2][:, :],
                                  start=True, stop=False)
                        pe.wait_ge(masked, (j * 2 + u) * NX + n + 1 + START)
                        pe.matmul(ps[:, 4 + n % 2, 0:RD], sT[n % 2][:, :], v[b][:, :],
                                  start=False, stop=True).then_inc(att, 1)


def fox_phase(nc, ps, ident, hT, square, w_in, v_rows, cq, ck, mixed):
    with Phase(nc, "fox") as ph:
        sb, sem = ph.sb, ph.sem
        AUG = FD + 2
        wqk = [sb(f"w{u}", [P, DC, 4 * FD]) for u in range(2)]
        vp = [sb(f"v{u}", [P, NB, 2 * FD]) for u in range(2)]
        qa, ka = sb("qa", [AUG, 2, SEQ]), sb("ka", [AUG, 2, TOK])
        fo = [sb(f"fo{u}", [P, NX, 2 * FD]) for u in range(2)]
        prob = [sb(f"prob{b}", [P, TOK]) for b in range(2)]
        pT = [sb(f"pT{b}", [P, BANK]) for b in range(4)]
        causal = sb("causal", [P, P])
        nm = [sb(f"nm{b}", [P, 3]) for b in range(2)]
        rs = [sb(f"rs{b}", [P, 2]) for b in range(2)]
        rsum = [sb(f"rsum{b}", [P, 1]) for b in range(2)]
        rinv = [sb(f"rinv{b}", [P, 1]) for b in range(2)]
        tab = sem("tab")
        w_s, v_s = ph.sems("w", 2), ph.sems("v", 2)
        c_s, fox_out = sem("c"), ph.sems("out", 2)
        proj, proj_a, proj_d = sem("proj"), sem("proj_a"), sem("proj_d")
        s_a, s_b, capped, maxed, negm = (sem(n) for n in ("s_a", "s_b", "capped", "maxed", "negm"))
        exp_a, exp_b, turned, pt_a, pt_d = (sem(n) for n in ("exp_a", "exp_b", "turned", "pt_a", "pt_d"))
        attended, summed, inverted, normed = (sem(n) for n in ("attended", "summed", "inverted", "normed"))
        spare = [sem(f"spare{i}") for i in range(3)]
        HALF = 2 * BANK
        U = 2 * NX
        keys = [META + P * (i % NX + 1) for i in range(U)]
        wide = [k > HALF for k in keys]
        blocks = [-(-k // P) for k in keys]
        groups = [-(-n // 4) for n in blocks]
        base = [0 if wide[i] else i % 2 * HALF for i in range(U)]
        before_b = [sum(wide[:i]) for i in range(U + 1)]
        before_g = [sum(groups[:i]) for i in range(U + 1)]
        ga = [min(2, g) for g in groups]
        before_a = [sum(ga[:i]) for i in range(U + 1)]
        before_d = [before_g[i] - before_a[i] for i in range(U + 1)]
        QCH = [(0, BANK * i, META + BANK * i, BANK) for i in range(SEQ // BANK)]
        KCH = [(1, o, o, min(BANK, TOK - o)) for o in range(0, TOK, BANK)]
        CH = QCH + KCH
        block = ph.block()
        w = w_in.rearrange("(c p) n -> p c n", p=P)
        flatps = ps[:, :, :].rearrange("p a b -> p (a b)")

        @block.sync
        def _(sp):
            def load(p):
                u = p % 2
                if p >= 2:
                    sp.wait_ge(normed, U * (p - 1) + START)
                sp.dma_start(wqk[u][:, :, 0:2 * FD], w[:, :, FQ0 + 2 * FD * p:FQ0 + 2 * FD * (p + 1)]).then_inc(w_s[u], 16)
                sp.dma_start(wqk[u][:, :, 2 * FD:4 * FD], w[:, :, FK0 + 2 * FD * p:FK0 + 2 * FD * (p + 1)]).then_inc(w_s[u], 16)
                full = (NB - 1) * P
                sp.dma_start(vp[u][:, 0:NB - 1, :],
                             v_rows[0:full, 2 * FD * p:2 * FD * (p + 1)].rearrange("(n p) d -> p n d", p=P)).then_inc(v_s[u], 16)
                sp.dma_start(vp[u][0:TOK - full, NB - 1, :],
                             v_rows[full:TOK, 2 * FD * p:2 * FD * (p + 1)]).then_inc(v_s[u], 16)

            sp.dma_start(causal[:, :], square[:, SQ_CAUSAL:SQ_CAUSAL + P]).then_inc(tab, 16)
            load(0)
            load(1)
            for p in range(PAIRS):
                if p >= 1:
                    sp.wait_ge(normed, U * p + START)
                for a in range(2):
                    sp.dma_start(qa[FD:AUG, a, :], cq[2 * p + a, :, META:TOK]).then_inc(c_s, 16)
                    sp.dma_start(ka[FD:AUG, a, :], ck[2 * p + a]).then_inc(c_s, 16)
                if 1 <= p and p + 1 < PAIRS:
                    load(p + 1)
                if p >= 1:
                    sp.dma_start(mixed[:, RH * RD + 2 * FD * (p - 1):RH * RD + 2 * FD * p].rearrange("(n p) d -> p n d", p=P),
                                 fo[(p - 1) % 2][:, :, :]).then_inc(fox_out[(p - 1) % 2], 16)
            p = PAIRS
            sp.wait_ge(normed, U * p + START)
            sp.dma_start(mixed[:, RH * RD + 2 * FD * (p - 1):RH * RD + 2 * FD * p].rearrange("(n p) d -> p n d", p=P),
                         fo[(p - 1) % 2][:, :, :]).then_inc(fox_out[(p - 1) % 2], 16)
            for u in range(2):
                sp.wait_ge(fox_out[u], 16 * (PAIRS // 2) + START)

        @block.scalar
        def _(act):
            with act.Fori(0, PAIRS // 2) as j:
                for pu in range(2):
                    p = j * 2 + pu

                    def proj_copy(t):
                        side, o, _, n = CH[t]
                        act.wait_ge(proj, p * len(CH) + t + 1 + START)
                        if t == 0:
                            act.wait_ge(attended, p * U + START)
                            act.sem_inc(spare[0], 1)
                        dst = (ka if side else qa)[0:FD, 0, o:o + n]
                        nc.scalar.activation(dst, ps[0:FD, t % 4, 0:n], ACT.Copy,
                                             scale=1.0 if side else FD ** -0.5).then_inc(proj_a, 1)

                    def exps(i):
                        b, k = i % 2, keys[i]
                        act.wait_ge(negm, p * U + i + 1 + START)
                        act.sem_inc(spare[0], 1)
                        if i >= 2:
                            act.wait_ge(normed, p * U + i - 1 + START)
                        bias = nm[b][:, 2:3] if wide[i] else nm[b][:, 0:1]
                        n = min(k, HALF)
                        nc.scalar.activation(prob[b][:, 0:n], flatps[:, base[i]:base[i] + n], ACT.Exp, bias=bias,
                                             accum_out=rs[b][:, 0:1]).then_inc(exp_a, 1)
                        if wide[i]:
                            nc.scalar.activation(prob[b][:, n:k], flatps[:, n:k], ACT.Exp, bias=bias,
                                                 accum_out=rs[b][:, 1:2]).then_inc(exp_b, 1)

                    def probs_back(i, g):
                        nb = blocks[i]
                        full = min(4, nb - 1 - 4 * g)
                        act.wait_ge(turned, p * before_g[U] + before_g[i] + g + 1 + START)
                        ins = None
                        if full > 0:
                            ins = nc.scalar.copy(pT[g % 4][:, 0:full * P], ps[:, 5 + g % 2, 0:full * P])
                        if full < 4:
                            ins = nc.scalar.copy(pT[g % 4][0:META, full * P:(full + 1) * P],
                                                 ps[0:META, 5 + g % 2, full * P:(full + 1) * P])
                        ins.then_inc(pt_a, 1)

                    for t in range(len(CH)):
                        proj_copy(t)
                    exps(0)
                    for i in range(U):
                        for g in range(ga[i]):
                            probs_back(i, g)
                        if i + 1 < U:
                            exps(i + 1)

        @block.vector
        def _(dve):
            dve.wait_ge(tab, 16 + START)
            with dve.Fori(0, PAIRS // 2) as j:
                for pu in range(2):
                    p = j * 2 + pu

                    def proj_copy(t):
                        side, o, _, n = CH[t]
                        dve.wait_ge(proj, p * len(CH) + t + 1 + START)
                        if t == 0:
                            dve.wait_ge(attended, p * U + START)
                            dve.sem_inc(spare[1], 1)
                        dst = (ka if side else qa)[0:FD, 1, o:o + n]
                        dve.tensor_scalar(dst, ps[FD:2 * FD, t % 4, 0:n], 1.0 if side else FD ** -0.5, None,
                                          ALU.mult).then_inc(proj_d, 1)

                    def maxima(i):
                        b, k = i % 2, keys[i]
                        dve.wait_ge(s_a, p * U + i + 1 + START)
                        dve.sem_inc(spare[1], 1)
                        diag = flatps[:, base[i] + k - P:base[i] + k]
                        n = min(k, HALF)
                        if i >= 2:
                            dve.wait_ge(exp_a, p * U + i - 1 + START)
                            dve.wait_ge(exp_b, p * before_b[U] + before_b[i - 1] + START)
                            dve.sem_inc(spare[1], 1)
                        if wide[i] and k - P < HALF:
                            dve.wait_ge(s_b, p * before_b[U] + before_b[i] + 1 + START)
                        late = wide[i] and k - P >= HALF
                        if not late:
                            dve.tensor_tensor(diag, diag, causal[:, :], ALU.add).then_inc(capped, 1)
                            dve.wait_ge(capped, p * U + i + 1 + START)
                        dve.tensor_reduce(nm[b][:, 0:1], flatps[:, base[i]:base[i] + n], AX.X, ALU.max,
                                          negate=True).then_inc(maxed if wide[i] else negm, 1)
                        if wide[i]:
                            if late:
                                dve.wait_ge(s_b, p * before_b[U] + before_b[i] + 1 + START)
                                dve.tensor_tensor(diag, diag, causal[:, :], ALU.add).then_inc(capped, 1)
                                dve.wait_ge(capped, p * U + i + 1 + START)
                            dve.tensor_reduce(nm[b][:, 1:2], flatps[:, n:k], AX.X, ALU.max,
                                              negate=True).then_inc(maxed, 1)
                            dve.wait_ge(maxed, (p * before_b[U] + before_b[i] + 1) * 2 + START)
                            dve.tensor_tensor(nm[b][:, 2:3], nm[b][:, 0:1], nm[b][:, 1:2], ALU.min).then_inc(negm, 1)

                    def probs_back(i, g):
                        nb = blocks[i]
                        full = min(4, nb - 1 - 4 * g)
                        dve.wait_ge(turned, p * before_g[U] + before_g[i] + g + 1 + START)
                        if full > 0:
                            ins = dve.tensor_copy(pT[g % 4][:, 0:full * P], ps[:, 5 + g % 2, 0:full * P])
                        if full < 4:
                            ins = dve.tensor_copy(pT[g % 4][0:META, full * P:(full + 1) * P],
                                                  ps[0:META, 5 + g % 2, full * P:(full + 1) * P])
                        ins.then_inc(pt_d, 1)

                    def normalise(i):
                        b, a = i % 2, i // NX
                        dve.wait_ge(exp_a, p * U + i + 1 + START)
                        src = rs[b][:, 0:1]
                        if wide[i]:
                            dve.wait_ge(exp_b, p * before_b[U] + before_b[i] + 1 + START)
                            dve.sem_inc(spare[1], 1)
                            dve.tensor_tensor(rsum[b][:, :], rs[b][:, 0:1], rs[b][:, 1:2], ALU.add).then_inc(summed, 1)
                            dve.wait_ge(summed, p * before_b[U] + before_b[i] + 1 + START)
                            src = rsum[b][:, :]
                        dve.reciprocal(rinv[b][:, :], src).then_inc(inverted, 1)
                        dve.wait_ge(inverted, p * U + i + 1 + START)
                        dve.wait_ge(attended, p * U + i + 1 + START)
                        dve.tensor_scalar(fo[pu][:, i % NX, a * FD:(a + 1) * FD], ps[:, 7, a * FD:(a + 1) * FD], rinv[b][:, 0:1], None,
                                          ALU.mult).then_inc(normed, 1)

                    for t in range(len(CH)):
                        proj_copy(t)
                    dve.wait_ge(fox_out[pu], j * 16 + START)
                    dve.sem_inc(spare[1], 1)
                    maxima(0)
                    for i in range(U):
                        if i + 1 < U:
                            maxima(i + 1)
                        for g in range(ga[i], groups[i]):
                            probs_back(i, g)
                        normalise(i)

        @block.tensor
        def _(pe):
            with pe.Fori(0, PAIRS // 2) as j:
                for pu in range(2):
                    p = j * 2 + pu

                    def project(t):
                        side, o, tok, n = CH[t]
                        if t >= 4:
                            pe.wait_ge(proj_a, p * len(CH) + t - 3 + START)
                            pe.wait_ge(proj_d, p * len(CH) + t - 3 + START)
                        for c in range(DC):
                            ins = pe.matmul(ps[:, t % 4, 0:n], wqk[pu][:, c, side * 2 * FD:(side + 1) * 2 * FD],
                                            hT[:, c, tok:tok + n], start=(c == 0), stop=(c == DC - 1))
                        ins.then_inc(proj, 1)

                    def scores(i):
                        k, a = keys[i], i // NX
                        q = qa[:, a, (i % NX) * P:(i % NX + 1) * P]
                        if i >= 1 and not wide[i] and not wide[i - 1]:
                            pe.wait_ge(exp_a, p * U + i - 1 + START)
                        else:
                            pe.wait_ge(exp_a, p * U + i + START)
                            if not wide[i]:
                                pe.wait_ge(exp_b, p * before_b[U] + before_b[i] + START)
                        for o in range(0, k, BANK):
                            n = min(BANK, k - o)
                            if o == HALF:
                                pe.wait_ge(exp_b, p * before_b[U] + before_b[i] + START)
                            ins = pe.matmul(ps[:, (base[i] + o) // BANK, 0:n], q, ka[:, a, o:o + n], start=True, stop=True)
                            if o + n == min(k, HALF):
                                ins.then_inc(s_a, 1)
                        if wide[i]:
                            ins.then_inc(s_b, 1)

                    def attend(i):
                        nb, a, b = blocks[i], i // NX, i % 2

                        def turn(g):
                            pe.wait_ge(pt_a, p * before_a[U] + before_a[i] + min(max(g - 1, 0), ga[i]) + START)
                            pe.wait_ge(pt_d, p * before_d[U] + before_d[i] + max(g - 3, 0) + START)
                            if 4 * g * P >= HALF:
                                pe.wait_ge(exp_b, p * before_b[U] + before_b[i] + 1 + START)
                            for x in range(4 * g, min(4 * g + 4, nb)):
                                rows = META if x == nb - 1 else P
                                ins = pe.transpose(ps[0:rows, 5 + g % 2, (x % 4) * P:(x % 4 + 1) * P],
                                                   prob[b][:, x * P:x * P + rows], ident[:, :])
                            ins.then_inc(turned, 1)

                        def weigh(g):
                            if g < ga[i]:
                                pe.wait_ge(pt_a, p * before_a[U] + before_a[i] + g + 1 + START)
                            else:
                                pe.wait_ge(pt_d, p * before_d[U] + before_d[i] + g - 1 + START)
                            for x in range(4 * g, min(4 * g + 4, nb)):
                                rows = META if x == nb - 1 else P
                                ins = pe.matmul(ps[:, 7, 0:2 * FD], pT[g % 4][0:rows, (x % 4) * P:(x % 4 + 1) * P],
                                                vp[pu][0:rows, x, :],
                                                start=(x == 0), stop=(x == nb - 1))
                            return ins

                        pe.wait_ge(exp_a, p * U + i + 1 + START)
                        pe.wait_ge(normed, p * U + i + START)
                        turn(0)
                        for g in range(groups[i]):
                            if g + 1 < groups[i]:
                                turn(g + 1)
                            ins = weigh(g)
                        ins.then_inc(attended, 1)

                    pe.wait_ge(w_s[pu], j * 32 + 32 + START)
                    pe.wait_ge(exp_a, p * U + START)
                    for t in range(len(CH)):
                        project(t)
                    pe.wait_ge(proj_a, (p + 1) * len(CH) + START)
                    pe.wait_ge(proj_d, (p + 1) * len(CH) + START)
                    pe.wait_ge(c_s, (p + 1) * 64 + START)
                    pe.wait_ge(v_s[pu], j * 32 + 32 + START)
                    scores(0)
                    for i in range(U):
                        if i + 1 < U:
                            scores(i + 1)
                        attend(i)


def wide(ap):
    return ap.rearrange("p a b -> p (a b)")


def middle_phase(nc, ps, square, mixed, h_rows, w_out, ln_g, ln_b, w_router, router_bias,
                 ws_gate, ws_up, ws_down, t_rows, base_rows, table, route):
    ident, iota, tables = route.ident, route.iota, route.tables
    with Phase(nc, "mid") as ph:
        sb, sem = ph.sb, ph.sem
        wo = sb("wo", [P, MIX // P, D])
        wgu = sb("wgu", [P, DC, 2 * FF])
        wdn = sb("wdn", [P, FC, D])
        wr = sb("wr", [P, DC, NE])
        grow, brow, rb = sb("grow", [P, D]), sb("brow", [P, D]), sb("rb", [P, NE])
        blank = sb("blank", [P, 2 * NE * SLOTS // P])
        zrow = sb("zrow", [1, D])
        mix = [sb(f"mix{b}", [P, MIX]) for b in range(2)]
        y = [sb(f"y{b}", [P, D]) for b in range(2)]
        mT = sb("mT", [P, MIX // P, P])
        tT = sb("tT", [P, DC, P])
        t = [sb(f"t{b}", [P, D]) for b in range(2)]
        base = [sb(f"base{b}", [P, D]) for b in range(2)]
        st, mv, ve, rstd, mhalf = (sb(n, s) for n, s in (("st", [P, 2, 6]), ("mv", [P, 2]), ("ve", [P, 1]),
                                                          ("rstd", [P, 1]), ("mhalf", [P, 1])))
        sc = [sb(f"sc{b}", [P, NE]) for b in range(2)]
        sig, hs, h2, h2T = sb("sig", [P, FF]), sb("hs", [P, FF]), sb("h2", [P, FF]), sb("h2T", [P, FC, P])
        biased, masked = sb("biased", [P, NE]), sb("masked", [P, NE])
        g8, gs, gv, gif, gm = sb("g8", [P, NG, 8]), sb("gs", [P, NG]), sb("gv", [P, 8]), sb("gif", [P, 8]), sb("gm", [P, NG])
        gi, e8 = sb("gi", [P, 8], U32), sb("e8", [P, 8], U32)
        goh = sb("goh", [P, NG, TOPG])
        v8, ef = sb("v8", [P, 8]), sb("ef", [P, 8])
        oh, tmp = sb("oh", [P, TOPK, NE]), sb("tmp", [P, TOPK, NE])
        chosen = sb("chosen", [P, NE])
        gk, gsum, ginv, rk = sb("gk", [P, TOPK]), sb("gsum", [P, 1]), sb("ginv", [P, 1]), sb("rk", [P, TOPK])
        slot = [sb(f"slot{b}", [P, TOPK], U32) for b in range(2)]
        entry = [sb(f"entry{b}", [P, TOPK, 2]) for b in range(2)]
        wo_s, w_s, const, cleared, blank_s = sem("wo"), sem("w"), sem("const"), sem("cleared"), sem("blank")
        mix_in, h_in = ph.sems("mix_in", 2), ph.sems("h_in", 2)
        t_out, base_out, scat = ph.sems("t_out", 2), ph.sems("base_out", 2), ph.zero_sems("scat", 2)
        mturned, mT_a, mT_d, projected, summed = (sem(n) for n in ("mturned", "mT_a", "mT_d", "projected", "summed"))
        stats, aggr, epsd, rstds, centred, scaled, t_ready = (
            sem(n) for n in ("stats", "aggr", "epsd", "rstds", "centred", "scaled", "t_ready"))
        tturned, tT_a, tT_d, routed, scored, gated_up, sigd, h_half, h_done, hturned, hT_c = (
            sem(n) for n in ("tturned", "tT_a", "tT_d", "routed", "scored", "gated_up", "sigd", "h_half", "h_done",
                             "hturned", "hT_c"))
        down, based, ranked, slotted, chain, run_s, tokens = (
            sem(n) for n in ("down", "based", "ranked", "slotted", "chain", "run", "tokens"))
        spare = [sem(f"spare{i}") for i in range(2)]
        block = ph.block()
        PAIRS_ = NX // 2
        CH_N = 20

        def pairs(eng, body):
            body(0)
            with eng.Fori(1, PAIRS_ - 1) as j:
                body(j)
            body(PAIRS_ - 1)

        def is_first(j, b):
            return isinstance(j, int) and j == 0 and b == 0

        def is_last(j, b):
            return isinstance(j, int) and j == PAIRS_ - 1 and b == 1

        def rows(ap, i):
            return ap[bass.ds(i * P, P), :]

        @block.sync
        def _(sp):
            def load(i, k, b):
                if k is not None:
                    sp.wait_ge(mturned, k + START)
                sp.dma_start(mix[b][:, :], rows(mixed, i)).then_inc(mix_in[b], 16)
                if k is not None:
                    sp.wait_ge(scaled, k + START)
                sp.dma_start(y[b][:, :], rows(h_rows, i)).then_inc(h_in[b], 16)

            load(0, None, 0)
            sp.dma_start(wo[:, :, :], w_out.rearrange("(c p) n -> p c n", p=P)).then_inc(wo_s, 16)
            load(1, None, 1)
            sp.dma_start(grow[:, :], ln_g.partition_broadcast(P)).then_inc(const, 16)
            sp.dma_start(brow[:, :], ln_b.partition_broadcast(P)).then_inc(const, 16)
            sp.dma_start(rb[:, :], router_bias.partition_broadcast(P)).then_inc(const, 16)
            sp.dma_start(wr[:, :, :], w_router.rearrange("(c p) n -> p c n", p=P)).then_inc(w_s, 16)
            sp.dma_start(wgu[:, :, 0:FF], ws_gate.rearrange("(c p) n -> p c n", p=P)).then_inc(w_s, 16)
            sp.dma_start(wgu[:, :, FF:2 * FF], ws_up.rearrange("(c p) n -> p c n", p=P)).then_inc(w_s, 16)
            sp.dma_start(wdn[:, :, :], ws_down.rearrange("(c p) n -> p c n", p=P)).then_inc(w_s, 16)
            sp.wait_ge(blank_s, 2 + START)
            sp.dma_start(table.rearrange("(p n) o -> p (n o)", p=P), blank[:, :]).then_inc(cleared, 16)
            sp.dma_start(t_rows[SEQ:SEQ + 1, :], zrow[:, :]).then_inc(cleared, 16)
            sp.dma_start(base_rows[SEQ:SEQ + 1, :], zrow[:, :]).then_inc(cleared, 16)

            def body(j):
                for b in range(2):
                    i = j * 2 + b
                    sp.wait_ge(t_ready, i + 1 + START)
                    sp.dma_start(rows(t_rows, i), t[b][:, :]).then_inc(t_out[b], 16)
                    if not (isinstance(j, int) and j == PAIRS_ - 1):
                        load(i + 2, i + 1, b)
                    sp.wait_ge(based, i + 1 + START)
                    sp.dma_start(rows(base_rows, i), base[b][:, :]).then_inc(base_out[b], 16)

            pairs(sp, body)
            for b in range(2):
                sp.wait_ge(t_out[b], 16 * PAIRS_ + START)
                sp.wait_ge(base_out[b], 16 * PAIRS_ + START)

        @block.gpsimd
        def _(pool):
            pool.memset(mhalf[:, :], -0.5).then_inc(tokens, 1)
            pool.memset(blank[:, :], float(SEQ)).then_inc(blank_s, 1)
            pool.memset(zrow[:, :], 0.0).then_inc(blank_s, 1)
            pool.memset(route.count[:, :], 0.0).then_inc(tokens, 1)
            for b in range(2):
                pool.wait_ge(tables, 16)
                pool.tensor_scalar(entry[b][:, :, 0], route.pcol.to_broadcast([P, TOPK]), float((b - 2) * P), None,
                                   ALU.add).then_inc(tokens, 1)
            pool.wait_ge(tokens, 4 + START)
            pool.wait_ge(const, 48 + START)

            def norm(i):
                pool.wait_ge(aggr, i + 1 + START)
                pool.sem_inc(spare[0], 1)
                pool.tensor_scalar(ve[:, :], mv[:, 1:2], EPS, None, ALU.add).then_inc(epsd, 1)
                pool.wait_ge(epsd, i + 1 + START)
                pool.tensor_tensor(rstd[:, :], ve[:, :], mhalf[:, :], ALU.pow).then_inc(rstds, 1)

            def shift(i, b):
                pool.wait_ge(scaled, i + 1 + START)
                pool.tensor_tensor(t[b][:, :], t[b][:, :], brow[:, :], ALU.add).then_inc(t_ready, 1)

            def scatter(i, j, b):
                if not (isinstance(i, int) and i == 0):
                    pool.wait_ge(scat[1 - b], (j + b) * (16 * TOPK))
                    pool.sem_inc(spare[0], 1)
                pool.tensor_scalar(entry[b][:, :, 0], entry[b][:, :, 0], float(2 * P), None, ALU.add).then_inc(tokens, 1)
                pool.wait_ge(tokens, i + 5 + START)
                pool.wait_ge(slotted, i + 1 + START)
                pool.sem_inc(spare[0], 1)
                for k in range(TOPK):
                    pool.indirect_dma_start(out=table, out_offset=bass.IndirectOffsetOnAxis(ap=slot[b][:, k:k + 1], axis=0),
                                            in_=entry[b][:, k, :], in_offset=None).then_inc(scat[b], 16)

            norm(0)
            shift(0, 0)
            pool.wait_ge(cleared, 48 + START)

            def body(j):
                for b in range(2):
                    i = j * 2 + b
                    if not is_last(j, b):
                        norm(i + 1)
                        shift(i + 1, 1 - b)
                    if not is_first(j, b):
                        scatter(i - 1, j - 1 + b, 1 - b)

            pairs(pool, body)
            scatter(NX - 1, PAIRS_ - 1, 1)
            for b in range(2):
                pool.wait_ge(scat[b], 16 * TOPK * PAIRS_)

        @block.scalar
        def _(act):
            def mT_copy(i):
                act.wait_ge(mturned, i + 1 + START)
                nc.scalar.copy(flat(mT[:, 0:4, :]), ps[:, 0, :]).then_inc(mT_a, 1)

            mT_copy(0)

            def body(j):
                for b in range(2):
                    i = j * 2 + b
                    if not is_last(j, b):
                        mT_copy(i + 1)
                    act.wait_ge(tturned, i + 1 + START)
                    nc.scalar.copy(flat(tT[:, 0:4, :]), ps[:, 0, :]).then_inc(tT_a, 1)
                    act.wait_ge(chain, i * CH_N + START)
                    act.wait_ge(routed, i + 1 + START)
                    act.sem_inc(spare[1], 1)
                    nc.scalar.activation(sc[b][:, :], ps[:, 6, 0:NE], ACT.Sigmoid).then_inc(scored, 1)
                    act.wait_ge(gated_up, i + 1 + START)
                    act.wait_ge(h_done, i + START)
                    act.sem_inc(spare[1], 1)
                    nc.scalar.activation(sig[:, :], ps[:, 7, 0:FF], ACT.Sigmoid).then_inc(sigd, 1)
                    act.wait_ge(hturned, i + 1 + START)
                    nc.scalar.copy(flat(h2T[:, :, :]), ps[:, 6, 0:FF]).then_inc(hT_c, 1)

            pairs(act, body)

        @block.vector
        def _(dve):
            dve.wait_ge(const, 48 + START)
            dve.wait_ge(tables, 16)
            dve.wait_ge(tokens, 4 + START)

            def mT_copy(i):
                dve.wait_ge(mturned, i + 1 + START)
                dve.tensor_copy(flat(mT[:, 4:8, :]), ps[:, 1, :]).then_inc(mT_d, 1)

            def residual(i, b):
                dve.wait_ge(h_in[b], (i - b) * 8 + 16 + START)
                dve.wait_ge(projected, i + 1 + START)
                dve.sem_inc(spare[0], 1)
                dve.scalar_tensor_tensor(out=y[b][:, :], in0=y[b][:, :], scalar=ALPHA, in1=wide(ps[:, 2:4, :]),
                                         op0=ALU.mult, op1=ALU.add).then_inc(summed, 1)
                dve.wait_ge(summed, i + 1 + START)
                for a in range(2):
                    dve.bn_stats(st[:, a, :], y[b][:, a * BANK:(a + 1) * BANK]).then_inc(stats, 1)
                dve.wait_ge(stats, i * 2 + 2 + START)
                dve.wait_ge(scaled, i + START)
                dve.sem_inc(spare[0], 1)
                dve.bn_aggr(mv[:, :], st[:, :, :]).then_inc(aggr, 1)
                dve.wait_ge(rstds, i + 1 + START)
                dve.wait_ge(aggr, i + 1 + START)
                dve.sem_inc(spare[0], 1)
                dve.tensor_scalar(y[b][:, :], y[b][:, :], mv[:, 0:1], rstd[:, 0:1], ALU.subtract, ALU.mult).then_inc(centred, 1)
                dve.wait_ge(t_out[b], (i - b) * 8 + START)
                dve.wait_ge(centred, i + 1 + START)
                dve.sem_inc(spare[0], 1)
                dve.tensor_tensor(t[b][:, :], y[b][:, :], grow[:, :], ALU.mult).then_inc(scaled, 1)

            def pick(i, b, at):
                n = [0]

                def link(ins, hold=False):
                    n[0] += 1
                    ins.then_inc(chain, 1)
                    dve.wait_ge(chain, i * CH_N + n[0] + START)
                    if hold:
                        dve.sem_inc(spare[0], 1)

                dve.wait_ge(scored, i + 1 + START)
                link(dve.tensor_tensor(biased[:, :], sc[b][:, :], rb[:, :], ALU.add), True)
                for g in range(NG):
                    ins = dve.max(g8[:, g, :], biased[:, g * GE:(g + 1) * GE])
                link(ins)
                link(dve.tensor_tensor(gs[:, :], g8[:, :, 0], g8[:, :, 1], ALU.add), True)
                link(dve.max(gv[:, :], gs[:, :]), True)
                link(dve.max_index(gi[:, :], gv[:, :], gs[:, :]))
                link(dve.tensor_copy(gif[:, :], gi[:, :]))
                link(dve.tensor_tensor(goh[:, :, :], iota[:, 0:NG].unsqueeze(2).to_broadcast([P, NG, TOPG]),
                                       gif[:, 0:TOPG].unsqueeze(1).to_broadcast([P, NG, TOPG]), ALU.is_equal))
                link(dve.tensor_reduce(gm[:, :], goh[:, :, :], AX.X, ALU.max))
                link(dve.tensor_scalar(gm[:, :], gm[:, :], -1.0, -NEG, ALU.add, ALU.mult))
                link(dve.tensor_tensor(masked[:, :].rearrange("p (g e) -> p g e", g=NG),
                                       biased[:, :].rearrange("p (g e) -> p g e", g=NG),
                                       gm[:, :].unsqueeze(2).to_broadcast([P, NG, GE]), ALU.add), True)
                link(dve.max(v8[:, :], masked[:, :]), True)
                link(dve.max_index(e8[:, :], v8[:, :], masked[:, :]))
                link(dve.tensor_copy(ef[:, :], e8[:, :]))
                link(dve.tensor_tensor(oh[:, :, :], iota.unsqueeze(1).to_broadcast([P, TOPK, NE]),
                                       ef[:, 0:TOPK].unsqueeze(2).to_broadcast([P, TOPK, NE]), ALU.is_equal))
                link(dve.tensor_reduce(chosen[:, :], oh[:, :, :].rearrange("p k e -> p e k"), AX.X, ALU.add))
                link(dve.tensor_tensor(tmp[:, :, :], oh[:, :, :], sc[b][:, :].unsqueeze(1).to_broadcast([P, TOPK, NE]),
                                       ALU.mult))
                link(dve.tensor_reduce(gk[:, :], tmp[:, :, :], AX.X, ALU.add))
                link(dve.tensor_reduce(gsum[:, :], gk[:, :], AX.X, ALU.add))
                link(dve.reciprocal(ginv[:, :], gsum[:, :]))
                dve.sem_inc(spare[0], 1)
                link(dve.tensor_scalar(route.gate[:, at, :], gk[:, :], ginv[:, 0:1], ROUTED, ALU.mult, ALU.mult))
                assert n[0] == CH_N

            def number(i, j, b, at):
                dve.wait_ge(ranked, i + 1 + START)
                dve.tensor_tensor(tmp[:, :, :], oh[:, :, :], ps[:, 6, 0:NE].unsqueeze(1).to_broadcast([P, TOPK, NE]),
                                  ALU.mult).then_inc(run_s, 1)
                dve.wait_ge(run_s, i * 3 + 1 + START)
                dve.tensor_reduce(rk[:, :], tmp[:, :, :], AX.X, ALU.add).then_inc(run_s, 1)
                dve.wait_ge(run_s, i * 3 + 2 + START)
                dve.wait_ge(tokens, i + 4 + START)
                dve.sem_inc(spare[0], 1)
                dve.tensor_copy(route.expert[:, at, :], ef[:, 0:TOPK])
                dve.tensor_copy(route.rank[:, at, :], rk[:, :])
                dve.tensor_copy(entry[b][:, :, 1], route.gate[:, at, :].rearrange("p a k -> p (a k)"))
                dve.tensor_tensor(route.count[:, :], route.count[:, :], chosen[:, :], ALU.add).then_inc(run_s, 1)
                dve.scalar_tensor_tensor(out=slot[b][:, :], in0=ef[:, 0:TOPK], scalar=float(SLOTS), in1=rk[:, :],
                                         op0=ALU.mult, op1=ALU.add).then_inc(slotted, 1)

            mT_copy(0)
            residual(0, 0)

            def body(j):
                for b in range(2):
                    i = j * 2 + b
                    prev = (i - 1) if isinstance(j, int) else bass.ds(i - 1, 1)
                    if not is_last(j, b):
                        mT_copy(i + 1)
                    if not is_first(j, b):
                        pick_at(i - 1, 1 - b)
                    dve.wait_ge(tturned, i + 1 + START)
                    dve.tensor_copy(flat(tT[:, 4:8, :]), ps[:, 1, :]).then_inc(tT_d, 1)
                    if not is_last(j, b):
                        residual(i + 1, 1 - b)
                    dve.wait_ge(sigd, i + 1 + START)
                    dve.tensor_tensor(hs[:, :], sig[:, :], ps[:, 7, 0:FF], ALU.mult).then_inc(h_half, 1)
                    dve.wait_ge(h_half, i + 1 + START)
                    dve.tensor_tensor(h2[:, :], hs[:, :], ps[:, 7, FF:2 * FF], ALU.mult).then_inc(h_done, 1)
                    if not is_first(j, b):
                        number_at(i - 1, j - 1 + b, 1 - b)
                    dve.wait_ge(base_out[b], j * 16 + START)
                    dve.wait_ge(down, i + 1 + START)
                    dve.wait_ge(t_ready, i + 1 + START)
                    dve.sem_inc(spare[0], 1)
                    dve.scalar_tensor_tensor(out=base[b][:, :], in0=t[b][:, :], scalar=ALPHA, in1=wide(ps[:, 4:6, :]),
                                             op0=ALU.mult, op1=ALU.add).then_inc(based, 1)

            def sl(i):
                return slice(i, i + 1) if isinstance(i, int) else bass.ds(i, 1)

            def pick_at(i, b):
                pick(i, b, sl(i))

            def number_at(i, j, b):
                number(i, j, b, sl(i))

            pairs(dve, body)
            pick_at(NX - 1, 1)
            number_at(NX - 1, PAIRS_ - 1, 1)

        @block.tensor
        def _(pe):
            def project(i, b):
                pe.wait_ge(mix_in[b], (i - b) * 8 + 16 + START)
                if not (isinstance(i, int) and i == 0):
                    pe.wait_ge(tT_a, i - 1 + START)
                    pe.wait_ge(tT_d, i - 1 + START)
                for c in range(MIX // P):
                    ins = pe.transpose(ps[:, c // 4, (c % 4) * P:(c % 4 + 1) * P], mix[b][:, c * P:(c + 1) * P], ident)
                ins.then_inc(mturned, 1)
                pe.wait_ge(mT_a, i + 1 + START)
                pe.wait_ge(mT_d, i + 1 + START)
                pe.wait_ge(summed, i + START)
                for a in range(2):
                    for c in range(MIX // P):
                        ins = pe.matmul(ps[:, 2 + a, :], mT[:, c, :], wo[:, c, a * BANK:(a + 1) * BANK],
                                        start=(c == 0), stop=(c == MIX // P - 1))
                ins.then_inc(projected, 1)

            def rank(i):
                pe.wait_ge(chain, i * CH_N + 15 + START)
                pe.wait_ge(run_s, i * 3 + START)
                pe.matmul(ps[:, 6, 0:NE], route.before, chosen[:, :], start=True, stop=False)
                pe.matmul(ps[:, 6, 0:NE], route.ones[:, :], route.count[:, :], start=False, stop=True).then_inc(ranked, 1)

            pe.wait_ge(wo_s, 16 + START)
            pe.wait_ge(tables, 16)
            pe.wait_ge(route.ones_set, 1)
            project(0, 0)
            pe.wait_ge(w_s, 16 * 4 + START)

            def body(j):
                for b in range(2):
                    i = j * 2 + b
                    if not is_last(j, b):
                        project(i + 1, 1 - b)
                        pe.wait_ge(mT_a, i + 2 + START)
                        pe.wait_ge(mT_d, i + 2 + START)
                    pe.wait_ge(t_ready, i + 1 + START)
                    for c in range(DC):
                        ins = pe.transpose(ps[:, c // 4, (c % 4) * P:(c % 4 + 1) * P], t[b][:, c * P:(c + 1) * P], ident)
                    ins.then_inc(tturned, 1)
                    pe.wait_ge(tT_a, i + 1 + START)
                    pe.wait_ge(tT_d, i + 1 + START)
                    pe.wait_ge(hT_c, i + START)
                    for c in range(DC):
                        ins = pe.matmul(ps[:, 6, 0:NE], tT[:, c, :], wr[:, c, :], start=(c == 0), stop=(c == DC - 1))
                    ins.then_inc(routed, 1)
                    pe.wait_ge(h_done, i + START)
                    for c in range(DC):
                        ins = pe.matmul(ps[:, 7, :], tT[:, c, :], wgu[:, c, :], start=(c == 0), stop=(c == DC - 1))
                    ins.then_inc(gated_up, 1)
                    pe.wait_ge(scored, i + 1 + START)
                    if not is_first(j, b):
                        rank(i - 1)
                        pe.wait_ge(run_s, i * 3 - 2 + START)
                    pe.wait_ge(h_done, i + 1 + START)
                    for c in range(FC):
                        ins = pe.transpose(ps[:, 6, c * P:(c + 1) * P], h2[:, c * P:(c + 1) * P], ident)
                    ins.then_inc(hturned, 1)
                    pe.wait_ge(hT_c, i + 1 + START)
                    pe.wait_ge(based, i + START)
                    for a in range(2):
                        for c in range(FC):
                            ins = pe.matmul(ps[:, 4 + a, :], h2T[:, c, :], wdn[:, c, a * BANK:(a + 1) * BANK],
                                            start=(c == 0), stop=(c == FC - 1))
                    ins.then_inc(down, 1)

            pairs(pe, body)
            rank(NX - 1)


class Route:

    def __init__(self, nc, ctx):
        sb = lambda n, s, dt=F32: ctx.enter_context(nc.sbuf_tensor(n, s, dt))
        self.sq = sb("sq", [P, SQ_COLS])
        self.ident = self.sq[:, SQ_IDENT:SQ_IDENT + P]
        self.causal = self.sq[:, SQ_CAUSAL:SQ_CAUSAL + P]
        self.before = self.sq[:, SQ_BEFORE:SQ_BEFORE + P]
        self.iota = self.sq[:, SQ_IOTA:SQ_IOTA + NE]
        self.slot0 = self.sq[:, SQ_SLOT0:SQ_SLOT0 + NE]
        self.thr = self.sq[:, SQ_THR:SQ_THR + NTHR]
        self.pcol = self.sq[:, SQ_PCOL:SQ_PCOL + 1]
        self.ones = sb("ones", [P, P])
        self.count = sb("count", [P, NE])
        self.expert = sb("expert", [P, NX, TOPK])
        self.rank = sb("rank", [P, NX, TOPK])
        self.gate = sb("gate", [P, NX, TOPK])
        self.extra0 = sb("extra0", [P, NE])
        self.index = sb("index", [P, NE * (CAP // P)], U32)
        self.over = sb("over", [1, 2 * P], I32)
        self.n_over = sb("n_over", [1, 1], I32)
        self.tables = ctx.enter_context(nc.semaphore("tables"))
        self.ones_set = ctx.enter_context(nc.semaphore("ones_set"))


def table_phase(nc, ps, table, over_rows, route):
    NBLK = NE * (CAP // P)
    with Phase(nc, "tab") as ph:
        sb, sem = ph.sb, ph.sem
        lists = sb("lists", [NBLK, P, 2])
        cnt, more, nov, end = sb("cnt", [P, NE]), sb("more", [P, NE, NTHR]), sb("nov", [P, NE]), sb("end", [P, NE])
        a_, b_, m_ = sb("a", [P, NE]), sb("b", [P, NE]), sb("m", [P, NE])
        place, onesr = sb("place", [P, NE]), sb("onesr", [P, NE])
        ej, sj, both = sb("ej", [P, 1]), sb("sj", [P, 1]), sb("both", [P, 2], I32)
        listed, turned, counted, chain, over_s, back, done = (
            sem(n) for n in ("listed", "turned", "counted", "chain", "over", "back", "done"))
        block = ph.block()

        @block.sync
        def _(sp):
            src = table.rearrange("(e b p) o -> e b (p o)", b=SLOTS // P, p=P)
            for k in range(CAP // P):
                sp.dma_start(flat(lists[k * NE:(k + 1) * NE, :, :]), src[:, k, :]).then_inc(listed, 16)
            sp.wait_ge(done, 1 + START)
            sp.dma_start(over_rows, both[:, :]).then_inc(over_s, 16)
            sp.wait_ge(over_s, 16 + START)
            sp.dma_start(route.over[:, :], over_rows.rearrange("(o p) k -> o (p k)", o=1)).then_inc(back, 16)
            sp.wait_ge(back, 16 + START)

        @block.tensor
        def _(pe):
            pe.matmul(ps[:, 0, 0:NE], route.ones[:, :], route.count[:, :], start=True, stop=True).then_inc(counted, 1)
            pe.wait_ge(listed, 16 * (CAP // P) + START)
            pe.transpose(ps[:, 1, 0:NBLK], lists[:, :, 0], route.ident).then_inc(turned, 1)

        @block.vector
        def _(dve):
            n = [0]

            def link(ins):
                n[0] += 1
                ins.then_inc(chain, 1)
                dve.wait_ge(chain, n[0] + START)

            link(dve.memset(onesr[:, :], 1.0))
            dve.wait_ge(counted, 1 + START)
            link(dve.tensor_copy(cnt[:, :], ps[:, 0, 0:NE]))
            link(dve.tensor_tensor(more[:, :, :], cnt[:, :].unsqueeze(2).to_broadcast([P, NE, NTHR]),
                                   route.thr.unsqueeze(1).to_broadcast([P, NE, NTHR]), ALU.is_gt))
            link(dve.tensor_reduce(nov[:, :], more[:, :, :], AX.X, ALU.add))
            link(dve.tensor_tensor_scan(end[:, :], onesr[:, :], nov[:, :], 0.0, ALU.mult, ALU.add))
            link(dve.tensor_tensor(route.extra0[:, :], end[:, :], nov[:, :], ALU.subtract))
            link(dve.tensor_copy(route.n_over[:, :], end[0:1, NE - 1:NE]))
            link(dve.tensor_scalar(a_[:, :], route.extra0[:, :], route.pcol, None, ALU.is_le))
            link(dve.tensor_scalar(b_[:, :], end[:, :], route.pcol, None, ALU.is_gt))
            link(dve.tensor_tensor(m_[:, :], a_[:, :], b_[:, :], ALU.mult))
            link(dve.tensor_tensor(a_[:, :], m_[:, :], route.iota, ALU.mult))
            link(dve.tensor_reduce(ej[:, :], a_[:, :], AX.X, ALU.add))
            link(dve.scalar_tensor_tensor(out=place[:, :], in0=route.extra0[:, :], scalar=-float(P), in1=route.slot0,
                                          op0=ALU.mult, op1=ALU.add))
            link(dve.tensor_scalar(a_[:, :], route.pcol.to_broadcast([P, NE]), float(P), float(CAP), ALU.mult, ALU.add))
            link(dve.tensor_tensor(place[:, :], place[:, :], a_[:, :], ALU.add))
            link(dve.tensor_tensor(b_[:, :], m_[:, :], place[:, :], ALU.mult))
            link(dve.tensor_reduce(sj[:, :], b_[:, :], AX.X, ALU.add))
            link(dve.tensor_copy(both[:, 0:1], ej[:, :]))
            dve.tensor_copy(both[:, 1:2], sj[:, :]).then_inc(done, 1)
            dve.wait_ge(turned, 1 + START)
            link(dve.tensor_copy(route.index[:, :], ps[:, 1, 0:NBLK]))


def expert_phase(nc, ps, t_rows, we_gate, we_up, we_down, y_rows, route):
    with Phase(nc, "exp") as ph:
        sb, sem = ph.sb, ph.sem
        NBK = CAP // P
        wg = [sb(f"wg{u}", [P, DC, FF]) for u in range(2)]
        wu = [sb(f"wu{u}", [P, DC, FF]) for u in range(2)]
        wd = [sb(f"wd{u}", [P, FC, D]) for u in range(2)]
        xg = [[sb(f"xg{u}{k}", [P, D]) for k in range(NBK)] for u in range(2)]
        ix = [[sb(f"ix{u}{k}", [P, 1], U32) for k in range(NBK)] for u in range(2)]
        xT = [sb(f"xT{u}", [P, DC, CAP]) for u in range(2)]
        sl = [sb(f"sl{f}", [P, CAP]) for f in range(FC)]
        hh = [sb(f"hh{u}", [P, FC, CAP]) for u in range(2)]
        yo = [[sb(f"yo{u}{k}", [P, D]) for k in range(NBK)] for u in range(2)]
        wgu_in, wd_in, rows_in = ph.sems("wgu_in", 2), ph.sems("wd_in", 2), ph.zero_sems("rows_in", 4)
        y_out = ph.sems("y_out", 4)
        turned, gu, down = ph.sems("turned", 2), ph.sems("gu", 2), ph.sems("down", 2)
        ixd, xT_a, xT_d, silud, hd, y_a, y_d = (sem(n) for n in ("ixd", "xT_a", "xT_d", "silud", "hd", "y_a", "y_d"))
        spare = [sem(f"spare{i}") for i in range(2)]
        block = ph.block()
        N2 = NE // 2

        @block.sync
        def _(sp):
            with sp.Fori(0, N2) as j:
                for u in range(2):
                    e = j * 2 + u
                    one = lambda w: w[bass.ds(e, 1)].rearrange("a (c p) f -> p (a c) f", p=P)
                    sp.wait_ge(gu[u], j * FC + START)
                    sp.dma_start(wg[u][:, :, :], one(we_gate)).then_inc(wgu_in[u], 16)
                    sp.dma_start(wu[u][:, :, :], one(we_up)).then_inc(wgu_in[u], 16)
                    sp.wait_ge(down[u], j * NBK + START)
                    sp.dma_start(wd[u][:, :, :], one(we_down)).then_inc(wd_in[u], 16)

        @block.gpsimd
        def _(pool):
            with pool.Fori(0, N2) as j:
                for u in range(2):
                    for k in range(NBK):
                        s = u * NBK + k
                        pool.wait_ge(turned[u], j * (2 * NBK) + START)
                        pool.sem_inc(spare[0], 1)
                        pool.tensor_copy(ix[u][k][:, :], route.index[:, bass.ds(j * 2 + (u + k * NE), 1)]).then_inc(ixd, 1)
                        pool.wait_ge(ixd, j * (2 * NBK) + s + 1 + START)
                        pool.sem_inc(spare[0], 1)
                        pool.indirect_dma_start(out=xg[u][k][:, :], out_offset=None, in_=t_rows,
                                                in_offset=bass.IndirectOffsetOnAxis(ap=ix[u][k][:, :], axis=0)
                                                ).then_inc(rows_in[s], 16)

        def run(eng, body):
            with eng.Fori(0, N2 - 1) as j:
                body(j)
            body(N2 - 1)

        def last(j, u):
            return isinstance(j, int) and u == 1

        @block.scalar
        def _(act):
            def x_copy(j, u, g):
                act.wait_ge(turned[u], j * 4 + g + 1 + START)
                k = g // 2
                nc.scalar.copy(xT[u][:, 0:4, k * P:(k + 1) * P],
                               ps[:, 0, :].rearrange("p (c t) -> p c t", c=4)).then_inc(xT_a, 1)

            x_copy(0, 0, 0)
            x_copy(0, 0, 2)

            def body(j):
                for u in range(2):
                    e = j * 2 + u
                    for f in range(FC):
                        act.wait_ge(gu[u], j * FC + f + 1 + START)
                        act.wait_ge(hd, e * FC + START)
                        act.sem_inc(spare[1], 1)
                        nc.scalar.activation(sl[f][:, :], ps[:, 2 + f, 0:CAP], ACT.Silu).then_inc(silud, 1)
                    if not last(j, u):
                        x_copy(j + u, 1 - u, 0)
                    for k in range(NBK):
                        act.wait_ge(y_out[u * NBK + k], j * 16 + START)
                        act.wait_ge(down[u], j * NBK + k + 1 + START)
                        act.sem_inc(spare[1], 1)
                        nc.scalar.copy(yo[u][k][:, 0:BANK], ps[:, 4 + 2 * k, :]).then_inc(y_a, 1)
                        if k == 0 and not last(j, u):
                            x_copy(j + u, 1 - u, 2)
                        act.wait_ge(y_d, e * NBK + k + 1 + START)
                        act.wait_ge(y_a, e * NBK + k + 1 + START)
                        act.dma_start(y_rows[bass.ds(e * CAP + k * P, P), :], yo[u][k][:, :]).then_inc(y_out[u * NBK + k], 16)

            run(act, body)
            for s in range(2 * NBK):
                act.wait_ge(y_out[s], 16 * N2 + START)

        @block.vector
        def _(dve):
            def x_copy(j, u, g):
                dve.wait_ge(turned[u], j * 4 + g + 1 + START)
                k = g // 2
                dve.tensor_copy(xT[u][:, 4:8, k * P:(k + 1) * P],
                                ps[:, 1, :].rearrange("p (c t) -> p c t", c=4)).then_inc(xT_d, 1)

            x_copy(0, 0, 1)
            x_copy(0, 0, 3)

            def body(j):
                for u in range(2):
                    e = j * 2 + u
                    for f in range(FC):
                        dve.wait_ge(silud, e * FC + f + 1 + START)
                        dve.tensor_tensor(hh[u][:, f, :], sl[f][:, :], ps[:, 2 + f, CAP:2 * CAP], ALU.mult).then_inc(hd, 1)
                    if not last(j, u):
                        x_copy(j + u, 1 - u, 1)
                    for k in range(NBK):
                        dve.wait_ge(y_out[u * NBK + k], j * 16 + START)
                        dve.wait_ge(down[u], j * NBK + k + 1 + START)
                        dve.sem_inc(spare[0], 1)
                        dve.tensor_copy(yo[u][k][:, BANK:D], ps[:, 5 + 2 * k, :]).then_inc(y_d, 1)
                        if k == 0 and not last(j, u):
                            x_copy(j + u, 1 - u, 3)

            run(dve, body)

        @block.tensor
        def _(pe):
            def turn(e, j, u, g):
                k, h = g // 2, g % 2
                if h == 0:
                    pe.wait_ge(rows_in[u * NBK + k], j * 16 + 16)
                pe.wait_ge(xT_d if h else xT_a, e * 2 + k + START)
                for c in range(4):
                    ins = pe.transpose(ps[:, h, c * P:(c + 1) * P], xg[u][k][:, (4 * h + c) * P:(4 * h + c + 1) * P],
                                       route.ident)
                ins.then_inc(turned[u], 1)

            for g in range(4):
                turn(0, 0, 0, g)

            def body(j):
                for u in range(2):
                    e = j * 2 + u
                    pe.wait_ge(xT_a, e * 2 + 2 + START)
                    pe.wait_ge(xT_d, e * 2 + 2 + START)
                    pe.wait_ge(wgu_in[u], j * 32 + 32 + START)
                    for f in range(FC):
                        pe.wait_ge(hd, e * FC + START)
                        for s, w in enumerate((wg[u], wu[u])):
                            for c in range(DC):
                                ins = pe.matmul(ps[:, 2 + f, s * CAP:(s + 1) * CAP], w[:, c, f * P:(f + 1) * P],
                                                xT[u][:, c, :], start=(c == 0), stop=(c == DC - 1))
                        ins.then_inc(gu[u], 1)
                    nj = j + u
                    if not last(j, u):
                        turn(e + 1, nj, 1 - u, 0)
                        turn(e + 1, nj, 1 - u, 1)
                    pe.wait_ge(hd, e * FC + FC + START)
                    pe.wait_ge(wd_in[u], j * 16 + 16 + START)
                    for k in range(NBK):
                        pe.wait_ge(y_a, e * NBK + START)
                        pe.wait_ge(y_d, e * NBK + START)
                        for h in range(2):
                            for f in range(FC):
                                ins = pe.matmul(ps[:, 4 + 2 * k + h, :], hh[u][:, f, k * P:(k + 1) * P],
                                                wd[u][:, f, h * BANK:(h + 1) * BANK], start=(f == 0), stop=(f == FC - 1))
                        ins.then_inc(down[u], 1)
                        if k == 0 and not last(j, u):
                            turn(e + 1, nj, 1 - u, 2)
                            turn(e + 1, nj, 1 - u, 3)

            run(pe, body)


def overflow_phase(nc, ps, t_rows, table, we_gate, we_up, we_down, base_rows, route):
    with Phase(nc, "ovf") as ph:
        sb, sem = ph.sb, ph.sem
        wg, wu, wd = sb("wg", [P, DC, FF]), sb("wu", [P, DC, FF]), sb("wd", [P, FC, D])
        ids, ix = sb("ids", [P, 2]), sb("ix", [P, 1], U32)
        xg, xT, base = sb("xg", [P, D]), sb("xT", [P, DC, P]), sb("base", [P, D])
        sl, hh, yo = sb("sl", [P, FC, P]), sb("hh", [P, FC, P]), sb("yo", [P, D])
        w_s, ids_in, ixd, freed = (sem(n) for n in ("w", "ids_in", "ixd", "freed"))
        rows_in, sums_in, y_done = (ph.zero_sems(n, 1)[0] for n in ("rows_in", "sums_in", "y_done"))
        turned, xT_c, gu, silud, hd, down, copied = (
            sem(n) for n in ("turned", "xT_c", "gu", "silud", "hd", "down", "copied"))
        spare = [sem(f"spare{i}") for i in range(3)]
        block = ph.block()

        def blocks(eng, body):
            n = eng.value_load(route.n_over[0:1, 0:1], min_val=0, max_val=MAXOV)
            with eng.Fori(0, MAXOV) as j:
                with eng.If(n > j):
                    body(j)
                eng.nop()

        @block.sync
        def _(sp):
            def body(j):
                e = sp.value_load(route.over[0:1, bass.ds(j * 2, 1)], min_val=0, max_val=NE - 1)
                s = sp.value_load(route.over[0:1, bass.ds(j * 2 + 1, 1)], min_val=0, max_val=NE * SLOTS - P)
                one = lambda w: w[bass.ds(e, 1)].rearrange("a (c p) f -> p (a c) f", p=P)
                sp.wait_ge(freed, j + START)
                sp.sem_inc(spare[0], 1)
                sp.dma_start(ids[:, :], table[bass.ds(s, P), :]).then_inc(ids_in, 16)
                sp.dma_start(wg[:, :, :], one(we_gate)).then_inc(w_s, 16)
                sp.dma_start(wu[:, :, :], one(we_up)).then_inc(w_s, 16)
                sp.dma_start(wd[:, :, :], one(we_down)).then_inc(w_s, 16)

            blocks(sp, body)

        @block.gpsimd
        def _(pool):
            def body(j):
                pool.wait_ge(ids_in, j * 16 + 16 + START)
                pool.sem_inc(spare[1], 1)
                pool.tensor_copy(ix[:, :], ids[:, 0:1]).then_inc(ixd, 1)
                pool.wait_ge(ixd, j + 1 + START)
                pool.sem_inc(spare[1], 1)
                pool.indirect_dma_start(out=xg[:, :], out_offset=None, in_=t_rows,
                                        in_offset=bass.IndirectOffsetOnAxis(ap=ix[:, :], axis=0)).then_inc(rows_in, 16)
                pool.indirect_dma_start(out=base[:, :], out_offset=None, in_=base_rows,
                                        in_offset=bass.IndirectOffsetOnAxis(ap=ix[:, :], axis=0)).then_inc(sums_in, 16)
                pool.wait_ge(copied, j + 1 + START)
                pool.sem_inc(spare[1], 1)
                pool.indirect_dma_start(out=base_rows, out_offset=bass.IndirectOffsetOnAxis(ap=ix[:, :], axis=0),
                                        in_=yo[:, :], in_offset=None).then_inc(y_done, 16)
                pool.wait_ge(y_done, j * 16 + 16)
                pool.sem_inc(freed, 1)

            blocks(pool, body)

        @block.tensor
        def _(pe):
            def body(j):
                pe.wait_ge(rows_in, j * 16 + 16)
                for c in range(DC):
                    ins = pe.transpose(ps[:, c // 4, (c % 4) * P:(c % 4 + 1) * P], xg[:, c * P:(c + 1) * P], route.ident)
                ins.then_inc(turned, 1)
                pe.wait_ge(xT_c, j + 1 + START)
                pe.wait_ge(w_s, j * 48 + 48 + START)
                for s, w in enumerate((wg, wu)):
                    for f in range(FC):
                        for c in range(DC):
                            ins = pe.matmul(ps[:, 2 + s, f * P:(f + 1) * P], w[:, c, f * P:(f + 1) * P], xT[:, c, :],
                                            start=(c == 0), stop=(c == DC - 1))
                ins.then_inc(gu, 1)
                pe.wait_ge(hd, j + 1 + START)
                for h in range(2):
                    for f in range(FC):
                        ins = pe.matmul(ps[:, 4 + h, :], hh[:, f, :], wd[:, f, h * BANK:(h + 1) * BANK],
                                        start=(f == 0), stop=(f == FC - 1))
                ins.then_inc(down, 1)

            blocks(pe, body)

        @block.scalar
        def _(act):
            def body(j):
                act.wait_ge(gu, j + 1 + START)
                nc.scalar.activation(flat(sl[:, :, :]), ps[:, 2, 0:FF], ACT.Silu).then_inc(silud, 1)

            blocks(act, body)

        @block.vector
        def _(dve):
            def body(j):
                dve.wait_ge(turned, j + 1 + START)
                dve.tensor_copy(flat(xT[:, :, :]), wide(ps[:, 0:2, :])).then_inc(xT_c, 1)
                dve.wait_ge(silud, j + 1 + START)
                dve.tensor_tensor(flat(hh[:, :, :]), flat(sl[:, :, :]), ps[:, 3, 0:FF], ALU.mult).then_inc(hd, 1)
                dve.wait_ge(down, j + 1 + START)
                dve.wait_ge(sums_in, j * 16 + 16)
                dve.sem_inc(spare[2], 1)
                dve.scalar_tensor_tensor(out=yo[:, :], in0=wide(ps[:, 4:6, :]), scalar=ids[:, 1:2], in1=base[:, :],
                                         op0=ALU.mult, op1=ALU.add).then_inc(copied, 1)

            blocks(dve, body)


def combine_phase(nc, ps, base_rows, y_rows, ln_g, ln_b, out, route):
    with Phase(nc, "com") as ph:
        sb, sem = ph.sb, ph.sem
        grow, brow = sb("grow", [P, D]), sb("brow", [P, D])
        base = [sb(f"base{b}", [P, D]) for b in range(2)]
        g = [[sb(f"g{b}{k}", [P, D]) for k in range(TOPK)] for b in range(2)]
        dg = [sb(f"dg{b}", [P, TOPK, P]) for b in range(2)]
        o = [sb(f"o{b}", [P, D]) for b in range(2)]
        ex, rk, gt = sb("ex", [P, TOPK]), sb("rk", [P, TOPK]), [sb(f"gt{b}", [P, TOPK]) for b in range(2)]
        kept = sb("kept", [P, TOPK])
        slot = [sb(f"slot{b}", [P, TOPK], U32) for b in range(2)]
        st, mv, ve, rstd, mhalf = (sb(n, s) for n, s in (("st", [P, 2, 6]), ("mv", [P, 2]), ("ve", [P, 1]),
                                                          ("rstd", [P, 1]), ("mhalf", [P, 1])))
        const, half = sem("const"), sem("half")
        base_in, g_in, out_s = ph.sems("base_in", 2), ph.zero_sems("g_in", 2), ph.sems("out", 2)
        added = ph.sems("added", 2)
        chain, diag, summed, stats, aggr, epsd, rstds, centred, scaled, ready = (
            sem(n) for n in ("chain", "diag", "summed", "stats", "aggr", "epsd", "rstds", "centred",
                             "scaled", "ready"))
        spare = [sem(f"spare{i}") for i in range(2)]
        block = ph.block()
        N2 = NX // 2
        CH_N = 5

        @block.sync
        def _(sp):
            sp.dma_start(grow[:, :], ln_g.partition_broadcast(P)).then_inc(const, 16)
            sp.dma_start(brow[:, :], ln_b.partition_broadcast(P)).then_inc(const, 16)
            for b in range(2):
                sp.dma_start(base[b][:, :], base_rows[b * P:(b + 1) * P, :]).then_inc(base_in[b], 16)

            def body(j, more):
                for b in range(2):
                    i = j * 2 + b
                    if more:
                        sp.wait_ge(added[b], j + 1 + START)
                        sp.dma_start(base[b][:, :], base_rows[bass.ds((i + 2) * P, P), :]).then_inc(base_in[b], 16)
                    sp.wait_ge(ready, i + 1 + START)
                    sp.dma_start(out[bass.ds(i * P, P), :], o[b][:, :]).then_inc(out_s[b], 16)

            with sp.Fori(0, N2 - 1) as j:
                body(j, True)
            body(N2 - 1, False)
            for b in range(2):
                sp.wait_ge(out_s[b], 16 * N2 + START)

        @block.gpsimd
        def _(pool):
            pool.memset(mhalf[:, :], -0.5).then_inc(half, 1)
            pool.wait_ge(half, 1 + START)
            pool.wait_ge(const, 32 + START)

            def gather(i, j, b):
                pool.wait_ge(chain, i * CH_N + CH_N + START)
                pool.wait_ge(added[b], j + START)
                pool.sem_inc(spare[0], 1)
                for k in range(TOPK):
                    pool.indirect_dma_start(out=g[b][k][:, :], out_offset=None, in_=y_rows,
                                            in_offset=bass.IndirectOffsetOnAxis(ap=slot[b][:, k:k + 1], axis=0)
                                            ).then_inc(g_in[b], 16)

            def norm(i, b):
                pool.wait_ge(aggr, i + 1 + START)
                pool.sem_inc(spare[0], 1)
                pool.tensor_scalar(ve[:, :], mv[:, 1:2], EPS, None, ALU.add).then_inc(epsd, 1)
                pool.wait_ge(epsd, i + 1 + START)
                pool.tensor_tensor(rstd[:, :], ve[:, :], mhalf[:, :], ALU.pow).then_inc(rstds, 1)
                pool.wait_ge(scaled, i + 1 + START)
                pool.tensor_tensor(o[b][:, :], o[b][:, :], brow[:, :], ALU.add).then_inc(ready, 1)

            gather(0, 0, 0)
            gather(1, 0, 1)

            def body(j, more):
                for b in range(2):
                    i = j * 2 + b
                    norm(i, b)
                    if more:
                        gather(i + 2, j + 1, b)

            with pool.Fori(0, N2 - 1) as j:
                body(j, True)
            body(N2 - 1, False)

        @block.vector
        def _(dve):
            dve.wait_ge(const, 32 + START)

            def slots(i, j, b):
                n = [0]

                def link(ins):
                    n[0] += 1
                    ins.then_inc(chain, 1)
                    dve.wait_ge(chain, i * CH_N + n[0] + START)

                at = slice(i, i + 1) if isinstance(i, int) else bass.ds(i, 1)
                row = lambda x: x[:, at, :].rearrange("p a k -> p (a k)")
                dve.wait_ge(added[b], j + START)
                dve.sem_inc(spare[1], 1)
                dve.tensor_copy(rk[:, :], row(route.rank))
                dve.tensor_copy(gt[b][:, :], row(route.gate))
                link(dve.tensor_copy(ex[:, :], row(route.expert)))
                link(dve.tensor_scalar(kept[:, :], rk[:, :], float(CAP), None, ALU.is_lt))
                link(dve.tensor_scalar(rk[:, :], rk[:, :], float(CAP - 1), None, ALU.min))
                link(dve.tensor_tensor(gt[b][:, :], gt[b][:, :], kept[:, :], ALU.mult))
                link(dve.scalar_tensor_tensor(out=slot[b][:, :], in0=ex[:, :], scalar=float(CAP), in1=rk[:, :],
                                              op0=ALU.mult, op1=ALU.add))
                assert n[0] == CH_N
                for k in range(TOPK):
                    ins = dve.tensor_scalar(dg[b][:, k, :], route.ident, gt[b][:, k:k + 1], None, ALU.mult)
                ins.then_inc(diag, 1)

            def finish(i, j, b):
                dve.wait_ge(out_s[b], j * 16 + START)
                dve.wait_ge(base_in[b], j * 16 + 16 + START)
                dve.wait_ge(summed, i + 1 + START)
                dve.sem_inc(spare[1], 1)
                dve.tensor_tensor(o[b][:, :], base[b][:, :], wide(ps[:, 2 * b:2 * b + 2, :]), ALU.add).then_inc(added[b], 1)
                dve.wait_ge(added[b], j + 1 + START)
                for a in range(2):
                    dve.bn_stats(st[:, a, :], o[b][:, a * BANK:(a + 1) * BANK]).then_inc(stats, 1)
                dve.wait_ge(stats, i * 2 + 2 + START)
                dve.sem_inc(spare[1], 1)
                dve.bn_aggr(mv[:, :], st[:, :, :]).then_inc(aggr, 1)

            def finish2(i, b):
                dve.wait_ge(rstds, i + 1 + START)
                dve.wait_ge(aggr, i + 1 + START)
                dve.sem_inc(spare[1], 1)
                dve.tensor_scalar(o[b][:, :], o[b][:, :], mv[:, 0:1], rstd[:, 0:1], ALU.subtract, ALU.mult).then_inc(centred, 1)
                dve.wait_ge(centred, i + 1 + START)
                dve.tensor_tensor(o[b][:, :], o[b][:, :], grow[:, :], ALU.mult).then_inc(scaled, 1)

            slots(0, 0, 0)
            slots(1, 0, 1)

            def body(j, more):
                for b in range(2):
                    i = j * 2 + b
                    finish(i, j, b)
                    if more:
                        slots(i + 2, j + 1, b)
                    finish2(i, b)

            with dve.Fori(0, N2 - 1) as j:
                body(j, True)
            body(N2 - 1, False)

        @block.tensor
        def _(pe):
            with pe.Fori(0, N2) as j:
                for b in range(2):
                    i = j * 2 + b
                    pe.wait_ge(diag, i + 1 + START)
                    pe.wait_ge(g_in[b], j * (16 * TOPK) + 16 * TOPK)
                    pe.wait_ge(added[b], j + START)
                    for h in range(2):
                        for k in range(TOPK):
                            ins = pe.matmul(ps[:, 2 * b + h, :], dg[b][:, k, :], g[b][k][:, h * BANK:(h + 1) * BANK],
                                            start=(k == 0), stop=(k == TOPK - 1))
                    ins.then_inc(summed, 1)


def build(nc, a, out):
    Phase.used = []
    dram = lambda name, shape, dt=F32: nc.dram_tensor(name, shape, dt).ap()
    h_rows, v_rows = dram("h_rows", (SEQ, D)), dram("v_rows", (TOK, FH * FD))
    cq, ck = dram("cq", (FH, 2, TOK)), dram("ck", (FH, 2, TOK))
    mixed, t_rows, base_rows = dram("mixed", (SEQ, MIX)), dram("t_rows", (SEQ + 1, D)), dram("base_rows", (SEQ + 1, D))
    table, over_rows = dram("table", (NE * SLOTS, 2)), dram("over_rows", (P, 2), I32)
    y_rows = dram("y_rows", (NE * CAP, D))
    with ExitStack() as ctx:
        ps = ctx.enter_context(nc.psum_tensor("ps", [P, 8, BANK], F32))
        with ExitStack() as first:
            ident = first.enter_context(nc.sbuf_tensor("ident", [P, P], F32))
            hT = first.enter_context(nc.sbuf_tensor("hT", [P, DC, TOK], F32))
            embed_phase(nc, ps, ident, hT, a["square"], a["x"], a["meta"], a["ln0_g"], a["ln0_b"], a["ln0_gcol"],
                        a["ln0_bcol"], a["w_in"], a["b_forget"], h_rows, v_rows, cq, ck)
            retention_phase(nc, ps, ident, hT, a["w_in"], a["rope"], a["retc"], mixed)
            fox_phase(nc, ps, ident, hT, a["square"], a["w_in"], v_rows, cq, ck, mixed)
        Phase.reset(nc)
        route = Route(nc, ctx)
        with nc.Block() as block:
            @block.sync
            def _(sp):
                sp.dma_start(route.sq[:, :], a["square"]).then_inc(route.tables, 16)
                sp.wait_ge(route.tables, 16)

            @block.gpsimd
            def _(pool):
                pool.memset(route.ones[:, :], 1.0).then_inc(route.ones_set, 1)
                pool.wait_ge(route.ones_set, 1)
        middle_phase(nc, ps, a["square"], mixed, h_rows, a["w_out"], a["ln1_g"], a["ln1_b"], a["w_router"],
                     a["router_bias"], a["ws_gate"], a["ws_up"], a["ws_down"], t_rows, base_rows, table, route)
        table_phase(nc, ps, table, over_rows, route)
        expert_phase(nc, ps, t_rows, a["we_gate"], a["we_up"], a["we_down"], y_rows, route)
        overflow_phase(nc, ps, t_rows, table, a["we_gate"], a["we_up"], a["we_down"], base_rows, route)
        combine_phase(nc, ps, base_rows, y_rows, a["ln2_g"], a["ln2_b"], out, route)


def kernel(**inputs):
    import concourse.bacc as bacc
    from concourse.bass_utils import run_bass_kernel_spmd

    nc = bacc.Bacc("TRN2", target_bir_lowering=False, num_devices=1)
    one = {"w_in", "b_forget", "w_out", "ln1_g", "ln1_b", "w_router", "router_bias", "we_gate", "we_up", "we_down",
           "ws_gate", "ws_up", "ws_down", "ln2_g", "ln2_b", "x"}
    data = {n: np.asarray(v)[0] if n in one else np.asarray(v) for n, v in inputs.items()}
    for n in ("g", "b"):
        data[f"ln0_{n}col"] = data[f"ln0_{n}"].reshape(DC, P).T
    data.update(constants())
    arrays, aps = {}, {}
    for n, v in data.items():
        v = np.ascontiguousarray(v)
        arrays[f"in_{n}"] = v
        aps[n] = nc.dram_tensor(f"in_{n}", v.shape, mybir.dt.from_np(v.dtype), kind="ExternalInput").ap()
    out = nc.dram_tensor("out", (SEQ, D), F32, kind="ExternalOutput").ap()
    build(nc, aps, out)
    got = run_bass_kernel_spmd(nc, [arrays], core_ids=[0])
    return got.results[0]["out"].reshape(1, SEQ, D)
```
